# Optimizing a Trainium2 kernel written in Bass

```python
import functools
import jax, jax.numpy as jnp
from jax import lax
import numpy as np

D_MODEL = 1024
BATCH = 1
SEQ = 256
DEPTH = 2
DEC_BATCH = 8
DEC_SEQ = 4
PAST_LEN = 256
PAGE_SIZE = 128

N_EVEN = (DEPTH + 1) // 2
N_ODD = DEPTH // 2
FOX_HEADS = 8
HEAD_DIM = 64
FOX_W = FOX_HEADS * HEAD_DIM
RWKV_HEADS = 8
RWKV_N = 64
RWKV_W = RWKV_HEADS * RWKV_N
W_LORA = 64
A_LORA = 64
G_LORA = 128
FOX_IN = 3 * FOX_W + FOX_HEADS
RWKV_IN = 3 * RWKV_W + W_LORA + A_LORA + G_LORA
IN_W = FOX_IN + RWKV_IN
MIX_W = FOX_W + RWKV_W
Q_BLOCK = 128
POOL_WINDOWS = (2, 4, 8, 16)
POOL_GROUPS = len(POOL_WINDOWS)
POOL_C = D_MODEL // POOL_GROUPS
POOL_BUF = max(POOL_WINDOWS) - 1
D_FF = 128 * ((8 * D_MODEL // 3 + 127) // 128)
N_EXPERTS = 8
TOP_K = 2
D_FF_EXPERT = 7 * D_MODEL // 2
RMS_EPS = 1e-6
GN_EPS = 64e-5
NEG_INF = -1e30

kernel_name = 'fox_rwkv7_pool_moe_decoder_step'

def rms_norm(x, g):
    xf = x.astype(jnp.float32)
    y = xf * lax.rsqrt(jnp.mean(xf * xf, axis=-1, keepdims=True) + RMS_EPS)
    return (y * g.astype(jnp.float32)).astype(x.dtype)

def ada_params(c, w, b):
    mod = jnp.einsum('bd,de->be', jax.nn.silu(c), w) + b
    return jnp.split(mod[:, None, :], 6, axis=-1)

def modulate(x, g, shift, scale):
    return rms_norm(x, g) * (1 + scale) + shift

def fox_prompt_attention(q, k, v, logf):
    B, T, H, Dh = q.shape
    scale = Dh ** -0.5
    FT = jnp.swapaxes(jnp.cumsum(logf, axis=1), 1, 2)
    nb = T // Q_BLOCK
    qb = jnp.moveaxis(q.reshape(B, nb, Q_BLOCK, H, Dh), 1, 0)
    Fb = jnp.moveaxis(FT.reshape(B, H, nb, Q_BLOCK), 2, 0)
    kpos = jnp.arange(T)

    def block(args):
        i, qi, Fi = args
        s = jnp.einsum('bqhd,bkhd->bhqk', qi, k).astype(jnp.float32) * scale
        s = s + Fi[..., :, None] - FT[..., None, :]
        qpos = i * Q_BLOCK + jnp.arange(Q_BLOCK)
        s = jnp.where(kpos[None, :] <= qpos[:, None], s, NEG_INF)
        p = jax.nn.softmax(s, axis=-1).astype(v.dtype)
        return jnp.einsum('bhqk,bkhd->bqhd', p, v)

    o = lax.map(block, (jnp.arange(nb), qb, Fb))
    return jnp.moveaxis(o, 0, 1).reshape(B, T, H * Dh)

def fox_sample_attention(q, k, v, logf, k_past, v_past, logf_past):
    B, T, H, Dh = q.shape
    P = k_past.shape[1]
    scale = Dh ** -0.5
    cs = jnp.cumsum(logf_past.astype(jnp.float32), axis=1)
    suffix = jnp.swapaxes(cs[:, -1:] - cs, 1, 2)
    Fn = jnp.swapaxes(jnp.cumsum(logf, axis=1), 1, 2)
    s_past = jnp.einsum('bqhd,bkhd->bhqk', q, k_past.astype(q.dtype)).astype(jnp.float32) * scale
    s_past = s_past + Fn[..., :, None] + suffix[..., None, :]
    s_new = jnp.einsum('bqhd,bkhd->bhqk', q, k).astype(jnp.float32) * scale
    s_new = s_new + Fn[..., :, None] - Fn[..., None, :]
    s_new = jnp.where(jnp.tril(jnp.ones((T, T), bool)), s_new, NEG_INF)
    p = jax.nn.softmax(jnp.concatenate([s_past, s_new], axis=-1), axis=-1).astype(v.dtype)
    o = jnp.einsum('bhqk,bkhd->bqhd', p[..., :P], v_past.astype(v.dtype))
    o = o + jnp.einsum('bhqk,bkhd->bqhd', p[..., P:], v)
    return o.reshape(B, T, H * Dh)

def rwkv7_time_mix(p, prev, S0, mu, w0, w2, a0, a2, g2, k_k, k_a, r_k, ln_w, ln_b):
    B, T, _ = p.shape
    f32 = jnp.float32
    shifted = jnp.concatenate([prev[:, None, :].astype(p.dtype), p[:, :-1]], axis=1)
    xm = p + (shifted - p) * mu
    cuts = np.cumsum([RWKV_W, W_LORA, RWKV_W, RWKV_W, A_LORA]).tolist()
    r, wl, k, v, al, gl = jnp.split(xm, cuts, axis=-1)
    w = -jax.nn.softplus(-(w0 + jnp.tanh(wl) @ w2).astype(f32)) - 0.5
    decay = jnp.exp(-jnp.exp(w))
    a = jax.nn.sigmoid((a0 + al @ a2).astype(f32))
    g = jax.nn.sigmoid(gl) @ g2
    heads = lambda t: t.reshape(B, T, RWKV_HEADS, RWKV_N)
    kk = heads((k * k_k).astype(f32))
    kk = kk * lax.rsqrt(jnp.maximum(jnp.sum(kk * kk, axis=-1, keepdims=True), 1e-24))
    k_mod = k.astype(f32) * (1 + (a - 1) * k_a)
    r_h, k_h, v_h, w_h, a_h = heads(r.astype(f32)), heads(k_mod), heads(v.astype(f32)), heads(decay), heads(a)

    def step(S, inp):
        r_t, w_t, k_t, v_t, kk_t, a_t = inp
        sa = jnp.einsum('bhvk,bhk->bhv', S, -kk_t)
        S = S * w_t[:, :, None, :] + sa[..., None] * (kk_t * a_t)[:, :, None, :] + v_t[..., None] * k_t[:, :, None, :]
        return S, jnp.einsum('bhvk,bhk->bhv', S, r_t)

    tm = lambda t: jnp.swapaxes(t, 0, 1)
    S_T, y_t = lax.scan(step, S0.astype(f32), (tm(r_h), tm(w_h), tm(k_h), tm(v_h), tm(kk), tm(a_h)))
    y = tm(y_t)
    mean = jnp.mean(y, axis=-1, keepdims=True)
    var = jnp.mean(jnp.square(y - mean), axis=-1, keepdims=True)
    y = (y - mean) * lax.rsqrt(var + GN_EPS) * ln_w.reshape(RWKV_HEADS, RWKV_N) + ln_b.reshape(RWKV_HEADS, RWKV_N)
    y = y + jnp.sum(r_h * k_h * r_k, axis=-1, keepdims=True) * v_h
    y = y.reshape(B, T, RWKV_W) * g
    return y.astype(p.dtype), S_T, p[:, -1]

def even_mixer(h, attend, S0, prev, w_in, w_out, q_gain, k_gain, f_bias, rwkv_params):
    B, T, _ = h.shape
    proj = jnp.einsum('btd,de->bte', h, w_in)
    fp, rp = proj[..., :FOX_IN], proj[..., FOX_IN:]
    hd = lambda t: t.reshape(B, T, FOX_HEADS, HEAD_DIM)
    q = rms_norm(hd(fp[..., :FOX_W]), q_gain)
    k = rms_norm(hd(fp[..., FOX_W:2 * FOX_W]), k_gain)
    v = hd(fp[..., 2 * FOX_W:3 * FOX_W])
    logf = jax.nn.log_sigmoid((fp[..., 3 * FOX_W:] + f_bias).astype(jnp.float32))
    o_fox = attend(q, k, v, logf)
    o_rwkv, S_T, last = rwkv7_time_mix(rp, prev, S0, *rwkv_params)
    y = jnp.einsum('bte,ed->btd', jnp.concatenate([o_fox.astype(h.dtype), o_rwkv], axis=-1), w_out)
    return y, (k, v, logf, S_T, last)

def pool_mixer(h, buf, start_pos, w_pool, pool_scale):
    B, T, D = h.shape
    f32 = jnp.float32
    ext = jnp.concatenate([buf.astype(h.dtype), h], axis=1)
    pos = start_pos + jnp.arange(POOL_BUF + T)
    ext_v = jnp.where((pos >= 0)[None, :, None], ext.astype(f32), 0.0)
    cs = jnp.concatenate([jnp.zeros((B, 1, D), f32), jnp.cumsum(ext_v, axis=1)], axis=1)
    tpos = pos[POOL_BUF:]
    groups = []
    for gi, win in enumerate(POOL_WINDOWS):
        csg = cs[..., gi * POOL_C:(gi + 1) * POOL_C]
        wsum = csg[:, POOL_BUF + 1:POOL_BUF + 1 + T] - csg[:, POOL_BUF + 1 - win:POOL_BUF + 1 - win + T]
        cnt = jnp.minimum(tpos + 1, win).astype(f32)
        groups.append(wsum / cnt[None, :, None])
    pooled = jnp.concatenate(groups, axis=-1)
    z = (pooled - h.astype(f32)).astype(h.dtype).reshape(B, T, POOL_GROUPS, POOL_C)
    y = jnp.einsum('btgc,gce->btge', z, w_pool).reshape(B, T, D) * pool_scale
    return y, ext[:, -POOL_BUF:]

def swiglu(h, wg, wu, wd):
    return jnp.einsum('btf,fd->btd', jax.nn.silu(h @ wg) * (h @ wu), wd)

def moe_ffn(h, router_w, router_b, wg, wu, wd):
    f32 = jnp.float32
    logits = jnp.einsum('btd,de->bte', h, router_w).astype(f32) + router_b
    top_v, top_i = lax.top_k(logits, TOP_K)
    gates = jax.nn.softmax(top_v, axis=-1)
    combine = jnp.einsum('btk,btke->bte', gates, jax.nn.one_hot(top_i, N_EXPERTS, dtype=f32))
    y = jnp.zeros(h.shape, f32)
    for e in range(N_EXPERTS):
        y = y + combine[..., e:e + 1] * swiglu(h, wg[e], wu[e], wd[e]).astype(f32)
    return y.astype(h.dtype)

def setup_inputs(seed: int = 0) -> dict:
    key = jax.random.key(seed)
    keys = jax.random.split(key, 64)
    counter = [0]

    def nk():
        counter[0] += 1
        return keys[counter[0] - 1]

    f32 = jnp.float32
    nrm = lambda shape, s: jax.random.normal(nk(), shape, f32) * s
    n_pages = PAST_LEN // PAGE_SIZE
    n_used = DEC_BATCH * n_pages
    n_phys = n_used + n_used // 4
    D = D_MODEL
    inp = {}
    inp['x_prompt'] = nrm((BATCH, SEQ, D), 1.0)
    inp['x_sample'] = nrm((DEC_BATCH, DEC_SEQ, D), 1.0)
    inp['c_prompt'] = nrm((BATCH, D), 1.0)
    inp['c_sample'] = nrm((DEC_BATCH, D), 1.0)
    inp['cache_fox_k'] = nrm((N_EVEN, n_phys, PAGE_SIZE, FOX_HEADS, HEAD_DIM), 1.0)
    inp['cache_fox_v'] = nrm((N_EVEN, n_phys, PAGE_SIZE, FOX_HEADS, HEAD_DIM), 1.0)
    inp['cache_fox_logf'] = jax.nn.log_sigmoid(3.0 + nrm((N_EVEN, n_phys, PAGE_SIZE, FOX_HEADS), 1.0))
    inp['page_table'] = jax.random.permutation(nk(), n_phys)[:n_used].reshape(DEC_BATCH, n_pages).astype(jnp.int32)
    inp['state_rwkv'] = nrm((N_EVEN, DEC_BATCH, RWKV_HEADS, RWKV_N, RWKV_N), 1.0)
    inp['state_rwkv_shift'] = nrm((N_EVEN, DEC_BATCH, RWKV_IN), 1.0)
    inp['state_pool'] = nrm((N_ODD, DEC_BATCH, POOL_BUF, D), 1.0)
    inp['norm1_g'] = 1.0 + nrm((DEPTH, D), 0.1)
    inp['norm2_g'] = 1.0 + nrm((DEPTH, D), 0.1)
    inp['ada_w'] = nrm((DEPTH, D, 6 * D), 0.5 * D ** -0.5)
    inp['ada_b'] = nrm((DEPTH, 6 * D), 0.02)
    inp['w_in'] = nrm((N_EVEN, D, IN_W), D ** -0.5)
    inp['w_out'] = nrm((N_EVEN, MIX_W, D), MIX_W ** -0.5)
    inp['fox_q_gain'] = 1.0 + nrm((N_EVEN, HEAD_DIM), 0.1)
    inp['fox_k_gain'] = 1.0 + nrm((N_EVEN, HEAD_DIM), 0.1)
    inp['fox_f_bias'] = 3.0 + nrm((N_EVEN, FOX_HEADS), 0.5)
    inp['rwkv_mu'] = jax.random.uniform(nk(), (N_EVEN, RWKV_IN), f32)
    inp['rwkv_w0'] = jnp.linspace(-6.5, -1.5, RWKV_W, dtype=f32)[None, :] + nrm((N_EVEN, RWKV_W), 0.1)
    inp['rwkv_w2'] = nrm((N_EVEN, W_LORA, RWKV_W), 0.1)
    inp['rwkv_a0'] = nrm((N_EVEN, RWKV_W), 0.1)
    inp['rwkv_a2'] = nrm((N_EVEN, A_LORA, RWKV_W), A_LORA ** -0.5)
    inp['rwkv_g2'] = nrm((N_EVEN, G_LORA, RWKV_W), G_LORA ** -0.5)
    inp['rwkv_k_k'] = 0.85 + nrm((N_EVEN, RWKV_W), 0.05)
    inp['rwkv_k_a'] = 1.0 + nrm((N_EVEN, RWKV_W), 0.05)
    inp['rwkv_r_k'] = nrm((N_EVEN, RWKV_HEADS, RWKV_N), 0.1)
    inp['rwkv_ln_w'] = 1.0 + nrm((N_EVEN, RWKV_W), 0.1)
    inp['rwkv_ln_b'] = nrm((N_EVEN, RWKV_W), 0.02)
    inp['ffn_w_gate'] = nrm((N_EVEN, D, D_FF), D ** -0.5)
    inp['ffn_w_up'] = nrm((N_EVEN, D, D_FF), D ** -0.5)
    inp['ffn_w_down'] = nrm((N_EVEN, D_FF, D), D_FF ** -0.5)
    inp['pool_w'] = nrm((N_ODD, POOL_GROUPS, POOL_C, POOL_C), POOL_C ** -0.5)
    inp['pool_scale'] = 1.0 + nrm((N_ODD, D), 0.1)
    inp['moe_router_w'] = nrm((N_ODD, D, N_EXPERTS), D ** -0.5)
    inp['moe_router_b'] = nrm((N_ODD, N_EXPERTS), 0.01)
    inp['moe_w_gate'] = nrm((N_ODD, N_EXPERTS, D, D_FF_EXPERT), D ** -0.5)
    inp['moe_w_up'] = nrm((N_ODD, N_EXPERTS, D, D_FF_EXPERT), D ** -0.5)
    inp['moe_w_down'] = nrm((N_ODD, N_EXPERTS, D_FF_EXPERT, D), D_FF_EXPERT ** -0.5)
    return inp

def reference(x_prompt, x_sample, c_prompt, c_sample, cache_fox_k, cache_fox_v, cache_fox_logf,
              page_table, state_rwkv, state_rwkv_shift, state_pool,
              norm1_g, norm2_g, ada_w, ada_b, w_in, w_out, fox_q_gain, fox_k_gain, fox_f_bias,
              rwkv_mu, rwkv_w0, rwkv_w2, rwkv_a0, rwkv_a2, rwkv_g2, rwkv_k_k, rwkv_k_a, rwkv_r_k,
              rwkv_ln_w, rwkv_ln_b, ffn_w_gate, ffn_w_up, ffn_w_down,
              pool_w, pool_scale, moe_router_w, moe_router_b, moe_w_gate, moe_w_up, moe_w_down):
    xp, xs = x_prompt, x_sample
    bp, bs = xp.shape[0], xs.shape[0]
    n_past = page_table.shape[1] * PAGE_SIZE
    kp_l, ks_l, vp_l, vs_l, fp_l, fs_l = [], [], [], [], [], []
    sp_l, ss_l, shp_l, shs_l, pp_l, ps_l = [], [], [], [], [], []
    for li in range(DEPTH):
        sh1p, sc1p, g1p, sh2p, sc2p, g2p = ada_params(c_prompt, ada_w[li], ada_b[li])
        sh1s, sc1s, g1s, sh2s, sc2s, g2s = ada_params(c_sample, ada_w[li], ada_b[li])
        hp = modulate(xp, norm1_g[li], sh1p, sc1p)
        hs = modulate(xs, norm1_g[li], sh1s, sc1s)
        if li % 2 == 0:
            e = li // 2
            rw = (rwkv_mu[e], rwkv_w0[e], rwkv_w2[e], rwkv_a0[e], rwkv_a2[e], rwkv_g2[e],
                  rwkv_k_k[e], rwkv_k_a[e], rwkv_r_k[e], rwkv_ln_w[e], rwkv_ln_b[e])
            shared = (w_in[e], w_out[e], fox_q_gain[e], fox_k_gain[e], fox_f_bias[e], rw)
            s0p = jnp.zeros((bp, RWKV_HEADS, RWKV_N, RWKV_N), jnp.float32)
            prevp = jnp.zeros((bp, RWKV_IN), xp.dtype)
            yp, (kq, vq, lfq, sq, lastq) = even_mixer(hp, fox_prompt_attention, s0p, prevp, *shared)
            k_past = cache_fox_k[e][page_table].reshape(bs, n_past, FOX_HEADS, HEAD_DIM)
            v_past = cache_fox_v[e][page_table].reshape(bs, n_past, FOX_HEADS, HEAD_DIM)
            lf_past = cache_fox_logf[e][page_table].reshape(bs, n_past, FOX_HEADS)
            attend_s = functools.partial(fox_sample_attention, k_past=k_past, v_past=v_past, logf_past=lf_past)
            ysm, (kn, vn, lfn, sn, lastn) = even_mixer(hs, attend_s, state_rwkv[e], state_rwkv_shift[e], *shared)
            kp_l.append(kq); ks_l.append(kn); vp_l.append(vq); vs_l.append(vn)
            fp_l.append(lfq); fs_l.append(lfn); sp_l.append(sq); ss_l.append(sn)
            shp_l.append(lastq); shs_l.append(lastn)
            xp = xp + g1p * yp
            xs = xs + g1s * ysm
            xp = xp + g2p * swiglu(modulate(xp, norm2_g[li], sh2p, sc2p), ffn_w_gate[e], ffn_w_up[e], ffn_w_down[e])
            xs = xs + g2s * swiglu(modulate(xs, norm2_g[li], sh2s, sc2s), ffn_w_gate[e], ffn_w_up[e], ffn_w_down[e])
        else:
            o = li // 2
            yp, bufp = pool_mixer(hp, jnp.zeros((bp, POOL_BUF, D_MODEL), hp.dtype), -POOL_BUF, pool_w[o], pool_scale[o])
            ysm, bufs = pool_mixer(hs, state_pool[o], n_past - POOL_BUF, pool_w[o], pool_scale[o])
            pp_l.append(bufp); ps_l.append(bufs)
            xp = xp + g1p * yp
            xs = xs + g1s * ysm
            xp = xp + g2p * moe_ffn(modulate(xp, norm2_g[li], sh2p, sc2p), moe_router_w[o], moe_router_b[o],
                                    moe_w_gate[o], moe_w_up[o], moe_w_down[o])
            xs = xs + g2s * moe_ffn(modulate(xs, norm2_g[li], sh2s, sc2s), moe_router_w[o], moe_router_b[o],
                                    moe_w_gate[o], moe_w_up[o], moe_w_down[o])
    return (xp, xs, jnp.stack(kp_l), jnp.stack(ks_l), jnp.stack(vp_l), jnp.stack(vs_l),
            jnp.stack(fp_l), jnp.stack(fs_l), jnp.stack(sp_l), jnp.stack(ss_l),
            jnp.stack(shp_l), jnp.stack(shs_l), jnp.stack(pp_l), jnp.stack(ps_l))


_drawn_inputs = setup_inputs


def setup_inputs(seed=0):
    import zlib

    import numpy as np

    out = dict(_drawn_inputs(seed))
    spreads = {}
    factors = {'cache_fox_logf': 6.283,
     'fox_q_gain': 3.968,
     'rwkv_ln_w': 3.356,
     'rwkv_ln_b': 8.0,
     'moe_router_b': 23.902}
    for name, (base, spread) in spreads.items():
        noise = np.random.default_rng([zlib.crc32(name.encode()), seed]).standard_normal(out[name].shape)
        drawn = base * np.exp(spread * noise) if base else spread * noise
        out[name] = __import__('jax').numpy.asarray(drawn.astype(out[name].dtype))
    for name, factor in factors.items():
        out[name] = (out[name] * factor).astype(out[name].dtype)
    return out
```

```python
from contextlib import ExitStack

import numpy as np

import concourse.bass as bass
from concourse import mybir

F32 = mybir.dt.float32
I32 = mybir.dt.int32
U32 = mybir.dt.uint32
ALU = mybir.AluOpType
ACT = mybir.ActivationFunctionType
AX = mybir.AxisListType

P = 128
D = 1024
DC = D // P
NP, NB, NT = 256, 8, 4
NS = NB * NT
N = NP + NS
BLK = [(0, 128), (128, 128), (256, 32)]
H, DH = 8, 64
HW = H * DH
HC = HW // P
LORA, GLORA = 64, 128
FOX_IN = 3 * HW + H
RW_IN = 3 * HW + 2 * LORA + GLORA
IN_W = FOX_IN + RW_IN
PAGE, NPG, PAST = 128, 2, 256
FF = 2816
NE, FE = 8, 3584
PASSES = -(-N // P)
MORE = (2 * N - 1) // P
ITEMS = NE + MORE
PBUF = 15
WINS = (2, 4, 8, 16)
RMS_EPS, GN_EPS, NEG = 1e-6, 64e-5, -1e30
DECAY = float(np.exp(-0.5))
L = 64
NCH = NP // L
LEVELS = 6

PIECES = ([(P * i, P) for i in range(HC)] + [(HW, LORA)] + [(HW + LORA + P * i, P) for i in range(HC)]
          + [(2 * HW + LORA + P * i, P) for i in range(HC)] + [(3 * HW + LORA, LORA), (3 * HW + 2 * LORA, GLORA)])
NPC = len(PIECES)
PR, PWL, PK, PV, PAL, PGL = 0, 4, 5, 9, 13, 14

CONST = {}
_at = 0
for _name, _n in [("ident", 128), ("before", 128), ("suffix0", 260), ("suffix1", 260),
                  ("causal", 256), ("pairs", 128), ("chunk", 128), ("levels", 64 * LEVELS), ("fold", 9),
                  ("heads", 32), ("newmask", 4), ("seqmask", 16), ("iota", 128), ("count", 64), ("reset", 256),
                  ("restart", 288)]:
    CONST[_name] = (_at, _n)
    _at += _n
NCONST = _at
CONST["ones"] = (CONST["suffix1"][0], P)


def constants():
    c = np.zeros((P, NCONST), np.float32)
    p = np.arange(P)[:, None]

    def put(name, a):
        at, n = CONST[name]
        c[:a.shape[0], at:at + n] = a.reshape(a.shape[0], n)

    j = np.arange(P)[None, :]
    put("ident", (p == j) * 1.0)
    put("before", (p < j) * 1.0)
    later, z = (p > j) * 1.0, np.zeros((P, 4))
    put("suffix0", np.concatenate([later, 0 * later, z], 1))
    put("suffix1", np.concatenate([np.ones((P, P)), later, z], 1))
    put("causal", np.concatenate([np.zeros((P, P)), np.where(j <= p, 0.0, NEG)], 1))
    put("pairs", (p // DH == j // DH) * 1.0)
    s, t = p % L, np.arange(2 * L)[None, :]
    put("chunk", np.where(t < L, s < t, s <= t - L) * 1.0)
    s, t = np.arange(L)[:, None], np.arange(L)[None, :]
    put("levels", np.concatenate([((s // (2 * m) == t // (2 * m)) & (s // m % 2 == 0) & (t // m % 2 == 1)) * 1.0
                                  for m in (1 << i for i in range(LEVELS))], 1))
    put("fold", (p % 32 == np.arange(9)[None, :]) * 1.0)
    put("heads", (np.arange(H)[:, None] == np.arange(32)[None, :] // NT) * 1.0)
    put("newmask", np.where(np.arange(NT)[None, :] <= p % NT, 0.0, NEG))
    put("seqmask", (np.arange(16)[None, :] // 8 * 4 + p // 32 == np.arange(16)[None, :] % 8) * 1.0)
    put("iota", np.broadcast_to(j, (P, P)) * 1.0)
    cnt = np.stack([1.0 / np.minimum(np.arange(16) + 1, w) for w in WINS])
    put("count", np.broadcast_to(cnt[None], (P, 4, 16)).copy())
    put("reset", np.broadcast_to((np.arange(NP) % L != 0)[None] * 1.0, (P, NP)).copy())
    t = np.arange(N)
    put("restart", np.broadcast_to(((t != 0) & ((t < NP) | (t % NT != 0)))[None] * 1.0, (P, N)).copy())
    return c


def weight_tiles():
    tiles = [("ada0", i) for i in range(12)] + [("win", i) for i in range(8)] + [("ada1", i) for i in range(12)]
    tiles += [("wout", i) for i in range(2)]
    for i in range(6):
        tiles += [("gate", i), ("up", i), ("down", i)]
    return tiles


TILES = weight_tiles()
SLOTS, SLOT = 6, 4096
MIX_TILE = TILES.index(("wout", 0))
FGRP = [(512 * i, min(512, FF - 512 * i)) for i in range(6)]
WIN = [
    (0, 512, [("f", i, P * i, P) for i in range(4)]),
    (512, 512, [("f", 4 + i, P * i, P) for i in range(4)]),
    (1024, 512, [("f", 8 + i, P * i, P) for i in range(4)]),
    (1536, 8, [("l", 0, 0, 8)]),
    (1544, 512, [("r", i, P * i, P) for i in range(4)]),
    (2056, 448, [("r", PWL, 0, 64)] + [("r", PK + i, 64 + P * i, P) for i in range(3)]),
    (2504, 512, [("r", PK + 3, 0, P)] + [("r", PV + i, P + P * i, P) for i in range(3)]),
    (3016, 320, [("r", PV + 3, 0, P), ("r", PAL, P, 64), ("r", PGL, 192, P)]),
]
WCHUNKS = [c for _, _, cs in WIN for c in cs]


class Banks:

    def __init__(self, tiles):
        self.tiles, self.n, self.owner, self.at = tiles, 0, [None] * len(tiles), {}

    def open(self, pe, name, freed):
        b = self.n % len(self.tiles)
        self.n += 1
        if self.owner[b] is not None:
            pe.wait_ge(*self.owner[b])
        self.owner[b] = freed
        self.at[name] = b
        return self.tiles[b]

    def __getitem__(self, name):
        return self.tiles[self.at[name]]


class Named:

    def __init__(self, nc, ctx):
        self.nc, self.ctx, self.made = nc, ctx, {}

    def __call__(self, name):
        if name not in self.made:
            self.made[name] = self.ctx.enter_context(self.nc.semaphore(name))
        return self.made[name]


ONCE = {
    "vector": ("vec_copied lf_abs lf_one logf_ready negF_ready k_ready q_ready last_ready rp_mixed "
              "psm_shifted psm_ready kk_scaled rk_ready cum_ready delta_ops packed oddw_copied "
              "final_state gn_centred mix_ready exts_zero z_ready z_used top_ready picked planned res4"),
    "scalar": ("siluc c_copied qk_squared lf_exp lf_ln qk_rooted psm_exped so_copied wl_tanh gl_sigmoid "
              "kk_squared kk_rooted fst_copied syt_copied gn_squared gn_rooted top_exped"),
    "tensor": ("vec_turned c_turned lf_turned last_turned so_mm oddw_mm fst_mm syt_mm route_mm rank_mm"),
    "gpsimd": ("vrow_zero silucT_zero last_zero"),
}


class Once:

    def __init__(self, s):
        self.s, self.given = s, {e: 0 for e in ONCE}
        self.place = {name: (e, i + 1) for e, names in ONCE.items() for i, name in enumerate(names.split())}

    def __call__(self, name):
        engine, value = self.place[name]
        return self.s(f"{engine}_once"), value

    def give(self, name):
        engine, value = self.place[name]
        self.given[engine] += 1
        assert self.given[engine] == value, name
        return self.s(f"{engine}_once")


class Counted:

    def __init__(self, eng):
        self.eng, self.n = eng, {}

    def give(self, ins, sem):
        ins.then_inc(sem, 1)
        self.n[sem.name] = self.n.get(sem.name, 0) + 1

    def step(self, ins, sem):
        self.give(ins, sem)
        self.eng.wait_ge(sem, self.n[sem.name])


def spread(ap, axis, n):
    ap = ap.unsqueeze(axis)
    shape = list(ap.shape)
    shape[axis] = n
    return ap.to_broadcast(shape)


def flat(t):
    return t[:, :, :].rearrange("p a b -> p (a b)")


XJOBS = [(0, 0, 4), (0, 4, 4), (1, 0, 4), (1, 4, 4), (2, 0, 8)]


def kth(n, lv):
    return 2 * LEVELS * (n // 2) + 2 * lv + n % 2


def t_count(n, lv):
    per_pair = 2 * (2 * (LEVELS - 1) + 1)
    base = per_pair * (n // 2)
    return base + (4 * lv + 2 * (n % 2) + 2 if lv < LEVELS - 1 else 4 * lv + n % 2 + 1)


CACHE_STORES = 6 + 2 * NPC

VB_MU, VB_W0, VB_A0, VB_KK, VB_KA, VB_RK, VB_LNW, VB_LNB, VB_PS, VB_QG, VB_KG = 0, 15, 19, 23, 27, 31, 35, 39, 43, 51, 52
VA_ADA, VA_NORM = 0, (96, 112, 104, 120)



def t_mms(n, lv):
    per_pair = 2 * (2 * (LEVELS - 2) + 1)
    base = per_pair * (n // 2)
    return base + (4 * (lv - 1) + 2 * (n % 2) + 2 if lv < LEVELS - 1 else 4 * (lv - 1) + n % 2 + 1)


def build_program(nc, a, y_p, y_s, k_p, k_s, v_p, v_s, lf_p, lf_s, st_p, st_s, sh_p, sh_s, pool_p, pool_s):
    ctx = ExitStack()
    with ctx:
        def sb(name, shape, dt=F32):
            return ctx.enter_context(nc.sbuf_tensor(name, shape, dt))

        s = Named(nc, ctx)
        once = Once(s)

        def sums(name, which, n):
            return s(f"sums_{which}"), 3 * ("kks", "bon", "gnm", "gnv").index(name) + n

        def lora(name, which, n):
            return s(f"lora_{which}"), HC * ("dec", "icl", "gat").index(name) + n

        banks = Banks([ctx.enter_context(nc.psum_tensor(f"bank{i}", [P, 512], F32)) for i in range(8)])

        const = sb("const", [P, NCONST])

        def K(name, rows=P):
            at, n = CONST[name]
            return const[0:rows, at:at + n]

        ident = K("ident")
        xT = sb("xT", [P, DC, N])
        hT = sb("hT", [P, DC, N])
        tmpT = sb("tmpT", [P, DC, N])
        yT = sb("yT", [P, DC, N])
        modT = [sb(f"modT{i}", [P, 48, 9]) for i in range(2)]
        gainT = [sb(f"gainT{i}", [P, DC, 9]) for i in range(4)]
        silucT = sb("silucT", [P, DC, 32])
        vrow = sb("vrow", [P, 3, P])
        vT = sb("vT", [P, 3, P])
        rstd = sb("rstd", [P, N])
        w2 = sb("w2", [LORA, HW])
        a2 = sb("a2", [LORA, HW])
        g2 = sb("g2", [GLORA, HW])
        fbias = sb("fbias", [H, 1])
        routerw = sb("routerw", [P, DC, NE])
        routerb = sb("routerb", [P, NE])
        pages = sb("pages", [1, NB * NPG], I32)
        ring = sb("ring", [P, SLOTS * SLOT])
        other = sb("other", [P, 12672])

        def slot(g):
            return ring[:, (g % SLOTS) * SLOT:(g % SLOTS + 1) * SLOT]

        class Region:
            def __init__(self, tensor, at=0):
                self.tensor, self.at = tensor, at

            def cut(self, *shape, rows=P):
                n = int(np.prod(shape))
                ap = self.tensor[0:rows, self.at:self.at + n]
                self.at += n
                names = "abcd"[:len(shape)]
                if len(shape) == 1:
                    return ap
                return ap.rearrange(f"p ({' '.join(names)}) -> p {' '.join(names)}",
                                    **dict(zip(names[1:], shape[1:])))

        R = Region(other)
        rp = R.cut(NPC, N)
        diff = R.cut(NPC, N)
        fqkv = R.cut(3 * HC, N)
        pastlf4 = R.cut(NB, NPG, H * NT)
        D2 = Region(other, NPC * N)
        lw = D2.cut(HC, N)
        icl = D2.cut(HC, N)
        gate = D2.cut(HC, N)
        R = Region(ring)
        X = Region(other)
        xrow = X.cut(3, D)
        crow = X.cut(D)
        scrow = X.cut(D)
        adap = Region(flat(yT), HC * N).cut(2, 512)
        R = Region(ring)
        ksamp = R.cut(2, NPG, HW)
        vsamp = R.cut(NB, NPG, HW)
        ktb = R.cut(2, HC, PAST + NT)
        qbd = R.cut(NB, HC, 32)
        pr = R.cut(2, 2, 256)
        prT = R.cut(2, 2, 2, P)
        psm = R.cut(2, PAST + NT)
        pnew = R.cut(2, NB, NT)
        psT = R.cut(2, 3, P)
        pastlf = R.cut(NB, NPG, H)
        logf = R.cut(N, rows=H)
        negF = R.cut(N, rows=H)
        lftmp = R.cut(2, N, rows=H)
        kvrow = R.cut(2, 3, HW)
        lfrow = R.cut(3, H)
        lastS = R.cut(NPC, NB)
        lastP = R.cut(NPC)
        lastrow = R.cut(2, P)
        ATT_END = R.at
        sst = R.cut(32, DH)
        sval = R.cut(NT, 32)
        ssa = R.cut(32)
        sy = R.cut(NT, 32)
        syrow = R.cut(HW, rows=NS)
        assert R.at <= SLOTS * SLOT, R.at
        R = Region(ring)
        kkT = R.cut(HC, N)
        bT = R.cut(HC, N)
        ar = R.cut(HC, NCH, 2, L)
        bk = R.cut(HC, NCH, 2, L)
        zv = R.cut(HC, NCH, 2, L)
        gt = R.cut(2, H, 2 * L)
        bkt = R.cut(2, H, DH)
        sav = R.cut(2, H, DH)
        su = R.cut(2, H, DH)
        lu = R.cut(NCH, H, L)
        assert R.at <= ATT_END, (R.at, ATT_END)
        Q = Region(other, 2 * NPC * N)
        rt = Q.cut(NCH, H, L, rows=L)
        tb = Q.cut(2, H, L, rows=L)
        assert Q.at <= 12672, Q.at
        Q = Region(flat(tmpT))
        wdec = Q.cut(HC, NP)
        winv = Q.cut(HC, NP)
        Q = Region(flat(hT))
        wprev = Q.cut(HC, NP)
        tt = Q.cut(2, H, L, rows=L)
        Q = Region(ring, R.at)
        xb = Q.cut(2, H, L, rows=L)
        nm = Q.cut(2, H, L, rows=L)
        ub = xb
        wlx = Q.cut(H, NCH, rows=L)
        srow = Region(ring, Q.at).cut(6, HW, rows=NS)
        svec = Q.cut(NT, 6, DH)
        sprod = Q.cut(32, DH)
        assert Q.at <= ATT_END, (Q.at, ATT_END)

        small = sb("small", [P, 64])
        plan = sb("plan", [1, 1 + MORE], I32)
        mix_stores = [0]

        R = Region(other)
        ffact = R.cut(2, 4, N)
        ffsilu = R.cut(2, N)
        prow = R.cut(D)
        poolw = R.cut(4, 2, 256)
        ext = R.cut(DC, 16 + NP)
        exts = R.cut(DC, NB, 20)
        hlast = R.cut(D)
        assert R.at <= 12672, R.at
        R = Region(other)
        htok = R.cut(3, D)
        xe = R.cut(DC, P)
        sg = R.cut(512)
        ea = R.cut(512)
        eaT = R.cut(2, 4, P)
        ye = R.cut(D)
        hot = R.cut(3, P)
        hotw = R.cut(3, P)
        gT = R.cut(N)
        pick = R.cut(3, NE)
        logit = R.cut(3, NE)
        comb = R.cut(3, ITEMS + 1)
        slot_at = R.cut(3, ITEMS + 1)
        later = R.cut(3, (PASSES - 1) * NE)
        top = R.cut(3, 8)
        topi = R.cut(3, 8)
        gate2 = R.cut(3, 4)
        outrow = R.cut(3, D)
        R.at -= 3 * D
        wanted = R.cut((PASSES - 1) * NE)
        ordinal = R.cut((PASSES - 1) * NE)
        which = R.cut(MORE, (PASSES - 1) * NE)
        expert = R.cut(MORE, NE)
        chosen = R.cut(3, MORE, (PASSES - 1) * NE)
        planf = R.cut(1 + MORE)
        R.at = max(R.at, 0)
        assert R.at <= 12672, R.at

        def vector_rows():
            out = [(vrow[48 * l:48 * l + 48, 0, :], a["ada_b"][l].rearrange("(r p) -> r p", p=P)) for l in range(2)]
            for i, name in enumerate(("norm1_g", "norm2_g")):
                out.append((vrow[96 + 16 * i:112 + 16 * i, 0, :], a[name].rearrange("l (r p) -> (l r) p", p=P)))
            for i, (at, w) in enumerate(PIECES):
                out.append((vrow[VB_MU + i:VB_MU + i + 1, 1, 0:w], a["rwkv_mu"][:, at:at + w]))
                out.append((vrow[NB * i:NB * i + NB, 2, 0:w], a["state_rwkv_shift"][0, :, at:at + w]))
            for name, row in (("rwkv_w0", VB_W0), ("rwkv_a0", VB_A0), ("rwkv_k_k", VB_KK), ("rwkv_k_a", VB_KA),
                              ("rwkv_ln_w", VB_LNW), ("rwkv_ln_b", VB_LNB)):
                out.append((vrow[row:row + HC, 1, :], a[name][0].rearrange("(r p) -> r p", p=P)))
            out.append((vrow[VB_RK:VB_RK + HC, 1, :], a["rwkv_r_k"][0].rearrange("(c a) k -> c (a k)", a=2)))
            out.append((vrow[VB_PS:VB_PS + DC, 1, :], a["pool_scale"][0].rearrange("(r p) -> r p", p=P)))
            for name, row in (("fox_q_gain", VB_QG), ("fox_k_gain", VB_KG)):
                for par in range(2):
                    out.append((vrow[row:row + 1, 1, DH * par:DH * (par + 1)], a[name]))
            return out

        cumv = winv

        def sample_operands():
            return [lw, kkT, bT, rp[:, PK:PK + HC, :], rp[:, PR:PR + HC, :], rp[:, PV:PV + HC, :]]

        scratch = nc.dram_tensor("sample_operands", [NB, NT, 6, H, DH], F32, kind="Internal").ap()
        scratch_y = nc.dram_tensor("sample_outputs", [NB, NT, 2 * H, 32], F32, kind="Internal").ap()

        def used(g):
            kind, i = TILES[g]
            if kind[:3] == "ada":
                return s("ada_mm"), 12 * int(kind[3]) + i + 1
            if kind == "win":
                return s("win_mm"), sum(len(c) for _, _, c in WIN[:i + 1])
            if kind == "wout":
                return s("wo_mm"), 4 * (i + 1)
            if kind == "down":
                return s("down_mm"), DC * (i + 1)
            return s(f"{kind}_mm"), 4 * i + FGRP[i][1] // P

        def tile_source(g):
            kind, i = TILES[g]

            def cols(w, at, n):
                return (slot(g)[:, 0:DC * n].rearrange("p (c f) -> p c f", c=DC),
                        w.rearrange("(c p) f -> p c f", p=P)[:, :, at:at + n])

            if kind[:3] == "ada":
                return cols(a["ada_w"][int(kind[3])], 512 * i, 512)
            if kind == "win":
                return cols(a["w_in"][0], WIN[i][0], WIN[i][1])
            if kind == "wout":
                return cols(a["w_out"][0], 512 * i, 512)
            at, n = FGRP[i]
            if kind == "down":
                return (slot(g)[:, 0:n // P * D].rearrange("p (c f) -> p c f", f=D),
                        a["ffn_w_down"][0, at:at + n, :].rearrange("(c p) f -> p c f", p=P))
            return cols(a[f"ffn_w_{kind}"][0], at, n)

        NT7 = FE // 512
        GRP = 3 * SLOT

        def moe_tile(it, t, kind):
            return ((it + t) % 2) * GRP + kind * SLOT

        def moe_gather(pe, mm, k):
            pe.wait_ge(s("hot_ready"), k + 1)
            for half in range(2):
                b = banks.tiles[5 - half]
                for c in range(4):
                    for blk, (_, w) in enumerate(BLK):
                        o = P * (4 * half + c)
                        last = mm(b[:, P * c:P * (c + 1)], htok[0:w, blk, o:o + P], hot[0:w, blk, :], blk == 0, blk == 2)
                last.then_inc(s("gather_mm"), 1)

        def moe_tensor_item(pe, mm, it):
            B = banks.tiles

            def hidden(t, kind):
                n = NT7 * it + t
                if kind == 0:
                    pe.wait_ge(s(f"moe_gu{t}"), 32 * it + 32)
                pe.wait_ge(s("moe_silu") if kind == 0 else s("moe_act"), n if t == 0 else n - 1)
                at = moe_tile(it, t, kind)
                for c in range(DC):
                    last = mm(B[2 * kind + t % 2][:, :], xe[:, c, :], ring[:, bass.ds(at + 512 * c, 512)], c == 0, c == DC - 1)
                last.then_inc(s("moe_gate" if kind == 0 else "moe_up"), 1)

            def turn(t):
                n = NT7 * it + t
                pe.wait_ge(s("moe_act"), n + 1)
                if t == 0:
                    pe.wait_ge(s("comb_added"), DC * it)
                else:
                    pe.wait_ge(s("eaT_ready"), n)
                for j in range(4):
                    last = pe.transpose(B[4][:, P * j:P * (j + 1)], ea[:, P * j:P * (j + 1)], ident)
                last.then_inc(s("moe_turn"), 1)

            def down(t):
                n = NT7 * it + t
                pe.wait_ge(s("eaT_ready"), n + 1)
                pe.wait_ge(s(f"moe_d{t}"), 16 * it + 16)
                if t == 0:
                    pe.wait_ge(s("ye_act"), it)
                    pe.wait_ge(s("ye_dve"), it)
                at = moe_tile(it, t, 2)
                for j in range(4):
                    for half in range(2):
                        last = mm(B[6 + half][:, :], eaT[:, t % 2, j, :], ring[:, bass.ds(at + D * j + 512 * half, 512)],
                                  t == 0 and j == 0, t == NT7 - 1 and j == 3)
                last.then_inc(s("moe_down"), 1)

            pe.wait_ge(s("xe_ready"), 2 * it + 2)
            hidden(0, 0)
            pe.wait_ge(s("comb_added"), DC * it)
            for blk, (t0, w) in enumerate(BLK):
                last = pe.transpose(B[5][:, t0:t0 + w], hotw[0:w, blk, :], ident[0:w, 0:w])
            last.then_inc(s("g_mm"), 1)
            hidden(0, 1)
            for t in range(1, NT7):
                hidden(t, 0)
                turn(t - 1)
                hidden(t, 1)
                down(t - 1)
            turn(NT7 - 1)
            pe.wait_ge(s("gT_ready"), it + 1)
            pe.wait_ge(s("eaT_ready"), NT7 * it + NT7)
            moe_gather(pe, mm, it + 1)
            down(NT7 - 1)
            pe.wait_ge(s("ye_act"), it + 1)
            pe.wait_ge(s("ye_dve"), it + 1)
            for j in range(DC):
                if j < 2:
                    pe.wait_ge(s("xe_ready"), 2 * it + 3 + j)
                if j >= 2:
                    pe.wait_ge(s("comb_added"), DC * it + j - 1)
                mm(B[5 - j % 2][:, 0:N], ye[:, P * j:P * (j + 1)], gT, True, True).then_inc(s("comb_mm"), 1)

        def moe_scalar_item(act, me, it):
            B = banks.tiles

            def turned(t):
                n = NT7 * it + t
                act.wait_ge(s("moe_turn"), n + 1)
                act.wait_ge(s("moe_down"), n if t == 0 else n - 1)
                me.give(act.activation(eaT[:, t % 2].rearrange("p j s -> p (j s)"), B[4][:, :], ACT.Copy), s("eaT_ready"))

            for t in range(NT7):
                n = NT7 * it + t
                act.wait_ge(s("moe_gate"), n + 1)
                act.wait_ge(s("moe_act"), n)
                me.give(act.activation(sg, B[t % 2][:, :], ACT.Silu), s("moe_silu"))
                if t:
                    turned(t - 1)
            turned(NT7 - 1)
            moe_gathered(act, me, it + 1)
            act.wait_ge(s("moe_down"), NT7 * it + NT7)
            act.wait_ge(s("comb_mm"), DC * it)
            me.give(act.activation(ye[:, 0:512], B[6][:, :], ACT.Copy), s("ye_act"))

        def moe_gathered(act, me, k):
            for half in range(2):
                act.wait_ge(s("gather_mm"), 2 * k + half + 1)
                me.give(act.activation(xe[:, 4 * half:4 * half + 4, :].rearrange("p c s -> p (c s)"),
                                       banks.tiles[5 - half][:, :], ACT.Copy), s("xe_ready"))

        def moe_hot(dve, it):
            for blk, (_, w) in enumerate(BLK):
                at = slot_at[0:w, blk, bass.ds(it, 1)]
                dve.tensor_scalar(hot[0:w, blk, :], K("iota")[0:w], at, None, ALU.is_equal)
                last = dve.tensor_scalar(hotw[0:w, blk, :], K("iota")[0:w], at, comb[0:w, blk, bass.ds(it, 1)],
                                         ALU.is_equal, ALU.mult)
            last.then_inc(s("hot_ready"), 1)

        def moe_vector_item(dve, it):
            B = banks.tiles
            for t in range(NT7):
                n = NT7 * it + t
                dve.wait_ge(s("moe_silu"), n + 1)
                dve.wait_ge(s("moe_up"), n + 1)
                dve.wait_ge(s("moe_turn"), n)
                dve.tensor_tensor(ea, sg, B[2 + t % 2][:, :], ALU.mult).then_inc(s("moe_act"), 1)
                if t == 0:
                    dve.wait_ge(s("g_mm"), it + 1)
                    dve.wait_ge(s("comb_mm"), DC * it)
                    dve.tensor_copy(gT, B[5][:, 0:N]).then_inc(s("gT_ready"), 1)
                if t == 1:
                    moe_hot(dve, it + 1)
            dve.wait_ge(s("moe_down"), NT7 * it + NT7)
            dve.tensor_copy(ye[:, 512:1024], B[7][:, :]).then_inc(s("ye_dve"), 1)
            dve.wait_ge(s("comb_added"), DC * it)
            for j in range(DC):
                dve.wait_ge(s("comb_mm"), DC * it + j + 1)
                dve.tensor_tensor(yT[:, j, :], yT[:, j, :], B[5 - j % 2][:, 0:N], ALU.add).then_inc(s("comb_added"), 1)

        def moe_sync_item(sp, it, e, first=False):
            wg, wu, wd = (a[f"moe_w_{k}"][0, bass.ds(e, 1)] for k in ("gate", "up", "down"))
            for t in range(NT7):
                n = NT7 * it + t
                for kind, w in enumerate((wg, wu, wd)):
                    if first and t < 2:
                        base = len(TILES) + 2 + 3 * t + kind - SLOTS
                        if base < len(TILES):
                            sp.wait_ge(*used(base))
                    elif kind == 0:
                        sp.wait_ge(s("moe_up"), n - 1)
                    elif kind == 2:
                        sp.wait_ge(s("moe_down"), n - 1)
                    dst = ring[:, bass.ds(moe_tile(it, t, kind), SLOT)]
                    if kind < 2:
                        sp.dma_start(dst.rearrange("p (c f) -> p c f", c=DC),
                                     w.rearrange("o (c p) f -> p (o c) f", p=P)[:, :, 512 * t:512 * (t + 1)])\
                            .then_inc(s(f"moe_gu{t}"), 16)
                    else:
                        sp.dma_start(dst.rearrange("p (c f) -> p c f", c=4),
                                     w.rearrange("o f d -> (o f) d")[512 * t:512 * (t + 1), :].rearrange("(c p) d -> p c d", p=P))\
                            .then_inc(s(f"moe_d{t}"), 16)

        def items(engine, step):
            with engine.Fori(0, NE) as it:
                step(it)
            engine.wait_ge(*once("planned"))
            count = engine.value_load(plan[0:1, 0:1], min_val=NE, max_val=ITEMS)
            with engine.Fori(NE, ITEMS) as it:
                with engine.If(count > it):
                    step(it)
            return count

        def moe_tensor(pe, mm):
            pe.wait_ge(s("ranked"), 3)
            pe.wait_ge(s("htok_ready"), 6)
            moe_gather(pe, mm, 0)
            items(pe, lambda it: moe_tensor_item(pe, mm, it))

        def moe_scalar(act, me):
            moe_gathered(act, me, 0)
            items(act, lambda it: moe_scalar_item(act, me, it))

        def moe_plan(dve, do):
            counts = small[:, 48:48 + NE]
            for p in range(1, PASSES):
                do(dve.tensor_scalar(wanted[:, NE * (p - 1):NE * p], counts, float(P * p), None, ALU.is_gt))
            do(dve.tensor_tensor_scan(ordinal, K("ones")[:, 0:(PASSES - 1) * NE], wanted, 0.0, ALU.mult, ALU.add))
            for r in range(MORE):
                do(dve.scalar_tensor_tensor(which[:, r, :], ordinal, float(r + 1), wanted, ALU.is_equal, ALU.mult))
            do(dve.tensor_tensor(chosen, spread(later, 2, MORE), spread(which, 1, 3), ALU.mult))
            do(dve.tensor_reduce(slot_at[:, :, NE:ITEMS], chosen, AX.X, ALU.add))
            do(dve.tensor_tensor(expert, which[:, :, 0:NE], which[:, :, NE:2 * NE], ALU.add))
            do(dve.tensor_tensor(chosen[:, :, :, 0:NE], spread(comb[:, :, 0:NE], 2, MORE), spread(expert, 1, 3), ALU.mult))
            do(dve.tensor_reduce(comb[:, :, NE:ITEMS], chosen[:, :, :, 0:NE], AX.X, ALU.add))
            do(dve.tensor_tensor(expert, expert, spread(K("iota")[:, 0:NE], 1, MORE), ALU.mult))
            do(dve.tensor_reduce(planf[:, 1:1 + MORE], expert, AX.X, ALU.add))
            do(dve.tensor_scalar(planf[:, 0:1], ordinal[:, 2 * NE - 1:2 * NE], float(NE), None, ALU.add))
            do(dve.tensor_copy(plan[:, :], planf[0:1, :]), once.give("planned"))

        def moe_vector(dve, do):
            moe_hot(dve, 0)
            moe_plan(dve, do)
            return items(dve, lambda it: moe_vector_item(dve, it))

        def moe_sync(sp):
            moe_sync_item(sp, 0, 0, first=True)
            with sp.Fori(1, NE) as it:
                moe_sync_item(sp, it, it)
            sp.wait_ge(*once("planned"))
            count = sp.value_load(plan[0:1, 0:1], min_val=NE, max_val=ITEMS)
            with sp.Fori(NE, ITEMS) as it:
                with sp.If(count > it):
                    e = sp.value_load(plan[0:1, bass.ds(it - (NE - 1), 1)], min_val=0, max_val=NE - 1)
                    moe_sync_item(sp, it, e)

        block = ctx.enter_context(nc.Block())

        @block.tensor
        def _(pe):
            def mm(out, lhsT, rhs, start, stop):
                return pe.matmul(out, lhsT, rhs, start=start, stop=stop, skip_group_check=True)

            pe.wait_ge(s("const_loaded"), 16)
            pe.wait_ge(s("vec_loaded"), 16 * len(vector_rows()))
            b = banks.open(pe, "vec", once("vec_copied"))
            for i in range(3):
                last = pe.transpose(b[:, P * i:P * (i + 1)], vrow[:, i, :], ident)
            last.then_inc(once.give("vec_turned"), 1)
            pe.wait_ge(*once("siluc"))
            b = banks.open(pe, "c", once("c_copied"))
            for c in range(DC):
                last = pe.transpose(b[:, 9 * c:9 * c + 9], scrow[0:9, P * c:P * (c + 1)], ident[0:9, 0:9])
            last.then_inc(once.give("c_turned"), 1)
            pe.wait_ge(s("x_loaded"), 48)
            for n, (blk, c0, nc_) in enumerate(XJOBS):
                w = BLK[blk][1]
                b = banks.open(pe, f"x{n}", (s("x_copied"), n + 1))
                for c in range(nc_):
                    last = pe.transpose(b[:, w * c:w * (c + 1)], xrow[0:w, blk, P * (c0 + c):P * (c0 + c + 1)],
                                        ident[0:w, 0:w])
                last.then_inc(s("x_turned"), 1)

            def mean_square(i):
                pe.wait_ge(s("squared"), i + 1)
                b = banks.open(pe, f"ms{i}", (s("ms_read"), i + 1))
                for c in range(DC):
                    last = mm(b[:, 0:N], K("ones"), tmpT[:, c, :], c == 0, c == DC - 1)
                last.then_inc(s("ms_ready"), 1)

            mean_square(0)

            def tile(g):
                pe.wait_ge(s(f"slot{g % SLOTS}"), 16 * (g // SLOTS + 1))
                return slot(g)

            def ada(layer):
                g0 = TILES.index((f"ada{layer}", 0))
                for i in range(13):
                    if i < 12:
                        w = tile(g0 + i).rearrange("p (c f) -> p c f", c=DC)
                        b = banks.open(pe, f"ada{layer}_{i}", (s("ada_copied"), 12 * layer + i + 1))
                        if layer + i == 0:
                            pe.wait_ge(*once("c_copied"))
                        for c in range(DC):
                            last = mm(b[32 * (c % 4):32 * (c % 4) + 32, :], silucT[:, c, :], w[:, c, :],
                                      c < 4, c >= 4)
                        last.then_inc(s("ada_mm"), 1)
                    if i > 0:
                        k = 12 * layer + i - 1
                        b = banks.open(pe, f"fold{layer}_{i - 1}", (s("mod_ready"), k + 1))
                        pe.wait_ge(s("ada_copied"), k + 1)
                        for j in range(4):
                            last = mm(b[:, 9 * j:9 * j + 9], adap[:, k % 2, P * j:P * (j + 1)], K("fold"), True, True)
                        last.then_inc(s("folded"), 1)

            ada(0)

            pe.wait_ge(s("h_ready"), 1)
            n = 0
            for i, (_, wd, chunks) in enumerate(WIN):
                w = tile(TILES.index(("win", i)))[:, 0:DC * wd].rearrange("p (c f) -> p c f", c=DC)
                for kind, idx, off, m in chunks:
                    b = banks.open(pe, f"win{n}", (s("win_act" if n % 2 else "win_dve"), n // 2 + 1))
                    for c in range(DC):
                        last = mm(b[0:m, 0:N], w[:, c, off:off + m], hT[:, c, :], c == 0, c == DC - 1)
                    last.then_inc(s("win_mm"), 1)
                    n += 1
            ada(1)

            pe.wait_ge(*once("qk_squared"))
            for i in range(6):
                b = banks.open(pe, f"qkms{i}", (s("qkms_read"), i + 1))
                mm(b[:, 0:384], K("pairs"), flat(tmpT)[:, 384 * i:384 * (i + 1)], True, True).then_inc(s("qkms"), 1)
            pe.wait_ge(*once("k_ready"))
            for n in range(6):
                which, blk = n // 3, n % 3
                t0, w = BLK[blk]
                b = banks.open(pe, f"kv{n}", (s("kv_copied"), n + 1))
                for c in range(HC):
                    last = pe.transpose(b[0:w, P * c:P * (c + 1)], fqkv[:, HC * (1 + which) + c, t0:t0 + w], ident)
                last.then_inc(s("kv_turned"), 1)
            pe.wait_ge(*once("logf_ready"))
            b = banks.open(pe, "lf", (s("lf_copied"), 3))
            for blk, (t0, w) in enumerate(BLK):
                last = pe.transpose(b[0:w, H * blk:H * (blk + 1)], logf[:, t0:t0 + w], ident[0:H, 0:H])
            last.then_inc(once.give("lf_turned"), 1)
            pe.wait_ge(*once("last_ready"))
            b = banks.open(pe, "last", (s("last_copied"), 2))
            pe.transpose(b[0:NPC * 8, 0:P], lastS.rearrange("p a b -> p (a b)"), ident)
            pe.transpose(b[0:NPC, P:2 * P], lastP, ident).then_inc(once.give("last_turned"), 1)

            def scores(c, qb):
                nk = P * (qb + 1)
                for par in range(2):
                    p0 = DH * par
                    b = banks.open(pe, f"s{c}{qb}{par}", (s("scored"), 4 * c + 2 * qb + par + 1))
                    mm(b[:, 0:nk], fqkv[p0:p0 + DH, c, P * qb:P * (qb + 1)], fqkv[p0:p0 + DH, HC + c, 0:nk], True, False)
                    h = 2 * c + par
                    mm(b[:, 0:nk], ident[0:H, h:h + 1].to_broadcast([H, P]), negF[0:H, 0:nk], False, True)\
                        .then_inc(s("s_mm"), 1)

            def turn_probs(c, qb):
                k = 2 * c + qb
                pe.wait_ge(s("probs"), k + 1)
                b = banks.open(pe, f"pt{c}{qb}", (s("probsT"), k + 1))
                for par in range(2):
                    for j in range(qb + 1):
                        o = P * ((qb + 1) * par + j)
                        last = pe.transpose(b[:, o:o + P], pr[:, k % 2, par, P * j:P * (j + 1)], ident)
                last.then_inc(s("pt_mm"), 1)

            def attend(c, qb):
                k = 2 * c + qb
                pe.wait_ge(s("probsT"), k + 1)
                b = banks.open(pe, f"o{c}{qb}", (s("o_copied"), k + 1))
                for par in range(2):
                    h = 2 * c + par
                    for j in range(qb + 1):
                        last = mm(b[DH * par:DH * par + DH, 0:P], kvrow[:, 1, j, DH * h:DH * (h + 1)],
                                  prT[:, k % 2, par, j, :], j == 0, j == qb)
                last.then_inc(s("o_mm"), 1)

            pe.wait_ge(*once("q_ready"))
            pe.wait_ge(*once("negF_ready"))
            pe.wait_ge(s("kv_copied"), 6)
            tasks = [(c, qb) for c in range(HC) for qb in range(2)]
            scores(*tasks[0])
            for k, t in enumerate(tasks):
                if k + 1 < len(tasks):
                    scores(*tasks[k + 1])
                turn_probs(*t)
                attend(*t)

            pe.wait_ge(s("qbd_ready"), 2 * HC)
            for q in range(NB):
                pe.wait_ge(s(f"k_page{q % 2}"), 64 * (q // 2 + 1))
                for half in range(2):
                    b = banks.open(pe, f"kt{q}{half}", (s("kt_copied"), 3 * q + half + 1))
                    for cc in range(2):
                        for j in range(NPG):
                            o = 256 * cc + P * j
                            last = pe.transpose(b[:, o:o + P], ksamp[:, q % 2, j, P * (2 * half + cc):P * (2 * half + cc + 1)], ident)
                    last.then_inc(s("kt_mm"), 1)
                pe.wait_ge(s("kt_copied"), 3 * q + 3)
                b = banks.open(pe, f"ss{q}", (s("ss_copied"), q + 1))
                o = b[0:32, 0:PAST + NT]
                for c in range(HC):
                    mm(o, qbd[:, q, c, :], ktb[:, q % 2, c, :], c == 0, False)
                pe.wait_ge(s("lf_spread"), q + 1)
                for j in range(NPG):
                    mm(o, pastlf4[:, q, j, :], K(f"suffix{j}"), False, False)
                mm(b[0:32, PAST:PAST + NT], K("heads", H), negF[0:H, NP + NT * q:NP + NT * (q + 1)],
                   False, True).then_inc(s("ss_mm"), 1)
            pe.wait_ge(*once("psm_ready"))
            for g in range(2):
                b = banks.open(pe, f"pst{g}", (s("psT_ready"), 2 * g + 2))
                for j in range(NPG):
                    pe.transpose(b[:, P * j:P * (j + 1)], psm[:, g, P * j:P * (j + 1)], ident)
                last = pe.transpose(b[0:32, 2 * P:3 * P], pnew[:, g, :, :].rearrange("p a b -> p (a b)"), ident)
                last.then_inc(s("pst_mm"), 1)
            pe.wait_ge(s("psT_ready"), 4)
            pe.wait_ge(s("v_pages"), 32 * NB)
            b = banks.open(pe, "so", once("so_copied"))
            so = b[:, 0:HC * NS].rearrange("p (c t) -> p c t", c=HC)
            for h in range(H):
                p0, c = DH * (h % 2), h // 2
                for g in range(2):
                    new = psT[0:32, g, 2, :].rearrange("p (s h t) -> p s h t", s=4, h=H)[:, :, h, :]
                    mm(so[p0:p0 + DH, c, 16 * g:16 * g + 16], kvrow[0:NS, 1, 2, DH * h:DH * (h + 1)], new,
                       h < 2 and g == 0, False)
            for q in range(NB):
                for h in range(H):
                    p0, c = DH * (h % 2), h // 2
                    for j in range(NPG):
                        at = 32 * (q % 4) + NT * h
                        last = mm(so[p0:p0 + DH, c, NT * q:NT * (q + 1)], vsamp[:, q, j, DH * h:DH * (h + 1)],
                                  psT[:, q // 4, j, at:at + NT], False, q == NB - 1 and j == NPG - 1)
            last.then_inc(once.give("so_mm"), 1)

            def lowrank(name, weights, src, need):
                pe.wait_ge(*once(need))
                for c in range(HC):
                    b = banks.open(pe, f"{name}{c}", lora(name, "ready", c + 1))
                    mm(b[:, 0:N], weights[:, P * c:P * (c + 1)], src, True, True).then_inc(s("lora_mm"), 1)

            lowrank("dec", w2[:, :], rp[0:LORA, PWL, :], "wl_tanh")
            lowrank("icl", a2[:, :], rp[0:LORA, PAL, :], "rp_mixed")
            lowrank("gat", g2[:, :], rp[:, PGL, :], "gl_sigmoid")

            def head_sums(name, src, n=3):
                for i in range(n):
                    b = banks.open(pe, f"{name}{i}", sums(name, "read", i + 1))
                    mm(b[:, 0:384], K("pairs"), src[:, 384 * i:384 * (i + 1)], True, True).then_inc(s("sums_mm"), 1)

            pe.wait_ge(*once("kk_squared"))
            head_sums("kks", flat(tmpT)[:, 0:HC * N])
            pe.wait_ge(*once("rk_ready"))
            head_sums("bon", flat(tmpT)[:, HC * N:2 * HC * N])
            pe.wait_ge(*once("delta_ops"))
            for i, src in enumerate(sample_operands()):
                b = banks.open(pe, f"sr{i}", (s("srow_copied"), i + 1))
                for c in range(HC):
                    last = pe.transpose(b[0:NS, P * c:P * (c + 1)], src[:, c, NP:N], ident)
                last.then_inc(s("sr_mm"), 1)

            pe.wait_ge(*once("packed"))
            for c in range(HC):
                b = banks.open(pe, f"odd{c}", (s("odd_copied"), 2 * c + 2))
                mm(b[0:L, :], ident[:, DH:P], ar[:, c].rearrange("p n a t -> p (n a t)"), True, True).then_inc(s("odd_mm"), 1)
            b = banks.open(pe, "oddw", once("oddw_copied"))
            mm(b[0:L, 0:HC * NCH].rearrange("p (c n) -> p c n", c=HC), ident[:, DH:P],
               wdec.rearrange("p c (n t) -> p c n t", t=L)[:, :, :, L - 1], True, True).then_inc(once.give("oddw_mm"), 1)

            def products(n):
                for par in range(2):
                    b = banks.open(pe, f"gt{n}{par}", (s("gt_ready"), 2 * n + par + 1))
                    for c in range(HC):
                        last = mm(b[:, P * c:P * (c + 1)], bk[DH * par:DH * par + DH, c, n].rearrange("p a t -> p (a t)"),
                                  ar[DH * par:DH * par + DH, c, n].rearrange("p a t -> p (a t)"), True, True)
                    last.then_inc(s("gt_mm"), 1)
                for src, nm_ in ((bk, "bkt"), (zv, "vt")):
                    b = banks.open(pe, f"{nm_}{n}", (s(f"{nm_}_ready"), n + 1))
                    for c in range(HC):
                        last = pe.transpose(b[:, P * c:P * (c + 1)], src[:, c, n].rearrange("p a t -> p (a t)"), ident)
                    last.then_inc(s(f"{nm_}_mm"), 1)

            def invert(pair):
                for lv in range(LEVELS):
                    for i in range(2):
                        n = 2 * pair + i
                        k = LEVELS * n + lv
                        pe.wait_ge(s("nm_ready"), kth(n, lv) + 1)
                        if lv:
                            pe.wait_ge(s("t_ready"), t_count(n, lv - 1))
                        b = banks.open(pe, f"x_{k}", (s("xb_ready"), kth(n, lv) + 1))
                        for h in range(H):
                            rhs = ident[0:L, 0:L] if lv == 0 else tb[:, i, h, :]
                            last = mm(b[0:L, L * h:L * (h + 1)], nm[:, i, h, :], rhs, True, True)
                        last.then_inc(s("x_mm"), 1)
                    for i in range(2):
                        n = 2 * pair + i
                        if lv == 0:
                            continue
                        pe.wait_ge(s("xb_ready"), kth(n, lv) + 1)
                        if lv < LEVELS - 1:
                            b = banks.open(pe, f"t_{n}{lv}", (s("t_ready"), t_count(n, lv) - 1))
                            for h in range(H):
                                last = mm(b[0:L, L * h:L * (h + 1)], tt[:, i, h, :], xb[:, i, h, :], True, True)
                            last.then_inc(s("t_mm"), 1)
                        b = banks.open(pe, f"tt_{n}{lv}", (s("t_ready"), t_count(n, lv)))
                        for h in range(H):
                            last = mm(b[0:L, L * h:L * (h + 1)], xb[:, i, h, :], tt[:, i, h, :], True, True)
                        last.then_inc(s("t_mm"), 1)

            def advance(n):
                i = n % 2
                pe.wait_ge(s("su_ready"), n + 1)
                pe.wait_ge(s("lu_ready"), n + 1)
                pe.wait_ge(s("odd_copied"), 2 * HC)
                pe.wait_ge(s("even_copied"), 2)
                pe.wait_ge(s("vt_ready"), n + 1)
                b = banks.open(pe, f"u{n}", (s("u_ready"), n + 1))
                for h in range(H):
                    last = mm(b[0:L, DH * h:DH * (h + 1)], lu[:, n, h, :], su[:, i, h, :], True, True)
                last.then_inc(s("u_mm"), 1)
                pe.wait_ge(s("u_ready"), n + 1)
                pe.wait_ge(s("t_ready"), t_count(n, LEVELS - 1))
                b = banks.open(pe, f"sa{n}", (s("sa_ready"), n + 1))
                for h in range(H):
                    last = mm(b[0:L, DH * h:DH * (h + 1)], tt[:, i, h, :], ub[:, i, h, :], True, True)
                last.then_inc(s("sa_mm"), 1)
                pe.wait_ge(s("sa_ready"), n + 1)
                pe.wait_ge(s("bkt_ready"), n + 1)
                b = banks.open(pe, f"st{n}", (s("state_read"), n + 1))
                for h in range(H):
                    last = mm(b[0:L, DH * h:DH * (h + 1)], bkt[:, i, h, :], sav[:, i, h, :], True, True)
                last.then_inc(s("st_mm"), 1)
                b = banks.open(pe, f"y{n}", (s("yc_copied"), n + 1))
                for h in range(H):
                    o = b[DH * (h % 2):DH * (h % 2) + DH, L * (h // 2):L * (h // 2 + 1)]
                    mm(o, su[0:L, i, h, :], rt[:, n, h, :], True, False)
                    last = mm(o, sav[:, i, h, :], gt[:, i, h, L:2 * L], False, True)
                last.then_inc(s("y_mm"), 1)

            for pair in range(NCH // 2):
                products(2 * pair)
                products(2 * pair + 1)
                invert(pair)
                advance(2 * pair)
                advance(2 * pair + 1)
            pe.wait_ge(*once("final_state"))
            b = banks.open(pe, "fst", once("fst_copied"))
            for c in range(HC):
                last = pe.transpose(b[:, DH * c:DH * (c + 1)], su[0:L, 0, 2 * c:2 * c + 2, :].rearrange("p h v -> p (h v)"),
                                    ident[0:L, 0:L])
            last.then_inc(once.give("fst_mm"), 1)
            pe.wait_ge(s("syrow_loaded"), 16)
            b = banks.open(pe, "syt", once("syt_copied"))
            for c in range(HC):
                last = pe.transpose(b[:, NS * c:NS * (c + 1)], syrow[:, P * c:P * (c + 1)], ident[0:NS, 0:NS])
            last.then_inc(once.give("syt_mm"), 1)
            pe.wait_ge(*once("syt_copied"))
            pe.wait_ge(s("yc_copied"), NCH)
            head_sums("gnm", flat(yT)[:, HC * N:2 * HC * N])
            pe.wait_ge(*once("gn_squared"))
            head_sums("gnv", flat(tmpT)[:, 0:HC * N])

            pe.wait_ge(*once("mix_ready"))
            pe.wait_ge(s("o_copied"), 2 * HC)
            pe.wait_ge(*once("so_copied"))
            for j in range(DC):
                w = tile(MIX_TILE + j // 4).rearrange("p (c f) -> p c f", c=DC)
                b = banks.open(pe, f"wo{j}", (s("res1"), j + 1))
                for c in range(DC):
                    last = mm(b[:, 0:N], w[:, c, P * (j % 4):P * (j % 4 + 1)], yT[:, c, :], c == 0, c == DC - 1)
                last.then_inc(s("wo_mm"), 1)
            mean_square(1)

            pe.wait_ge(s("h_ready"), 2)

            def hidden(i):
                nf = FGRP[i][1]
                for j in range(nf // P):
                    for kind in ("gate", "up"):
                        w = tile(TILES.index((kind, i)))[:, 0:DC * nf].rearrange("p (c f) -> p c f", c=DC)
                        n = 4 * i + j
                        b = banks.open(pe, f"{kind}{n}", (s("act_ready"), n + 1))
                        for c in range(DC):
                            last = mm(b[:, 0:N], w[:, c, P * j:P * (j + 1)], hT[:, c, :], c == 0, c == DC - 1)
                        last.then_inc(s(f"{kind}_mm"), 1)

            def down(i):
                nf = FGRP[i][1]
                w = tile(TILES.index(("down", i)))[:, 0:nf // P * D].rearrange("p (c f) -> p c f", f=D)
                pe.wait_ge(s("act_ready"), FGRP[i][0] // P + nf // P)
                for j in range(DC):
                    b = banks.open(pe, f"down{i}_{j}", (s("ff_added"), DC * i + j + 1))
                    for c in range(nf // P):
                        last = mm(b[:, 0:N], w[:, c, P * j:P * (j + 1)], ffact[:, i % 2, c, :], c == 0, c == nf // P - 1)
                    last.then_inc(s("down_mm"), 1)

            hidden(0)
            for i in range(1, 6):
                hidden(i)
                down(i - 1)
            down(5)

            mean_square(2)
            pe.wait_ge(s("pool_rows"), 16)
            b = banks.open(pe, "pb0", (s("pbuf_copied"), 1))
            for c in range(4):
                last = pe.transpose(b[:, 120 * c:120 * (c + 1)], prow[0:120, P * c:P * (c + 1)], ident[0:120, 0:120])
            last.then_inc(s("pb_mm"), 1)
            b = banks.open(pe, "pb1", (s("pbuf_copied"), 2))
            for c in range(4):
                last = pe.transpose(b[:, 120 * c:120 * (c + 1)], prow[0:120, P * (4 + c):P * (5 + c)], ident[0:120, 0:120])
            last.then_inc(s("pb_mm"), 1)
            pe.wait_ge(s("h_ready"), 3)
            for half in range(2):
                b = banks.open(pe, f"hl{half}", (s("hl_copied"), half + 1))
                for c in range(4):
                    last = pe.transpose(b[0:NS + 16, P * c:P * (c + 1)], hT[:, 4 * half + c, NP - 16:N], ident)
                last.then_inc(s("hl_mm"), 1)
            pe.wait_ge(*once("z_ready"))
            pe.wait_ge(s("poolw_loaded"), 16)
            for j in range(DC):
                b = banks.open(pe, f"pool{j}", (s("res3"), j + 1))
                for c in range(2):
                    last = mm(b[:, 0:N], poolw[:, j // 2, c, P * (j % 2):P * (j % 2 + 1)], yT[:, 2 * (j // 2) + c, :],
                              c == 0, c == 1)
                last.then_inc(s("pool_mm"), 1)
            mean_square(3)

            pe.wait_ge(s("h_ready"), 4)
            b = banks.open(pe, "route", (s("logits"), 3))
            for blk, (t0, w) in enumerate(BLK):
                for c in range(DC):
                    last = mm(b[0:w, NE * blk:NE * (blk + 1)], hT[:, c, t0:t0 + w], routerw[:, c, :], c == 0, c == DC - 1)
            last.then_inc(once.give("route_mm"), 1)
            for n in range(6):
                t0, w = BLK[n // 2]
                b = banks.open(pe, f"ht{n}", (s("htok_ready"), n + 1))
                for c in range(4):
                    last = pe.transpose(b[0:w, P * c:P * (c + 1)], hT[:, 4 * (n % 2) + c, t0:t0 + w], ident)
                last.then_inc(s("ht_mm"), 1)
            pe.wait_ge(*once("picked"))
            b = banks.open(pe, "rank", (s("ranked"), 3))
            for blk, (t0, w) in enumerate(BLK):
                for e in range(blk + 1):
                    we = BLK[e][1]
                    tri = K("before")[0:we, 0:w] if e == blk else K("ones")[0:we, 0:w]
                    mm(b[0:w, NE * blk:NE * (blk + 1)], tri, pick[0:we, e, :], e == 0, e == blk)
            for e in range(3):
                we = BLK[e][1]
                last = mm(b[0:P, 3 * NE:4 * NE], K("ones")[0:we, 0:P], pick[0:we, e, :], e == 0, e == 2)
            last.then_inc(once.give("rank_mm"), 1)
            moe_tensor(pe, mm)

            pe.wait_ge(*once("res4"))
            for n in range(6):
                t0, w = BLK[n // 2]
                b = banks.open(pe, f"out{n}", (s("out_copied"), n + 1))
                for c in range(4):
                    last = pe.transpose(b[0:w, P * c:P * (c + 1)], xT[:, 4 * (n % 2) + c, t0:t0 + w], ident)
                last.then_inc(s("out_mm"), 1)

        @block.scalar
        def _(act):
            me = Counted(act)
            chain = s("act_chain")

            def copy(out, in_, sem):
                me.give(act.activation(out, in_, ACT.Copy), sem)

            act.wait_ge(*once("vrow_zero"))
            for dst, src in vector_rows():
                act.dma_start(dst, src).then_inc(s("vec_loaded"), 16)
            act.wait_ge(s("c_loaded"), 32)
            me.step(act.activation(scrow[0:9, :], crow[0:9, :], ACT.Silu), once.give("siluc"))
            act.wait_ge(*once("c_turned"))
            act.wait_ge(*once("silucT_zero"))
            me.give(act.activation(silucT[:, :, 0:9], banks["c"][:, 0:72].rearrange("p (c j) -> p c j", c=DC),
                                   ACT.Copy), once.give("c_copied"))
            act.wait_ge(s("x_copied"), 5)

            def square_all(i):
                if i:
                    act.wait_ge(s("res"), i)
                me.give(act.activation(flat(tmpT), flat(xT), ACT.Square), s("squared"))

            def root(i):
                act.wait_ge(s("ms_read"), i + 1)
                me.give(act.activation(rstd[:, :], rstd[:, :], ACT.Sqrt), s("rooted"))

            square_all(0)
            root(0)

            def ada(layer):
                for i in range(12):
                    k = 12 * layer + i
                    act.wait_ge(s("ada_mm"), k + 1)
                    if k >= 2:
                        act.wait_ge(s("folded"), k - 1)
                    copy(adap[:, k % 2, :], banks[f"ada{layer}_{i}"][:, :], s("ada_copied"))

            ada(0)

            def proj_chunk(n):
                kind, idx, _, m = WCHUNKS[n]
                dst = {"f": fqkv, "r": rp}[kind]
                return dst[0:m, idx, :], banks[f"win{n}"][0:m, 0:N]

            act.wait_ge(*once("last_zero"))
            for n in range(1, len(WCHUNKS), 2):
                act.wait_ge(s("win_mm"), n + 1)
                copy(*proj_chunk(n), s("win_act"))
            act.wait_ge(s("win_dve"), (len(WCHUNKS) + 1) // 2)
            act.wait_ge(s("win_act"), len(WCHUNKS) // 2)
            me.give(act.activation(flat(tmpT), fqkv[:, 0:2 * HC, :].rearrange("p a b -> p (a b)"), ACT.Square), once.give("qk_squared"))
            ada(1)
            act.wait_ge(*once("lf_abs"))
            me.step(act.activation(lftmp[:, 0, :], lftmp[:, 0, :], ACT.Exp), once.give("lf_exp"))
            act.wait_ge(*once("lf_one"))
            me.give(act.activation(lftmp[:, 0, :], lftmp[:, 0, :], ACT.Ln), once.give("lf_ln"))
            act.wait_ge(s("qkms_read"), 6)
            me.give(act.activation(flat(tmpT), flat(tmpT), ACT.Sqrt), once.give("qk_rooted"))
            for n in range(6):
                act.wait_ge(s("kv_turned"), n + 1)
                w = BLK[n % 3][1]
                copy(kvrow[0:w, n // 3, n % 3, :], banks[f"kv{n}"][0:w, :], s("kv_copied"))
            act.wait_ge(*once("lf_turned"))
            for blk, (t0, w) in enumerate(BLK):
                copy(lfrow[0:w, blk, :], banks["lf"][0:w, H * blk:H * (blk + 1)], s("lf_copied"))
            act.wait_ge(*once("last_turned"))
            copy(lastrow[0:NPC * 8, 0, :], banks["last"][0:NPC * 8, 0:P], s("last_copied"))
            copy(lastrow[0:NPC, 1, :], banks["last"][0:NPC, P:2 * P], s("last_copied"))

            for k in range(8):
                nk = P * (k % 2 + 1)
                act.wait_ge(s("shifted"), k + 1)
                v = pr[:, k % 2, :, 0:nk]
                me.give(act.activation(v, v, ACT.Exp), s("exped"))
                act.wait_ge(s("pt_mm"), k + 1)
                if k >= 2:
                    act.wait_ge(s("o_mm"), k - 1)
                nb = k % 2 + 1
                copy(prT[:, k % 2, :, 0:nb, :],
                     banks[f"pt{k // 2}{k % 2}"][:, 0:2 * nb * P].rearrange("p (h j q) -> p h j q", h=2, j=nb), s("probsT"))
                act.wait_ge(s("o_mm"), k + 1)
                copy(yT[:, k // 2, P * (k % 2):P * (k % 2 + 1)], banks[f"o{k // 2}{k % 2}"][:, 0:P], s("o_copied"))
            for q in range(NB):
                for half in range(2):
                    act.wait_ge(s("kt_mm"), 2 * q + half + 1)
                    if q >= 2:
                        act.wait_ge(s("ss_mm"), q - 1)
                    copy(ktb[:, q % 2, 2 * half:2 * half + 2, 0:PAST],
                         banks[f"kt{q}{half}"][:, :].rearrange("p (c k) -> p c k", c=2), s("kt_copied"))
                copy(ktb[:, q % 2, :, PAST:PAST + NT], fqkv[:, HC:2 * HC, NP + NT * q:NP + NT * (q + 1)], s("kt_copied"))
            act.wait_ge(*once("psm_shifted"))
            me.give(act.activation(psm, psm, ACT.Exp), once.give("psm_exped"))
            for g in range(2):
                act.wait_ge(s("pst_mm"), g + 1)
                copy(psT[:, g, 0:2, :], banks[f"pst{g}"][:, 0:2 * P].rearrange("p (j q) -> p j q", j=2), s("psT_ready"))
                copy(psT[0:32, g, 2, :], banks[f"pst{g}"][0:32, 2 * P:3 * P], s("psT_ready"))
            act.wait_ge(*once("so_mm"))
            copy(yT[:, 0:HC, NP:N], banks["so"][:, 0:HC * NS].rearrange("p (c t) -> p c t", c=HC), once.give("so_copied"))

            act.wait_ge(*once("rp_mixed"))
            me.give(act.activation(rp[0:LORA, PWL, :], rp[0:LORA, PWL, :], ACT.Tanh), once.give("wl_tanh"))
            me.give(act.activation(rp[:, PGL, :], rp[:, PGL, :], ACT.Sigmoid), once.give("gl_sigmoid"))
            for name, dst, col in (("dec", lw, VB_W0), ("icl", icl, VB_A0)):
                for c in range(HC):
                    act.wait_ge(*lora(name, "mm", c + 1))
                    me.give(act.activation(dst[:, c, :], banks[f"{name}{c}"][:, 0:N], ACT.Sigmoid,
                                           bias=vT[:, 1, col + c:col + c + 1]), s("lora_ready"))
            for c in range(HC):
                act.wait_ge(*lora("gat", "mm", c + 1))
                copy(gate[:, c, :], banks[f"gat{c}"][:, 0:N], s("lora_ready"))
            act.wait_ge(*once("kk_scaled"))
            me.give(act.activation(flat(tmpT)[:, 0:HC * N], kkT.rearrange("p a b -> p (a b)"), ACT.Square), once.give("kk_squared"))
            act.wait_ge(*sums("kks", "read", 3))
            me.give(act.activation(flat(tmpT)[:, 0:HC * N], flat(tmpT)[:, 0:HC * N], ACT.Sqrt), once.give("kk_rooted"))
            act.wait_ge(*once("cum_ready"))
            me.give(act.activation(lw[:, :, NP:N], lw[:, :, NP:N], ACT.Exp), s("decay_exp"))
            me.give(act.activation(wdec, cumv, ACT.Exp), s("decay_exp"))
            me.give(act.activation(winv, cumv, ACT.Exp, scale=-1.0), s("decay_exp"))
            me.give(act.activation(wprev, wprev, ACT.Exp), s("decay_exp"))
            act.wait_ge(s("mix_stored"), 16 * CACHE_STORES)
            for i in range(6):
                act.wait_ge(s("sr_mm"), i + 1)
                copy(srow[:, i, :], banks[f"sr{i}"][0:NS, :], s("srow_copied"))
            for c in range(HC):
                act.wait_ge(s("odd_mm"), c + 1)
                v = banks[f"odd{c}"][0:L, :].rearrange("p (n a t) -> p n a t", n=NCH, a=2)
                copy(lu[0:L, :, 2 * c + 1, :], v[:, :, 0, :], s("odd_copied"))
                copy(rt[:, :, 2 * c + 1, :], v[:, :, 1, :], s("odd_copied"))
            for pair in range(NCH // 2):
                for n in (2 * pair, 2 * pair + 1):
                    act.wait_ge(s("bkt_mm"), n + 1)
                    copy(bkt[:, n % 2].rearrange("p h k -> p (h k)"), banks[f"bkt{n}"][:, :], s("bkt_ready"))
                    act.wait_ge(s("vt_mm"), n + 1)
                    me.give(act.activation(sav[L:P, n % 2].rearrange("p h k -> p (h k)"), banks[f"vt{n}"][L:P, :], ACT.Copy), chain)
                    me.give(act.activation(su[L:P, n % 2].rearrange("p h k -> p (h k)"), banks[f"vt{n}"][L:P, :], ACT.Copy), s("vt_ready"))
                for lv in range(LEVELS):
                    for n in (2 * pair, 2 * pair + 1):
                        act.wait_ge(s("x_mm"), kth(n, lv) + 1)
                        copy(xb[:, n % 2].rearrange("p h k -> p (h k)"), banks[f"x_{LEVELS * n + lv}"][0:L, :], s("xb_ready"))
                for n in (2 * pair, 2 * pair + 1):
                    act.wait_ge(s("u_mm"), n + 1)
                    copy(ub[:, n % 2].rearrange("p h k -> p (h k)"), banks[f"u{n}"][0:L, :], s("u_ready"))
                    act.wait_ge(s("sa_mm"), n + 1)
                    copy(sav[0:L, n % 2].rearrange("p h k -> p (h k)"), banks[f"sa{n}"][0:L, :], s("sa_ready"))
                    act.wait_ge(s("y_mm"), n + 1)
                    copy(yT[:, HC:2 * HC, L * n:L * (n + 1)], banks[f"y{n}"][:, 0:HC * L].rearrange("p (c t) -> p c t", c=HC),
                         s("yc_copied"))
            act.wait_ge(*once("fst_mm"))
            copy(bkt[:, 0, 0:HC, :], banks["fst"][:, 0:HC * DH].rearrange("p (c k) -> p c k", c=HC), once.give("fst_copied"))
            act.wait_ge(*once("syt_mm"))
            copy(yT[:, HC:2 * HC, NP:N], banks["syt"][:, 0:HC * NS].rearrange("p (c t) -> p c t", c=HC), once.give("syt_copied"))
            act.wait_ge(*once("gn_centred"))
            me.give(act.activation(flat(tmpT)[:, 0:HC * N], flat(yT)[:, HC * N:2 * HC * N], ACT.Square), once.give("gn_squared"))
            act.wait_ge(*sums("gnv", "read", 3))
            me.give(act.activation(flat(tmpT)[:, 0:HC * N], flat(tmpT)[:, 0:HC * N], ACT.Sqrt), once.give("gn_rooted"))

            square_all(1)
            root(1)
            for n in range(FF // P):
                act.wait_ge(s("gate_mm"), n + 1)
                if n >= 2:
                    act.wait_ge(s("act_ready"), n - 1)
                me.give(act.activation(ffsilu[:, n % 2, :], banks[f"gate{n}"][:, 0:N], ACT.Silu), s("silu_ready"))
            square_all(2)
            root(2)
            for half in range(2):
                act.wait_ge(s("pb_mm"), half + 1)
                act.wait_ge(*once("exts_zero"))
                me.give(act.activation(exts[:, 4 * half:4 * half + 4, :, 1:16],
                                       banks[f"pb{half}"][:, 0:480].rearrange("p (c b r) -> p c b r", c=4, r=PBUF),
                                       ACT.Copy), s("pbuf_copied"))
            for half in range(2):
                act.wait_ge(s("hl_mm"), half + 1)
                copy(hlast[0:NS + 16, 512 * half:512 * (half + 1)], banks[f"hl{half}"][0:NS + 16, :], s("hl_copied"))
            square_all(3)
            root(3)
            act.wait_ge(*once("z_used"))
            for n in range(6):
                w = BLK[n // 2][1]
                act.wait_ge(s("ht_mm"), n + 1)
                copy(htok[0:w, n // 2, 512 * (n % 2):512 * (n % 2 + 1)], banks[f"ht{n}"][0:w, :], s("htok_ready"))
            act.wait_ge(*once("top_ready"))
            me.give(act.activation(gate2[:, :, 0], gate2[:, :, 0], ACT.Exp), once.give("top_exped"))
            moe_scalar(act, me)
            for n in range(6):
                w = BLK[n // 2][1]
                act.wait_ge(s("out_mm"), n + 1)
                copy(outrow[0:w, n // 2, 512 * (n % 2):512 * (n % 2 + 1)], banks[f"out{n}"][0:w, :], s("out_copied"))

        @block.vector
        def _(dve):
            me = Counted(dve)
            chain = s("dve_chain")
            TT, TS, STT = dve.tensor_tensor, dve.tensor_scalar, dve.scalar_tensor_tensor

            def do(ins, sem=None):
                me.step(ins, sem or chain)

            dve.wait_ge(s("const_loaded"), 16)
            dve.wait_ge(*once("vec_turned"))
            do(dve.tensor_copy(flat(vT), banks["vec"][:, 0:3 * P]), once.give("vec_copied"))
            qg = vT[:, 1, VB_QG:VB_QG + 1]
            do(TS(qg, qg, DH ** -0.5, None, ALU.mult))
            for n, (blk, c0, nc_) in enumerate(XJOBS):
                t0, w = BLK[blk]
                dve.wait_ge(s("x_turned"), n + 1)
                do(dve.tensor_copy(xT[:, c0:c0 + nc_, t0:t0 + w],
                                   banks[f"x{n}"][:, 0:nc_ * w].rearrange("p (c t) -> p c t", c=nc_)), s("x_copied"))

            def mod_tiles(layer):
                for i in range(12):
                    dve.wait_ge(s("folded"), 12 * layer + i + 1)
                    bias = vT[:, 0, 48 * layer + 4 * i:48 * layer + 4 * i + 4]
                    do(TT(modT[layer][:, 4 * i:4 * i + 4, :], banks[f"fold{layer}_{i}"][:, 0:36].rearrange("p (j m) -> p j m", j=4),
                          spread(bias, 2, 9), ALU.add), s("mod_ready"))

            def mod(i, part):
                at = 24 * (i % 2) + 8 * part
                return modT[i // 2][:, at:at + 8, :]

            def gains(i):
                g = spread(vT[:, 0, VA_NORM[i]:VA_NORM[i] + 8], 2, 9)
                do(TS(gainT[i][:, :, :], mod(i, 1), 1.0, None, ALU.add))
                do(TT(gainT[i][:, :, :], gainT[i][:, :, :], g, ALU.mult))

            def mean_of(i):
                dve.wait_ge(s("ms_ready"), i + 1)
                do(TS(rstd[:, :], banks[f"ms{i}"][:, 0:N], 1.0 / D, RMS_EPS, ALU.mult, ALU.add), s("ms_read"))
                dve.wait_ge(s("rooted"), i + 1)
                do(dve.reciprocal(rstd[:, :], rstd[:, :]))

            def by_seq(ap):
                return ap.rearrange("p c (b t) -> p c b t", t=NT)

            def modulated(i):
                do(TT(hT[:, :, :], xT[:, :, :], spread(rstd[:, :], 1, DC), ALU.mult))
                hs = by_seq(hT[:, :, NP:N])
                do(TT(hs, hs, spread(gainT[i][:, :, 1:9], 3, NT), ALU.mult))
                do(TT(hs, hs, spread(mod(i, 0)[:, :, 1:9], 3, NT), ALU.add))
                for c in range(DC):
                    v = hT[:, c, 0:NP]
                    me.give(TS(v, v, gainT[i][:, c, 0:1], mod(i, 0)[:, c, 0:1], ALU.mult, ALU.add), chain)
                dve.wait_ge(chain, me.n[chain.name])
                do(dve.memset(small[:, 60:61], 0.0), s("h_ready"))

            def residual(src, gate_, j):
                do(STT(xT[:, j, 0:NP], src[:, 0:NP], gate_[:, j, 0:1], xT[:, j, 0:NP], ALU.mult, ALU.add))

            def residual_samples(src, gate_, j, sem):
                t = small[:, 0:NS]
                do(TT(t.rearrange("p (b t) -> p b t", t=NT), src[:, NP:N].rearrange("p (b t) -> p b t", t=NT),
                      spread(gate_[:, j, 1:9], 2, NT), ALU.mult), sem)
                do(TT(xT[:, j, NP:N], xT[:, j, NP:N], t, ALU.add))

            mean_of(0)
            mod_tiles(0)
            gains(0)
            gains(1)
            modulated(0)

            dve.wait_ge(*once("last_zero"))
            for n in range(0, len(WCHUNKS), 2):
                kind, idx, _, m = WCHUNKS[n]
                dve.wait_ge(s("win_mm"), n + 1)
                src = banks[f"win{n}"][0:m, 0:N]
                if kind == "l":
                    do(TS(rstd[0:H, :], src, fbias[:, 0:1], None, ALU.add), s("win_dve"))
                else:
                    do(dve.tensor_copy({"f": fqkv, "r": rp}[kind][0:m, idx, :], src), s("win_dve"))
            mod_tiles(1)
            gains(2)
            gains(3)
            gp = mod(2, 2)
            do(TT(gp, gp, spread(vT[:, 1, VB_PS:VB_PS + 8], 2, 9), ALU.mult))

            z = rstd[0:H, :]
            t0, t1 = lftmp[:, 0, :], lftmp[:, 1, :]
            dve.wait_ge(s("ada_mm"), 24)
            do(TS(t1, z, -1.0, None, ALU.mult))
            do(TT(t0, z, t1, ALU.min), once.give("lf_abs"))
            dve.wait_ge(*once("lf_exp"))
            do(TS(t0, t0, 1.0, None, ALU.add), once.give("lf_one"))
            do(TS(t1, z, 0.0, None, ALU.min))
            for i in range(6):
                dve.wait_ge(s("qkms"), i + 1)
                do(TS(flat(tmpT)[:, 384 * i:384 * (i + 1)], banks[f"qkms{i}"][:, 0:384], 1.0 / DH, RMS_EPS, ALU.mult, ALU.add),
                   s("qkms_read"))
            dve.wait_ge(*once("lf_ln"))
            do(TT(logf, t1, t0, ALU.subtract), once.give("logf_ready"))
            do(dve.tensor_tensor_scan(negF, K("restart", H), logf, 0.0, ALU.mult, ALU.add))
            do(TS(negF, negF, -1.0, None, ALU.mult), once.give("negF_ready"))
            dve.wait_ge(*once("qk_rooted"))
            do(dve.reciprocal(flat(tmpT), flat(tmpT)))
            dve.wait_ge(s("win_act"), len(WCHUNKS) // 2)
            for part, g, sem in ((1, VB_KG, "k_ready"), (0, VB_QG, "q_ready")):
                v = fqkv[:, HC * part:HC * (part + 1), :].rearrange("p a b -> p (a b)")
                r = flat(tmpT)[:, HC * N * part:HC * N * (part + 1)]
                do(STT(v, v, vT[:, 1, g:g + 1], r, ALU.mult, ALU.mult), once.give(sem))
            do(dve.tensor_copy(lastP, rp[:, :, NP - 1]))
            do(dve.tensor_copy(lastS, rp[:, :, NP + NT - 1:N:NT]), once.give("last_ready"))
            do(TT(diff[:, :, 1:NP], rp[:, :, 0:NP - 1], rp[:, :, 1:NP], ALU.subtract))
            do(TS(diff[:, :, 0], rp[:, :, 0], -1.0, None, ALU.mult))
            rs, ds_ = by_seq(rp[:, :, NP:N]), by_seq(diff[:, :, NP:N])
            do(TT(ds_[:, :, :, 1:NT], rs[:, :, :, 0:NT - 1], rs[:, :, :, 1:NT], ALU.subtract))
            prev = vT[:, 2, 0:NPC * NB].rearrange("p (c b) -> p c b", c=NPC)
            do(TT(ds_[:, :, :, 0], prev, rs[:, :, :, 0], ALU.subtract))
            do(TT(diff, diff, spread(vT[:, 1, VB_MU:VB_MU + NPC], 2, N), ALU.mult))
            do(TT(rp, rp, diff, ALU.add), once.give("rp_mixed"))

            for k in range(8):
                qb = k % 2
                nk = P * (qb + 1)
                if k >= 2:
                    dve.wait_ge(s("pt_mm"), k - 1)
                for par in range(2):
                    dve.wait_ge(s("s_mm"), 2 * k + par + 1)
                    do(TT(pr[:, k % 2, par, 0:nk], banks[f"s{k // 2}{qb}{par}"][:, 0:nk], K("causal")[:, 256 - nk:256], ALU.add),
                       s("scored"))
                v, m = pr[:, k % 2, :, 0:nk], small[:, 40:42]
                do(dve.tensor_reduce(m, v, AX.X, ALU.max))
                do(TT(v, v, spread(m, 2, nk), ALU.subtract), s("shifted"))
                dve.wait_ge(s("exped"), k + 1)
                do(dve.tensor_reduce(m, v, AX.X, ALU.add))
                do(dve.reciprocal(m, m))
                do(TT(v, v, spread(m, 2, nk), ALU.mult), s("probs"))
            for q in range(NB):
                dve.wait_ge(s("ss_mm"), q + 1)
                do(dve.tensor_copy(psm[32 * (q % 4):32 * (q % 4) + 32, q // 4, :], banks[f"ss{q}"][0:32, 0:PAST + NT]), s("ss_copied"))
            do(TT(psm[:, :, PAST:PAST + NT], psm[:, :, PAST:PAST + NT], spread(K("newmask"), 1, 2), ALU.add))
            m = small[:, 42:44]
            do(dve.tensor_reduce(m, psm, AX.X, ALU.max))
            do(TT(psm, psm, spread(m, 2, PAST + NT), ALU.subtract), once.give("psm_shifted"))
            dve.wait_ge(*once("psm_exped"))
            do(dve.tensor_reduce(m, psm, AX.X, ALU.add))
            do(dve.reciprocal(m, m))
            do(TT(psm, psm, spread(m, 2, PAST + NT), ALU.mult))
            for g in range(2):
                do(TT(pnew[:, g, :, :], spread(psm[:, g, PAST:PAST + NT], 1, NB),
                      spread(K("seqmask")[:, 8 * g:8 * g + 8], 2, NT), ALU.mult), chain if g == 0 else once.give("psm_ready"))

            kx, rx, vx = rp[:, PK:PK + HC, :], rp[:, PR:PR + HC, :], rp[:, PV:PV + HC, :]

            def fl(t):
                return t.rearrange("p a b -> p (a b)")

            dve.wait_ge(*once("so_mm"))
            dve.wait_ge(s("mix_stored"), 16 * CACHE_STORES)
            for c in range(HC):
                do(TS(kkT[:, c, :], kx[:, c, :], vT[:, 1, VB_KK + c:VB_KK + c + 1], None, ALU.mult),
                   once.give("kk_scaled") if c == HC - 1 else chain)
            dve.wait_ge(*lora("icl", "ready", HC))
            dve.wait_ge(*lora("dec", "ready", HC))
            for c in range(HC):
                t = flat(tmpT)[:, HC * N + N * c:HC * N + N * (c + 1)]
                do(TS(t, icl[:, c, :], -1.0, vT[:, 1, VB_KA + c:VB_KA + c + 1], ALU.add, ALU.mult))
                do(STT(kx[:, c, :], t, 1.0, kx[:, c, :], ALU.add, ALU.mult))
                do(STT(t, rx[:, c, :], vT[:, 1, VB_RK + c:VB_RK + c + 1], kx[:, c, :], ALU.mult, ALU.mult),
                   once.give("rk_ready") if c == HC - 1 else chain)
            for i in range(3):
                dve.wait_ge(*sums("kks", "mm", i + 1))
                do(TS(flat(tmpT)[:, 384 * i:384 * (i + 1)], banks[f"kks{i}"][:, 0:384], 1e-24, None, ALU.max), s("sums_read"))
            dve.wait_ge(*once("kk_rooted"))
            r = flat(tmpT)[:, 0:HC * N]
            do(dve.reciprocal(r, r))
            do(TT(fl(kkT), fl(kkT), r, ALU.mult))
            do(TT(fl(bT), fl(kkT), fl(icl), ALU.mult))
            do(TS(fl(kkT), fl(kkT), -1.0, None, ALU.mult))
            for i in range(3):
                dve.wait_ge(*sums("bon", "mm", i + 1))
                o = slice(384 * i, 384 * (i + 1))
                do(TT(fl(icl)[:, o], banks[f"bon{i}"][:, 0:384], fl(vx)[:, o], ALU.mult), s("sums_read"))
            do(TS(fl(lw), fl(lw), -DECAY, None, ALU.mult))
            for c in range(HC):
                do(dve.tensor_tensor_scan(cumv[:, c, :], K("reset"), lw[:, c, 0:NP], 0.0, ALU.mult, ALU.add))
            do(TT(wprev, cumv, lw[:, :, 0:NP], ALU.subtract), once.give("cum_ready"))
            dve.wait_ge(s("decay_exp"), 4)
            do(dve.memset(small[:, 61:62], 0.0), once.give("delta_ops"))

            def chunks(ap):
                return ap[:, :, 0:NP].rearrange("p c (n t) -> p c n t", t=L)

            do(TT(ar[:, :, :, 0, :], chunks(kkT), chunks(wprev), ALU.mult))
            do(TT(ar[:, :, :, 1, :], chunks(rx), chunks(wdec), ALU.mult))
            do(TT(bk[:, :, :, 0, :], chunks(bT), chunks(winv), ALU.mult))
            do(TT(bk[:, :, :, 1, :], chunks(kx), chunks(winv), ALU.mult))
            do(dve.tensor_copy(zv[:, :, :, 1, :], chunks(vx)))
            do(dve.memset(zv[:, :, :, 0, :], 0.0), once.give("packed"))
            dve.wait_ge(*once("oddw_mm"))
            do(dve.tensor_copy(wlx.rearrange("p (c a) n -> p c a n", a=2)[:, :, 1, :],
                               banks["oddw"][0:L, 0:HC * NCH].rearrange("p (c n) -> p c n", c=HC)), once.give("oddw_copied"))
            do(dve.tensor_copy(wlx.rearrange("p (c a) n -> p c a n", a=2)[:, :, 0, :],
                               wdec[0:L].rearrange("p c (n t) -> p c n t", t=L)[:, :, :, L - 1]))
            do(dve.memset(su[0:L, 0], 0.0), s("su_ready"))

            def rows(t, i):
                return spread(svec[:, t, i, :], 1, 32)

            def sample_ops():
                dve.wait_ge(s("svec_loaded"), 16 * 3 * NB)
                dve.wait_ge(s("sst_loaded"), 16)
                for t in range(NT):
                    yield lambda t=t: do(TT(sprod, sst, rows(t, 1), ALU.mult))
                    yield lambda t=t: do(dve.tensor_reduce(ssa, sprod, AX.X, ALU.add))
                    yield lambda t=t: do(TT(sst, sst, rows(t, 0), ALU.mult))
                    yield lambda t=t: do(TT(sprod, spread(ssa, 2, DH), rows(t, 2), ALU.mult))
                    yield lambda t=t: do(TT(sst, sst, sprod, ALU.add))
                    yield lambda t=t: do(TT(sprod, spread(sval[:, t, :], 2, DH), rows(t, 3), ALU.mult))
                    yield lambda t=t: do(TT(sst, sst, sprod, ALU.add))
                    yield lambda t=t: do(TT(sprod, sst, rows(t, 4), ALU.mult))
                    yield lambda t=t: do(dve.tensor_reduce(sy[:, t, :], sprod, AX.X, ALU.add), s("sy_ready"))

            pending = sample_ops()

            def some(k):
                for _, op in zip(range(k), pending):
                    op()

            def fh(ap):
                return ap.rearrange("p h k -> p (h k)")

            for pair in range(NCH // 2):
                for n in (2 * pair, 2 * pair + 1):
                    for par in range(2):
                        dve.wait_ge(s("gt_mm"), 2 * n + par + 1)
                        do(TT(gt[:, n % 2].rearrange("p (c a) t -> p c a t", a=2)[:, :, par, :],
                              banks[f"gt{n}{par}"][:, :].rearrange("p (c t) -> p c t", c=HC),
                              spread(K("chunk"), 1, HC), ALU.mult), s("gt_ready"))
                for lv in range(LEVELS):
                    for n in (2 * pair, 2 * pair + 1):
                        i = n % 2
                        if lv == 0:
                            dve.wait_ge(s("x_mm"), kth(n, lv) + 1)
                            dve.wait_ge(s("xb_ready"), kth(n, lv) + 1)
                            idb = spread(K("ident")[0:L, 0:L], 1, H)
                            do(TT(tb[:, i], xb[:, i], idb, ALU.add), s("t_ready"))
                            do(TT(tt[:, i], nm[:, i], idb, ALU.add), s("t_ready"))
                            continue
                        if lv < LEVELS - 1:
                            dve.wait_ge(s("t_mm"), t_mms(n, lv) - 1)
                            do(TT(fh(tb[:, i]), fh(tb[:, i]), banks[f"t_{n}{lv}"][0:L, :], ALU.add), s("t_ready"))
                        dve.wait_ge(s("t_mm"), t_mms(n, lv))
                        do(TT(fh(tt[:, i]), fh(tt[:, i]), banks[f"tt_{n}{lv}"][0:L, :], ALU.add), s("t_ready"))
                    some(3)
                for n in (2 * pair, 2 * pair + 1):
                    i = n % 2
                    dve.wait_ge(s("st_mm"), n + 1)
                    nxt = su[0:L, (n + 1) % 2]
                    do(TT(fh(nxt), fh(su[0:L, i]), banks[f"st{n}"][0:L, :], ALU.add), s("state_read"))
                    do(TT(nxt, nxt, spread(wlx[:, :, n], 2, DH), ALU.mult), s("su_ready") if n < NCH - 1 else once.give("final_state"))
            some(36)

            y2 = flat(yT)[:, HC * N:2 * HC * N]
            for i in range(3):
                o = slice(384 * i, 384 * (i + 1))
                dve.wait_ge(*sums("gnm", "mm", 3 if i == 0 else i + 1))
                do(STT(y2[:, o], banks[f"gnm{i}"][:, 0:384], -1.0 / DH, y2[:, o], ALU.mult, ALU.add), s("sums_read"))
            do(dve.memset(small[:, 62:63], 0.0), once.give("gn_centred"))
            for i in range(3):
                dve.wait_ge(*sums("gnv", "mm", i + 1))
                do(TS(flat(tmpT)[:, 384 * i:384 * (i + 1)], banks[f"gnv{i}"][:, 0:384], 1.0 / DH, GN_EPS, ALU.mult, ALU.add),
                   s("sums_read"))
            dve.wait_ge(*once("gn_rooted"))
            do(dve.reciprocal(r, r))
            do(TT(y2, y2, r, ALU.mult))
            for c in range(HC):
                v = yT[:, HC + c, :]
                do(TS(v, v, vT[:, 1, VB_LNW + c:VB_LNW + c + 1], vT[:, 1, VB_LNB + c:VB_LNB + c + 1], ALU.mult, ALU.add))
            do(TT(y2, y2, fl(icl), ALU.add))
            dve.wait_ge(*lora("gat", "ready", HC))
            do(TT(y2, y2, fl(gate), ALU.mult), once.give("mix_ready"))

            for j in range(DC):
                dve.wait_ge(s("wo_mm"), j + 1)
                src = banks[f"wo{j}"]
                residual(src, mod(0, 2), j)
                residual_samples(src, mod(0, 2), j, s("res1"))
            do(dve.memset(small[:, 63:64], 0.0), s("res"))
            mean_of(1)
            modulated(1)

            def hidden(i):
                for n in range(4 * i, min(4 * i + 4, FF // P)):
                    dve.wait_ge(s("silu_ready"), n + 1)
                    dve.wait_ge(s("up_mm"), n + 1)
                    if i >= 2:
                        dve.wait_ge(s("down_mm"), DC * (i - 1))
                    do(TT(ffact[:, i % 2, n % 4, :], ffsilu[:, n % 2, :], banks[f"up{n}"][:, 0:N], ALU.mult), s("act_ready"))

            def down(i):
                for j in range(DC):
                    dve.wait_ge(s("down_mm"), DC * i + j + 1)
                    src = banks[f"down{i}_{j}"][:, 0:N]
                    if i == 0:
                        do(dve.tensor_copy(yT[:, j, :], src), s("ff_added"))
                    else:
                        do(TT(yT[:, j, :], yT[:, j, :], src, ALU.add), s("ff_added"))

            hidden(0)
            for i in range(1, 6):
                hidden(i)
                down(i - 1)
            down(5)
            for j in range(DC):
                residual(yT[:, j, :], mod(1, 2), j)
                residual_samples(yT[:, j, :], mod(1, 2), j, chain)
            do(dve.memset(small[:, 59:60], 0.0), s("res"))

            do(dve.memset(exts[:, :, :, 0], 0.0), once.give("exts_zero"))
            do(dve.memset(ext[:, :, 0:16], 0.0))
            mean_of(2)
            modulated(2)
            do(dve.tensor_copy(ext[:, :, 16:16 + NP], hT[:, :, 0:NP]))
            dve.wait_ge(s("pbuf_copied"), 2)
            hs = by_seq(hT[:, :, NP:N])
            do(dve.tensor_copy(exts[:, :, :, 16:20], hs))
            ext2 = flat(tmpT)[:, 0:DC * (16 + NP)].rearrange("p (c t) -> p c t", c=DC)
            exts2 = other[:, 0:DC * NB * 20].rearrange("p (c b t) -> p c b t", c=DC, b=NB)
            pair_ = [(ext, exts), (ext2, exts2)]
            for lv in range(4):
                (a0, b0), (a1, b1) = pair_[lv % 2], pair_[1 - lv % 2]
                sh, c0, lo = 1 << lv, 2 * lv, (2 << lv) - 1
                do(TT(a1[:, c0:DC, lo:], a0[:, c0:DC, lo:], a0[:, c0:DC, lo - sh:16 + NP - sh], ALU.add))
                do(TT(b1[:, c0:DC, :, lo:], b0[:, c0:DC, :, lo:], b0[:, c0:DC, :, lo - sh:20 - sh], ALU.add))
                g = slice(c0, c0 + 2)
                do(STT(yT[:, g, 0:NP], a1[:, g, 16:16 + NP], 1.0 / WINS[lv], hT[:, g, 0:NP], ALU.mult, ALU.subtract))
                head = yT[:, g, 0:16]
                cnt = K("count").rearrange("p (g t) -> p g t", g=4)[:, lv, :]
                do(TT(head, a1[:, g, 16:32], spread(cnt, 1, 2), ALU.mult))
                do(TT(head, head, hT[:, g, 0:16], ALU.subtract))
                for c in (c0, c0 + 1):
                    do(STT(by_seq(yT[:, :, NP:N])[:, c], b1[:, c, :, 16:20], 1.0 / WINS[lv], hs[:, c], ALU.mult, ALU.subtract))
            do(dve.memset(small[:, 58:59], 0.0), once.give("z_ready"))
            for j in range(DC):
                dve.wait_ge(s("pool_mm"), j + 1)
                src = banks[f"pool{j}"]
                residual(src, mod(2, 2), j)
                residual_samples(src, mod(2, 2), j, s("res3"))
            do(dve.memset(small[:, 57:58], 0.0), s("res"))
            mean_of(3)
            modulated(3)
            dve.wait_ge(s("pool_stored"), 16 * (2 + NB))
            for table in (comb, slot_at, later):
                do(dve.memset(table, 0.0))
            do(dve.memset(flat(yT), 0.0), once.give("z_used"))

            dve.wait_ge(*once("route_mm"))
            for blk, (t0_, w) in enumerate(BLK):
                lg = logit[0:w, blk, :]
                do(TT(lg, banks["route"][0:w, NE * blk:NE * (blk + 1)], routerb[0:w, :], ALU.add), s("logits"))
                do(dve.max(top[0:w, blk, :], lg))
                do(dve.max_index(topi[0:w, blk, :].bitcast(U32), top[0:w, blk, :], lg))
                do(dve.tensor_copy(logit[0:w, blk, 0:2], topi[0:w, blk, 0:2].bitcast(U32)))
                for k, dst in enumerate((pick, comb)):
                    do(TS(dst[0:w, blk, 0:NE], K("iota")[0:w, 0:NE], logit[0:w, blk, k:k + 1], None, ALU.is_equal))
                do(TT(gate2[0:w, blk, 0:1], top[0:w, blk, 1:2], top[0:w, blk, 0:1], ALU.subtract),
                   once.give("top_ready") if blk == 2 else chain)
            dve.wait_ge(*once("top_exped"))
            for blk, (t0_, w) in enumerate(BLK):
                e, one, lo_, hi_ = (gate2[0:w, blk, i:i + 1] for i in range(4))
                do(TS(one, e, 1.0, None, ALU.add))
                do(dve.reciprocal(hi_, one))
                do(TT(lo_, e, hi_, ALU.mult))
                first, second = pick[0:w, blk, :], comb[0:w, blk, 0:NE]
                do(TT(logit[0:w, blk, :], first, second, ALU.add))
                do(TS(first, first, hi_, None, ALU.mult))
                do(STT(second, second, lo_, first, ALU.mult, ALU.add))
                do(dve.tensor_copy(first, logit[0:w, blk, :]), once.give("picked") if blk == 2 else chain)
            dve.wait_ge(*once("rank_mm"))
            do(dve.tensor_copy(small[:, 48:56], banks["rank"][:, 3 * NE:4 * NE]))
            for blk, (t0_, w) in enumerate(BLK):
                sl = slot_at[0:w, blk, 0:NE]
                do(STT(sl, banks["rank"][0:w, NE * blk:NE * (blk + 1)], 1.0, pick[0:w, blk, :], ALU.add, ALU.mult),
                   s("ranked"))
                do(TS(sl, sl, -1.0, None, ALU.add))
                for p in range(1, PASSES):
                    do(TS(later[0:w, blk, NE * (p - 1):NE * p], sl, -128.0 * p, None, ALU.add))
            count = moe_vector(dve, do)
            dve.wait_ge(s("comb_added"), count * DC)
            for j in range(DC):
                residual(yT[:, j, :], mod(3, 2), j)
                residual_samples(yT[:, j, :], mod(3, 2), j, chain)
            do(dve.memset(small[:, 56:57], 0.0), once.give("res4"))

        @block.gpsimd
        def _(pool):
            me = Counted(pool)
            me.step(pool.memset(vrow[:, 1:3, :], 0.0), once.give("vrow_zero"))
            me.step(pool.memset(silucT[:, :, :], 0.0), once.give("silucT_zero"))
            pool.wait_ge(s("x_turned"), len(XJOBS))
            me.step(pool.memset(rp[LORA:P, PWL, :], 0.0), s("pool_chain"))
            me.step(pool.memset(rp[LORA:P, PAL, :], 0.0), once.give("last_zero"))
            pool.wait_ge(s("ada_mm"), 24)
            me.step(pool.memset(qbd, 0.0), s("pool_chain"))
            pool.wait_ge(*once("q_ready"))
            for c in range(HC):
                for par in range(2):
                    p0, at = DH * par, NT * (2 * c + par)
                    me.step(pool.tensor_copy(qbd[p0:p0 + DH, :, c, at:at + NT],
                                             fqkv[p0:p0 + DH, c, NP:N].rearrange("p (q t) -> p q t", t=NT)), s("qbd_ready"))
            stores = []

            def store(dst, src):
                pool.dma_start(dst, src).then_inc(s("mix_stored"), 16)
                stores.append(1)

            pool.wait_ge(s("kv_copied"), 6)
            for i, (dp, dsm) in enumerate(((k_p, k_s), (v_p, v_s))):
                store(dp[0, 0].rearrange("(b p) h d -> p b (h d)", p=P), kvrow[:, i, 0:2, :])
                store(dsm[0].rearrange("b t h d -> (b t) (h d)"), kvrow[0:NS, i, 2, :])
            pool.wait_ge(s("lf_copied"), 3)
            store(lf_p[0, 0].rearrange("(b p) h -> p b h", p=P), lfrow[:, 0:2, :])
            store(lf_s[0].rearrange("b t h -> (b t) h"), lfrow[0:NS, 2, :])
            pool.wait_ge(s("last_copied"), 2)
            for i, (at, w) in enumerate(PIECES):
                store(sh_s[0][:, at:at + w], lastrow[NB * i:NB * (i + 1), 0, 0:w])
                store(sh_p[0][:, at:at + w], lastrow[i:i + 1, 1, 0:w])
            assert len(stores) == CACHE_STORES
            for q in range(NB):
                pool.wait_ge(s(f"k_page{q % 2}"), 64 * (q // 2 + 1))
                me.step(pool.tensor_copy(pastlf4[:, q].rearrange("p j (h t) -> p j h t", t=NT),
                                         spread(pastlf[:, q], 3, NT)), s("lf_spread"))
            pool.wait_ge(*once("packed"))
            lu5 = lu[0:L].rearrange("p n (c a) t -> p n c a t", a=2)
            rt5 = rt.rearrange("p n (c a) t -> p n c a t", a=2)
            for c in range(HC):
                me.step(pool.tensor_copy(lu5[:, :, c, 0, :], ar[0:L, c, :, 0, :]), s("even_copied") if c == HC - 1 else s("pool_chain"))
            for c in range(HC):
                me.step(pool.tensor_copy(rt5[:, :, c, 0, :], ar[0:L, c, :, 1, :]), s("even_copied") if c == HC - 1 else s("pool_chain"))

            def level(n, lv):
                mask = spread(K("levels")[0:L, L * lv:L * (lv + 1)], 1, H)
                me.step(pool.tensor_tensor(nm[:, n % 2], gt[0:L, n % 2, :, 0:L], mask, ALU.mult), s("nm_ready"))

            for pair in range(NCH // 2):
                both = (2 * pair, 2 * pair + 1)
                for n in both:
                    pool.wait_ge(s("gt_ready"), 2 * n + 2)
                    level(n, 0)
                for n in both:
                    me.step(pool.tensor_copy(lu[L:P, n], gt[L:P, n % 2, :, 0:L]), s("lu_ready"))
                for lv in range(1, LEVELS):
                    for n in both:
                        pool.wait_ge(s("x_mm"), kth(n, lv - 1) + 1)
                        if lv == 1:
                            pool.wait_ge(s("t_ready"), t_count(n, 0))
                        level(n, lv)
            pool.wait_ge(*once("fst_copied"))
            store(st_p[0, 0].rearrange("(c a) v k -> (a v) c k", a=2), bkt[:, 0, 0:HC, :])
            pool.wait_ge(s("sy_ready"), NT)
            store(st_s[0].rearrange("b h (f v) k -> (b h f) (v k)", f=2), sst.rearrange("p v k -> p (v k)"))
            mix_stores[0] = len(stores)
            pool.wait_ge(s("mix_stored"), 16 * len(stores))
            pool.dma_start(pool_s[0][:, 0:PBUF - NT, :], a["state_pool"][0][:, NT:PBUF, :]).then_inc(s("pool_stored"), 16)
            pool.wait_ge(s("hl_copied"), 2)
            pool.dma_start(pool_p[0, 0], hlast[1:16, :]).then_inc(s("pool_stored"), 16)
            for q in range(NB):
                pool.dma_start(pool_s[0, q, PBUF - NT:PBUF, :], hlast[16 + NT * q:16 + NT * (q + 1), :]).then_inc(s("pool_stored"), 16)
            pool.wait_ge(s("pool_stored"), 16 * (2 + NB))

        @block.sync
        def _(sp):
            sp.dma_start(const[:, :], a["constants"]).then_inc(s("const_loaded"), 16)
            sp.dma_start(crow[0:1, :], a["c_prompt"]).then_inc(s("c_loaded"), 16)
            sp.dma_start(crow[1:9, :], a["c_sample"]).then_inc(s("c_loaded"), 16)
            for blk in range(2):
                sp.dma_start(xrow[:, blk, :], a["x_prompt"][0, P * blk:P * (blk + 1), :]).then_inc(s("x_loaded"), 16)
            sp.dma_start(xrow[0:NS, 2, :], a["x_sample"].rearrange("b t d -> (b t) d")).then_inc(s("x_loaded"), 16)

            def load(g):
                if g >= SLOTS:
                    sp.wait_ge(*used(g - SLOTS))
                dst, src = tile_source(g)
                sp.dma_start(dst, src).then_inc(s(f"slot{g % SLOTS}"), 16)

            for g in range(4):
                load(g)
            small_loads = [(w2[:, :], a["rwkv_w2"][0]), (a2[:, :], a["rwkv_a2"][0]), (g2[:, :], a["rwkv_g2"][0]),
                           (fbias[:, :], a["fox_f_bias"].rearrange("o h -> h o")),
                           (routerw[:, :, :], a["moe_router_w"][0].rearrange("(c p) e -> p c e", p=P)),
                           (routerb[:, :], a["moe_router_b"].to_broadcast([P, NE])),
                           (pages[:, :], a["page_table"].rearrange("b j -> (b j)").unsqueeze(0))]
            for dst, src in small_loads:
                sp.dma_start(dst, src).then_inc(s("small_loaded"), 16)
            for g in range(4, MIX_TILE):
                load(g)
            sp.wait_ge(s("ada_mm"), 24)
            sp.dma_start(sst.rearrange("p v k -> p (v k)"),
                         a["state_rwkv"][0].rearrange("b h (f v) k -> (b h f) (v k)", f=2)).then_inc(s("sst_loaded"), 16)
            sp.wait_ge(s("small_loaded"), 16 * len(small_loads))
            for q in range(NB):
                if q >= 2:
                    sp.wait_ge(s("kt_mm"), 2 * (q - 1))
                for j in range(NPG):
                    page = sp.value_load(pages[0:1, NPG * q + j:NPG * q + j + 1], min_val=0,
                                         max_val=a["cache_fox_k"].shape[1] - 1)
                    for dst, name, sem in ((ksamp[:, q % 2, j, :], "cache_fox_k", f"k_page{q % 2}"),
                                           (vsamp[:, q, j, :], "cache_fox_v", "v_pages")):
                        sp.dma_start(dst, a[name][0, bass.ds(page, 1)].rearrange("o p h d -> (o p) (h d)")).then_inc(s(sem), 16)
                    sp.dma_start(pastlf[:, q, j, :], a["cache_fox_logf"][0, bass.ds(page, 1)].rearrange("o p h -> (o p) h"))\
                        .then_inc(s(f"k_page{q % 2}"), 16)
            sp.wait_ge(s("srow_copied"), 6)
            sp.dma_start(scratch.rearrange("b t q h k -> (b t) (q h k)"), srow.rearrange("p q k -> p (q k)")).then_inc(s("srow_stored"), 16)
            sp.wait_ge(s("srow_stored"), 16)
            for q in range(NB):
                for f in range(2):
                    sp.dma_start(svec[2 * H * q + f:2 * H * (q + 1):2].rearrange("p t i k -> p (t i) k"),
                                 scratch[q].rearrange("t i h k -> h (t i) k")).then_inc(s("svec_loaded"), 16)
                sp.dma_start(sval[2 * H * q:2 * H * (q + 1)], scratch[q, :, 5].rearrange("t h (f k) -> (h f) t k", f=2))\
                    .then_inc(s("svec_loaded"), 16)
            sp.wait_ge(s("sy_ready"), NT)
            for q in range(NB):
                sp.dma_start(scratch_y[q].rearrange("t f k -> f t k"), sy[2 * H * q:2 * H * (q + 1)]).then_inc(s("sy_stored"), 16)
            sp.wait_ge(s("sy_stored"), 16 * NB)
            sp.dma_start(syrow, scratch_y.rearrange("b t f k -> (b t) (f k)")).then_inc(s("syrow_loaded"), 16)
            sp.wait_ge(*once("mix_ready"))
            sp.wait_ge(s("mix_stored"), 16 * mix_stores[0])
            sp.dma_start(prow[0:NB * PBUF, :], a["state_pool"][0].rearrange("b r d -> (b r) d")).then_inc(s("pool_rows"), 16)
            sp.dma_start(poolw, a["pool_w"][0].rearrange("g (c p) f -> p g c f", p=P)).then_inc(s("poolw_loaded"), 16)
            for g in range(MIX_TILE, len(TILES)):
                load(g)
            moe_sync(sp)
            sp.wait_ge(s("out_copied"), 6)
            sp.dma_start(y_p[0].rearrange("(b p) d -> p b d", p=P), outrow[:, 0:2, :]).then_inc(s("y_stored"), 16)
            sp.dma_start(y_s.rearrange("b t d -> (b t) d"), outrow[0:NS, 2, :]).then_inc(s("y_stored"), 16)
            sp.wait_ge(s("y_stored"), 32)


INPUTS = ["x_prompt", "x_sample", "c_prompt", "c_sample", "cache_fox_k", "cache_fox_v", "cache_fox_logf", "page_table",
          "state_rwkv", "state_rwkv_shift", "state_pool", "norm1_g", "norm2_g", "ada_w", "ada_b", "w_in", "w_out",
          "fox_q_gain", "fox_k_gain", "fox_f_bias", "rwkv_mu", "rwkv_w0", "rwkv_w2", "rwkv_a0", "rwkv_a2", "rwkv_g2",
          "rwkv_k_k", "rwkv_k_a", "rwkv_r_k", "rwkv_ln_w", "rwkv_ln_b", "ffn_w_gate", "ffn_w_up", "ffn_w_down",
          "pool_w", "pool_scale", "moe_router_w", "moe_router_b", "moe_w_gate", "moe_w_up", "moe_w_down"]
OUTPUTS = [(1, NP, D), (NB, NT, D), (1, 1, NP, H, DH), (1, NB, NT, H, DH), (1, 1, NP, H, DH), (1, NB, NT, H, DH),
           (1, 1, NP, H), (1, NB, NT, H), (1, 1, H, DH, DH), (1, NB, H, DH, DH), (1, 1, RW_IN), (1, NB, RW_IN),
           (1, 1, PBUF, D), (1, NB, PBUF, D)]


def kernel(**inputs):
    import concourse.bacc as bacc
    from concourse.bass_utils import run_bass_kernel_spmd

    nc = bacc.Bacc("TRN2", target_bir_lowering=False, num_devices=1)
    arrays, args = {}, {}
    for name in INPUTS + ["constants"]:
        x = constants() if name == "constants" else np.ascontiguousarray(inputs[name])
        arrays[f"in_{name}"] = x
        args[name] = nc.dram_tensor(f"in_{name}", x.shape, mybir.dt.from_np(x.dtype), kind="ExternalInput").ap()
    outs = [nc.dram_tensor(f"out_{i}", shape, F32, kind="ExternalOutput").ap() for i, shape in enumerate(OUTPUTS)]
    build_program(nc, args, *outs)
    r = run_bass_kernel_spmd(nc, [arrays], core_ids=[0])
    return tuple(r.results[0][f"out_{i}"] for i in range(len(OUTPUTS)))
```

```python
from contextlib import ExitStack

import numpy as np

import concourse.bass as bass
from concourse import mybir

F32 = mybir.dt.float32
I32 = mybir.dt.int32
U32 = mybir.dt.uint32
ALU = mybir.AluOpType
ACT = mybir.ActivationFunctionType
AX = mybir.AxisListType

P = 128
D = 1024
DC = D // P
NP, NB, NT = 256, 8, 4
NS = NB * NT
N = NP + NS
BLK = [(0, 128), (128, 128), (256, 32)]
H, DH = 8, 64
HW = H * DH
HC = HW // P
LORA, GLORA = 64, 128
FOX_IN = 3 * HW + H
RW_IN = 3 * HW + 2 * LORA + GLORA
IN_W = FOX_IN + RW_IN
PAGE, NPG, PAST = 128, 2, 256
FF = 2816
NE, FE = 8, 3584
CAP, HALF = 192, 64
MORE = (2 * N - 1) // CAP
ITEMS = NE + MORE
PBUF = 15
WINS = (2, 4, 8, 16)
RMS_EPS, GN_EPS, NEG = 1e-6, 64e-5, -1e30
DECAY = float(np.exp(-0.5))
L = 64
NCH = NP // L
LEVELS = 6

PIECES = ([(P * i, P) for i in range(HC)] + [(HW, LORA)] + [(HW + LORA + P * i, P) for i in range(HC)]
          + [(2 * HW + LORA + P * i, P) for i in range(HC)] + [(3 * HW + LORA, LORA), (3 * HW + 2 * LORA, GLORA)])
NPC = len(PIECES)
PR, PWL, PK, PV, PAL, PGL = 0, 4, 5, 9, 13, 14

CONST = {}
_at = 0
for _name, _n in [("ident", 128), ("before", 128), ("suffix0", 260), ("suffix1", 260),
                  ("causal", 256), ("pairs", 128), ("chunk", 128), ("levels", 64 * LEVELS), ("fold", 9),
                  ("heads", 32), ("newmask", 4), ("seqmask", 16), ("iota", CAP + HALF), ("count", 64), ("reset", 256),
                  ("restart", 288)]:
    CONST[_name] = (_at, _n)
    _at += _n
NCONST = _at
CONST["ones"] = (CONST["suffix1"][0], P)


def constants():
    c = np.zeros((P, NCONST), np.float32)
    p = np.arange(P)[:, None]

    def put(name, a):
        at, n = CONST[name]
        c[:a.shape[0], at:at + n] = a.reshape(a.shape[0], n)

    j = np.arange(P)[None, :]
    put("ident", (p == j) * 1.0)
    put("before", (p < j) * 1.0)
    later, z = (p > j) * 1.0, np.zeros((P, 4))
    put("suffix0", np.concatenate([later, 0 * later, z], 1))
    put("suffix1", np.concatenate([np.ones((P, P)), later, z], 1))
    put("causal", np.concatenate([np.zeros((P, P)), np.where(j <= p, 0.0, NEG)], 1))
    put("pairs", (p // DH == j // DH) * 1.0)
    s, t = p % L, np.arange(2 * L)[None, :]
    put("chunk", np.where(t < L, s < t, s <= t - L) * 1.0)
    s, t = np.arange(L)[:, None], np.arange(L)[None, :]
    put("levels", np.concatenate([((s // (2 * m) == t // (2 * m)) & (s // m % 2 == 0) & (t // m % 2 == 1)) * 1.0
                                  for m in (1 << i for i in range(LEVELS))], 1))
    put("fold", (p % 32 == np.arange(9)[None, :]) * 1.0)
    put("heads", (np.arange(H)[:, None] == np.arange(32)[None, :] // NT) * 1.0)
    put("newmask", np.where(np.arange(NT)[None, :] <= p % NT, 0.0, NEG))
    put("seqmask", (np.arange(16)[None, :] // 8 * 4 + p // 32 == np.arange(16)[None, :] % 8) * 1.0)
    r = np.arange(CAP + HALF)[None, :]
    put("iota", np.broadcast_to(np.where(r < CAP, r, r - HALF), (P, CAP + HALF)) * 1.0)
    cnt = np.stack([1.0 / np.minimum(np.arange(16) + 1, w) for w in WINS])
    put("count", np.broadcast_to(cnt[None], (P, 4, 16)).copy())
    put("reset", np.broadcast_to((np.arange(NP) % L != 0)[None] * 1.0, (P, NP)).copy())
    t = np.arange(N)
    put("restart", np.broadcast_to(((t != 0) & ((t < NP) | (t % NT != 0)))[None] * 1.0, (P, N)).copy())
    return c


def weight_tiles():
    tiles = [("ada0", i) for i in range(4)]
    for i in range(8):
        tiles += [("win", i), ("ada0", 4 + i)]
    tiles += [("wout", i) for i in range(2)]
    tiles += [("gate", 0), ("up", 0)]
    for i in range(6):
        tiles += [("gate", i + 1), ("up", i + 1)] if i < 5 else []
        tiles += [("ada1", 2 * i), ("ada1", 2 * i + 1), ("down", i)]
    return tiles


TILES = weight_tiles()
SLOTS, SLOT = 6, 4096
MIX_TILE = TILES.index(("wout", 0))
FGRP = [(512 * i, min(512, FF - 512 * i)) for i in range(6)]
WIN = [
    (0, 512, [("f", i, P * i, P) for i in range(4)]),
    (512, 512, [("f", 4 + i, P * i, P) for i in range(4)]),
    (1024, 512, [("f", 8 + i, P * i, P) for i in range(4)]),
    (1536, 8, [("l", 0, 0, 8)]),
    (1544, 512, [("r", i, P * i, P) for i in range(4)]),
    (2056, 448, [("r", PWL, 0, 64)] + [("r", PK + i, 64 + P * i, P) for i in range(3)]),
    (2504, 512, [("r", PK + 3, 0, P)] + [("r", PV + i, P + P * i, P) for i in range(3)]),
    (3016, 320, [("r", PV + 3, 0, P), ("r", PAL, P, 64), ("r", PGL, 192, P)]),
]
WCHUNKS = [c for _, _, cs in WIN for c in cs]


class Banks:

    def __init__(self, tiles):
        self.tiles, self.n, self.owner, self.at = tiles, 0, [None] * len(tiles), {}

    def open(self, pe, name, freed):
        b = self.n % len(self.tiles)
        self.n += 1
        if self.owner[b] is not None:
            pe.wait_ge(*self.owner[b])
        self.owner[b] = freed
        self.at[name] = b
        return self.tiles[b]

    def __getitem__(self, name):
        return self.tiles[self.at[name]]


class Named:

    def __init__(self, nc, ctx):
        self.nc, self.ctx, self.made = nc, ctx, {}

    def __call__(self, name):
        if name not in self.made:
            self.made[name] = self.ctx.enter_context(self.nc.semaphore(name))
        return self.made[name]


ONCE = {
    "vector": ("vec_copied vec2_copied lf_abs lf_one logf_ready negF_ready k_ready q_ready last_ready rp_mixed "
              "psm_shifted psm_ready kk_scaled rk_ready cum_ready delta_ops packed oddw_copied "
              "final_state gn_centred mix_ready exts_zero z_ready z_used top_ready picked planned res4"),
    "scalar": ("siluc c_copied qk_squared lf_exp lf_ln qk_rooted psm_exped so_copied wl_tanh gl_sigmoid "
              "kk_squared kk_rooted fst_copied syt_copied gn_squared gn_rooted top_exped"),
    "tensor": ("c_turned vec_turned vec2_turned lf_turned last_turned so_mm oddw_mm fst_mm syt_mm route_mm rank_mm"),
    "gpsimd": ("vrow_zero silucT_zero last_zero"),
}


class Once:

    def __init__(self, s):
        self.s, self.given = s, {e: 0 for e in ONCE}
        self.place = {name: (e, i + 1) for e, names in ONCE.items() for i, name in enumerate(names.split())}

    def __call__(self, name):
        engine, value = self.place[name]
        return self.s(f"{engine}_once"), value

    def give(self, name):
        engine, value = self.place[name]
        self.given[engine] += 1
        assert self.given[engine] == value, name
        return self.s(f"{engine}_once")


class Counted:

    def __init__(self, eng):
        self.eng, self.n = eng, {}

    def give(self, ins, sem):
        ins.then_inc(sem, 1)
        self.n[sem.name] = self.n.get(sem.name, 0) + 1

    def step(self, ins, sem):
        self.give(ins, sem)
        self.eng.wait_ge(sem, self.n[sem.name])


def spread(ap, axis, n):
    ap = ap.unsqueeze(axis)
    shape = list(ap.shape)
    shape[axis] = n
    return ap.to_broadcast(shape)


def flat(t):
    return t[:, :, :].rearrange("p a b -> p (a b)")


XJOBS = [(0, 0, 4), (0, 4, 4), (1, 0, 4), (1, 4, 4), (2, 0, 8)]


def kth(n, lv):
    return 2 * LEVELS * (n // 2) + 2 * lv + n % 2


def t_count(n, lv):
    per_pair = 2 * (2 * (LEVELS - 1) + 1)
    base = per_pair * (n // 2)
    return base + (4 * lv + 2 * (n % 2) + 2 if lv < LEVELS - 1 else 4 * lv + n % 2 + 1)


HALF_ONLY, FULL_ONLY, BOTH, NONE = range(4)
CACHE_STORES = 6 + 2 * NPC

VB_MU, VB_W0, VB_A0, VB_KK, VB_KA, VB_RK, VB_LNW, VB_LNB, VB_PS, VB_QG, VB_KG = 0, 15, 19, 23, 27, 31, 35, 39, 43, 51, 52
VA_ADA, VA_NORM = 0, (96, 112, 104, 120)



def t_mms(n, lv):
    per_pair = 2 * (2 * (LEVELS - 2) + 1)
    base = per_pair * (n // 2)
    return base + (4 * (lv - 1) + 2 * (n % 2) + 2 if lv < LEVELS - 1 else 4 * (lv - 1) + n % 2 + 1)


def build_program(nc, a, y_p, y_s, k_p, k_s, v_p, v_s, lf_p, lf_s, st_p, st_s, sh_p, sh_s, pool_p, pool_s):
    ctx = ExitStack()
    with ctx:
        def sb(name, shape, dt=F32):
            return ctx.enter_context(nc.sbuf_tensor(name, shape, dt))

        s = Named(nc, ctx)
        once = Once(s)

        def sums(name, which, n):
            return s(f"sums_{which}"), 3 * ("kks", "bon", "gnm", "gnv").index(name) + n

        def lora(name, which, n):
            return s(f"lora_{which}"), HC * ("dec", "icl", "gat").index(name) + n

        banks = Banks([ctx.enter_context(nc.psum_tensor(f"bank{i}", [P, 512], F32)) for i in range(8)])

        const = sb("const", [P, NCONST])

        def K(name, rows=P):
            at, n = CONST[name]
            return const[0:rows, at:at + n]

        ident = K("ident")
        xT = sb("xT", [P, DC, N])
        hT = sb("hT", [P, DC, N])
        tmpT = sb("tmpT", [P, DC, N])
        yT = sb("yT", [P, DC, N])
        modT = [sb(f"modT{i}", [P, 48, 9]) for i in range(2)]
        gainT = [sb(f"gainT{i}", [P, DC, 9]) for i in range(4)]
        silucT = sb("silucT", [P, DC, 32])
        vT = sb("vT", [P, 3, P])
        rstd = sb("rstd", [P, N])
        w2 = sb("w2", [LORA, HW])
        a2 = sb("a2", [LORA, HW])
        g2 = sb("g2", [GLORA, HW])
        fbias = sb("fbias", [H, 1])
        routerw = sb("routerw", [P, DC, NE])
        routerb = sb("routerb", [P, NE])
        pages = sb("pages", [1, NB * NPG], I32)
        ring = sb("ring", [P, SLOTS * SLOT])
        other = sb("other", [P, 12672])

        def slot(g):
            return ring[:, (g % SLOTS) * SLOT:(g % SLOTS + 1) * SLOT]

        class Region:
            def __init__(self, tensor, at=0):
                self.tensor, self.at = tensor, at

            def cut(self, *shape, rows=P):
                n = int(np.prod(shape))
                ap = self.tensor[0:rows, self.at:self.at + n]
                self.at += n
                names = "abcd"[:len(shape)]
                if len(shape) == 1:
                    return ap
                return ap.rearrange(f"p ({' '.join(names)}) -> p {' '.join(names)}",
                                    **dict(zip(names[1:], shape[1:])))

        vrow = Region(other, 12672 - 3 * P).cut(3, P)
        R = Region(other)
        rp = R.cut(NPC, N)
        diff = R.cut(NPC, N)
        fqkv = R.cut(3 * HC, N)
        pastlf4 = R.cut(NB, NPG, H * NT)
        D2 = Region(other, NPC * N)
        lw = D2.cut(HC, N)
        icl = D2.cut(HC, N)
        gate = D2.cut(HC, N)
        R = Region(ring)
        X = Region(other)
        xrow = X.cut(3, D)
        crow = X.cut(D)
        scrow = X.cut(D)
        adap = [Region(flat(yT), HC * N).cut(2, 512)]
        R = Region(ring)
        ksamp = R.cut(2, NPG, HW)
        vsamp = R.cut(NB, NPG, HW)
        ktb = R.cut(2, HC, PAST + NT)
        qbd = R.cut(NB, HC, 32)
        pr = R.cut(2, 2, 256)
        prT = R.cut(2, 2, 2, P)
        psm = R.cut(2, PAST + NT)
        pnew = R.cut(2, NB, NT)
        psT = R.cut(2, 3, P)
        pastlf = R.cut(NB, NPG, H)
        logf = R.cut(N, rows=H)
        negF = R.cut(N, rows=H)
        lftmp = R.cut(2, N, rows=H)
        kvrow = R.cut(2, 3, HW)
        lfrow = R.cut(3, H)
        lastS = R.cut(NPC, NB)
        lastP = R.cut(NPC)
        lastrow = R.cut(2, P)
        ATT_END = R.at
        sst = R.cut(32, DH)
        sval = R.cut(NT, 32)
        ssa = R.cut(32)
        sy = R.cut(NT, 32)
        syrow = R.cut(HW, rows=NS)
        assert R.at <= SLOTS * SLOT, R.at
        R = Region(ring)
        kkT = R.cut(HC, N)
        bT = R.cut(HC, N)
        ar = R.cut(HC, NCH, 2, L)
        bk = R.cut(HC, NCH, 2, L)
        zv = R.cut(HC, NCH, 2, L)
        gt = R.cut(2, H, 2 * L)
        bkt = R.cut(2, H, DH)
        sav = R.cut(2, H, DH)
        su = R.cut(2, H, DH)
        lu = R.cut(NCH, H, L)
        assert R.at <= ATT_END, (R.at, ATT_END)
        Q = Region(other, 2 * NPC * N)
        rt = Q.cut(NCH, H, L, rows=L)
        tb = Q.cut(2, H, L, rows=L)
        assert Q.at <= 12672, Q.at
        Q = Region(flat(tmpT))
        wdec = Q.cut(HC, NP)
        winv = Q.cut(HC, NP)
        Q = Region(flat(hT))
        wprev = Q.cut(HC, NP)
        tt = Q.cut(2, H, L, rows=L)
        Q = Region(ring, R.at)
        xb = Q.cut(2, H, L, rows=L)
        nm = Q.cut(2, H, L, rows=L)
        ub = xb
        wlx = Q.cut(H, NCH, rows=L)
        srow = Region(ring, Q.at).cut(6, HW, rows=NS)
        svec = Q.cut(NT, 6, DH)
        sprod = Q.cut(32, DH)
        assert Q.at <= ATT_END, (Q.at, ATT_END)

        small = sb("small", [P, 64])
        plan = sb("plan", [1, ITEMS + MORE + 1], I32)
        mix_stores = [0]

        R = Region(other)
        ffact = R.cut(2, 4, N)
        ffsilu = R.cut(2, N)
        prow = R.cut(D)
        poolw = R.cut(4, 2, 256)
        ext = R.cut(DC, 16 + NP)
        exts = R.cut(DC, NB, 20)
        hlast = R.cut(D)
        adap.append(R.cut(2, 512))
        assert R.at <= 12672, R.at
        R = Region(other)
        htok = R.cut(3, D)
        outrow = Region(other).cut(3, D)
        xe = R.cut(DC, CAP)
        sg = R.cut(2, 512)
        ea = R.cut(2, 512)
        eaT = R.cut(2, 4, CAP)
        ye = R.cut(D)
        yeh = R.cut(512)
        hot = R.cut(3, CAP)
        hotw = R.cut(3, CAP + HALF)
        gT = R.cut(2, N)
        pick = R.cut(3, NE)
        logit = R.cut(3, NE)
        comb = R.cut(3, ITEMS + 1)
        slot_at = R.cut(3, ITEMS + 1)
        later = R.cut(3, NE)
        top = R.cut(3, 8)
        topi = R.cut(3, 8)
        gate2 = R.cut(3, 4)
        wanted = R.cut(NE)
        ordinal = R.cut(NE)
        which = R.cut(MORE, NE)
        chosen = R.cut(3, MORE, NE)
        load = R.cut(ITEMS)
        small_item = R.cut(ITEMS)
        planf = R.cut(ITEMS + MORE + 1)
        assert R.at <= 12672, R.at

        def vector_rows():
            out = [(vrow[48 * l:48 * l + 48, 0, :], a["ada_b"][l].rearrange("(r p) -> r p", p=P)) for l in range(2)]
            for i, name in enumerate(("norm1_g", "norm2_g")):
                out.append((vrow[96 + 16 * i:112 + 16 * i, 0, :], a[name].rearrange("l (r p) -> (l r) p", p=P)))
            first, out = out, []
            for i, (at, w) in enumerate(PIECES):
                out.append((vrow[VB_MU + i:VB_MU + i + 1, 1, 0:w], a["rwkv_mu"][:, at:at + w]))
                out.append((vrow[NB * i:NB * i + NB, 2, 0:w], a["state_rwkv_shift"][0, :, at:at + w]))
            for name, row in (("rwkv_w0", VB_W0), ("rwkv_a0", VB_A0), ("rwkv_k_k", VB_KK), ("rwkv_k_a", VB_KA),
                              ("rwkv_ln_w", VB_LNW), ("rwkv_ln_b", VB_LNB)):
                out.append((vrow[row:row + HC, 1, :], a[name][0].rearrange("(r p) -> r p", p=P)))
            out.append((vrow[VB_RK:VB_RK + HC, 1, :], a["rwkv_r_k"][0].rearrange("(c a) k -> c (a k)", a=2)))
            out.append((vrow[VB_PS:VB_PS + DC, 1, :], a["pool_scale"][0].rearrange("(r p) -> r p", p=P)))
            for name, row in (("fox_q_gain", VB_QG), ("fox_k_gain", VB_KG)):
                for par in range(2):
                    out.append((vrow[row:row + 1, 1, DH * par:DH * (par + 1)], a[name]))
            return first, out

        cumv = winv

        def sample_operands():
            return [lw, kkT, bT, rp[:, PK:PK + HC, :], rp[:, PR:PR + HC, :], rp[:, PV:PV + HC, :]]

        scratch = nc.dram_tensor("sample_operands", [NB, NT, 6, H, DH], F32, kind="Internal").ap()
        scratch_y = nc.dram_tensor("sample_outputs", [NB, NT, 2 * H, 32], F32, kind="Internal").ap()

        def used(g):
            kind, i = TILES[g]
            if kind[:3] == "ada":
                return s("ada_mm"), 12 * int(kind[3]) + i + 1
            if kind == "win":
                return s("win_mm"), sum(len(c) for _, _, c in WIN[:i + 1])
            if kind == "wout":
                return s("wo_mm"), 4 * (i + 1)
            if kind == "down":
                return s("down_mm"), DC * (i + 1)
            return s(f"{kind}_mm"), 4 * i + FGRP[i][1] // P

        def tile_source(g):
            kind, i = TILES[g]

            def cols(w, at, n):
                return (slot(g)[:, 0:DC * n].rearrange("p (c f) -> p c f", c=DC),
                        w.rearrange("(c p) f -> p c f", p=P)[:, :, at:at + n])

            if kind[:3] == "ada":
                return cols(a["ada_w"][int(kind[3])], 512 * i, 512)
            if kind == "win":
                return cols(a["w_in"][0], WIN[i][0], WIN[i][1])
            if kind == "wout":
                return cols(a["w_out"][0], 512 * i, 512)
            at, n = FGRP[i]
            if kind == "down":
                return (slot(g)[:, 0:n // P * D].rearrange("p (c f) -> p c f", f=D),
                        a["ffn_w_down"][0, at:at + n, :].rearrange("(c p) f -> p c f", p=P))
            return cols(a[f"ffn_w_{kind}"][0], at, n)

        NT7 = FE // 512
        GRP = 3 * SLOT

        def moe_tile(it, t, kind):
            return ((it + t) % 2) * GRP + kind * SLOT

        PRIMED = {"pe": ("moe_down", "moe_turn", "comb_mm"), "act": ("moe_silu", "ye_act"),
                  "dve": ("moe_act", "ye_dve", "comb_added")}

        def after(name, n):
            assert any(name in names for names in PRIMED.values())
            return s(name), n + 1

        GATE, UP, GU, TURNH, TURN, YEH, YE = range(7)

        def moe_gather(pe, mm, k, prime=()):
            pe.wait_ge(s("hot_ready"), k + 1)
            for q in range(4):
                for c in range(2):
                    for blk, (_, w) in enumerate(BLK):
                        o = P * (2 * q + c)
                        last = mm(banks.tiles[q][:, CAP * c:CAP * (c + 1)], htok[0:w, blk, o:o + P], hot[0:w, blk, :],
                                  blk == 0, blk == 2)
                    if c == 0 and q < len(prime):
                        last.then_inc(s(prime[q]), 1)
                last.then_inc(s("gather_mm"), 1)

        def moe_tensor_item(pe, mm, it, odd, full, half):
            B = banks.tiles

            def hidden(t):
                n = NT7 * it + t
                pe.wait_ge(*after("moe_silu", n))
                pe.wait_ge(*after("moe_act", n))
                pe.wait_ge(s(f"moe_gu{t}"), 32 * it + 32)
                gate, up = moe_tile(odd, t, 0), moe_tile(odd, t, 1)
                if full:
                    for c in range(DC):
                        last = mm(B[GATE][:, :], xe[:, c, 0:P], ring[:, gate + 512 * c:gate + 512 * (c + 1)], c == 0, c == DC - 1)
                    last.then_inc(s("moe_gate"), 1)
                if half:
                    for c in range(DC):
                        last = mm(B[GU][0:HALF, :], xe[:, c, P:CAP], ring[:, gate + 512 * c:gate + 512 * (c + 1)], c == 0, c == DC - 1)
                        if c == DC - 1 and not full:
                            last.then_inc(s("moe_gate"), 1)
                        last = mm(B[GU][HALF:P, :], xe[:, c, P:CAP], ring[:, up + 512 * c:up + 512 * (c + 1)], c == 0, c == DC - 1)
                if full:
                    for c in range(DC):
                        last = mm(B[UP][:, :], xe[:, c, 0:P], ring[:, up + 512 * c:up + 512 * (c + 1)], c == 0, c == DC - 1)
                last.then_inc(s("moe_up"), 1)

            def turn(t):
                n = NT7 * it + t
                pe.wait_ge(*after("moe_act", n + 1))
                if t == 0:
                    pe.wait_ge(s("gT_ready"), it + 1)
                else:
                    pe.wait_ge(s("eaT_ready"), n)
                for j in range(4):
                    if full:
                        last = pe.transpose(B[TURN][:, P * j:P * (j + 1)], ea[:, 0, P * j:P * (j + 1)], ident)
                    if half:
                        last = mm(B[TURNH][:, HALF * j:HALF * (j + 1)], ea[HALF:P, 1, P * j:P * (j + 1)],
                                  ident[HALF:P, HALF:P], True, True)
                last.then_inc(s("moe_turn"), 1)

            def down(t):
                n = NT7 * it + t
                pe.wait_ge(s("eaT_ready"), n + 1)
                if t == 0:
                    pe.wait_ge(*after("ye_act", it))
                    pe.wait_ge(*after("ye_dve", it))
                    pe.wait_ge(*after("comb_added", DC * it))
                pe.wait_ge(s(f"moe_d{t}"), 16 * it + 16)
                at = moe_tile(odd, t, 2)
                for j in range(4):
                    start, stop = t == 0 and j == 0, t == NT7 - 1 and j == 3
                    for p in range(2):
                        w = ring[:, at + D * j + 512 * p:at + D * j + 512 * (p + 1)]
                        if full:
                            last = mm(B[YE + p][:, :], eaT[:, t % 2, j, 0:P], w, start, stop)
                    for p in range(2):
                        w = ring[:, at + D * j + 512 * p:at + D * j + 512 * (p + 1)]
                        if half:
                            last = mm(B[YEH][HALF * p:HALF * (p + 1), :], eaT[:, t % 2, j, P:CAP], w, start, stop)
                last.then_inc(s("moe_down"), 1)

            pe.wait_ge(s("xe_ready"), 4 * it + 4)
            hidden(0)
            pe.wait_ge(*after("comb_added", DC * it))
            for blk, (t0, w) in enumerate(BLK):
                if full:
                    last = pe.transpose(B[TURN][:, t0:t0 + w], hotw[0:w, blk, 0:P], ident[0:w, 0:w])
                if half:
                    last = pe.transpose(B[TURNH][:, t0:t0 + w], hotw[0:w, blk, P:2 * P], ident[0:w, 0:w])
            last.then_inc(s("g_mm"), 1)
            for t in range(1, NT7):
                hidden(t)
                turn(t - 1)
                down(t - 1)
            turn(NT7 - 1)
            pe.wait_ge(s("eaT_ready"), NT7 * it + NT7)
            moe_gather(pe, mm, it + 1)
            down(NT7 - 1)
            pe.wait_ge(*after("ye_act", it + 1))
            pe.wait_ge(*after("ye_dve", it + 1))
            for j in range(DC):
                if j >= 2:
                    pe.wait_ge(*after("comb_added", DC * it + j - 1))
                o = B[TURN + j % 2][:, 0:N]
                if full:
                    last = mm(o, ye[:, P * j:P * (j + 1)], gT[:, 0, :], True, not half)
                if half:
                    p = HALF * (j // 4)
                    last = mm(o, yeh[p:p + HALF, P * (j % 4):P * (j % 4 + 1)], gT[p:p + HALF, 1, :], not full, True)
                last.then_inc(s("comb_mm"), 1)

        def moe_scalar_item(act, it, full, half):
            B = banks.tiles

            def turned(t):
                n = NT7 * it + t
                act.wait_ge(*after("moe_turn", n + 1))
                act.wait_ge(*after("moe_down", n if t == 0 else n - 1))
                if full:
                    last = act.activation(eaT[:, t % 2, :, 0:P], B[TURN][:, :].rearrange("p (j q) -> p j q", j=4), ACT.Copy)
                if half:
                    last = act.activation(eaT[:, t % 2, :, P:CAP],
                                          B[TURNH][:, 0:4 * HALF].rearrange("p (j q) -> p j q", j=4), ACT.Copy)
                last.then_inc(s("eaT_ready"), 1)

            for t in range(NT7):
                n = NT7 * it + t
                act.wait_ge(s("moe_gate"), n + 1)
                act.wait_ge(*after("moe_act", n))
                if full:
                    last = act.activation(sg[:, 0, :], B[GATE][:, :], ACT.Silu)
                if half:
                    if full:
                        act.wait_ge(s("moe_up"), n + 1)
                    last = act.activation(sg[HALF:P, 1, :], B[GU][0:HALF, :], ACT.Silu)
                last.then_inc(s("moe_silu"), 1)
                if t:
                    turned(t - 1)
            turned(NT7 - 1)
            moe_gathered(act, it + 1)
            act.wait_ge(*after("moe_down", NT7 * it + NT7))
            act.wait_ge(*after("comb_mm", DC * it))
            if full:
                last = act.activation(ye[:, 0:512], B[YE][:, :], ACT.Copy)
            if half:
                last = act.activation(yeh, B[YEH][:, :], ACT.Copy)
            last.then_inc(s("ye_act"), 1)

        def moe_gathered(act, k):
            for q in range(4):
                act.wait_ge(s("gather_mm"), 4 * k + q + 1)
                act.activation(xe[:, 2 * q:2 * q + 2, :].rearrange("p c s -> p (c s)"), banks.tiles[q][:, 0:2 * CAP], ACT.Copy)\
                    .then_inc(s("xe_ready"), 1)

        def moe_hot(dve, it):
            for blk, (_, w) in enumerate(BLK):
                at = slot_at[0:w, blk, bass.ds(it, 1)]
                dve.tensor_scalar(hot[0:w, blk, :], K("iota")[0:w, 0:CAP], at, None, ALU.is_equal)
                last = dve.tensor_scalar(hotw[0:w, blk, :], K("iota")[0:w, :], at, comb[0:w, blk, bass.ds(it, 1)],
                                         ALU.is_equal, ALU.mult)
            last.then_inc(s("hot_ready"), 1)

        def moe_vector_item(dve, it, full, half):
            B = banks.tiles
            for t in range(NT7):
                n = NT7 * it + t
                dve.wait_ge(*after("moe_silu", n + 1))
                dve.wait_ge(s("moe_up"), n + 1)
                dve.wait_ge(*after("moe_turn", n))
                if full:
                    last = dve.tensor_tensor(ea[:, 0, :], sg[:, 0, :], B[UP][:, :], ALU.mult)
                if half:
                    last = dve.tensor_tensor(ea[HALF:P, 1, :], sg[HALF:P, 1, :], B[GU][HALF:P, :], ALU.mult)
                last.then_inc(s("moe_act"), 1)
                if t == 0:
                    dve.wait_ge(s("g_mm"), it + 1)
                    dve.wait_ge(*after("comb_mm", DC * it))
                    if full:
                        last = dve.tensor_copy(gT[:, 0, :], B[TURN][:, 0:N])
                    if half:
                        last = dve.tensor_copy(gT[:, 1, :], B[TURNH][:, 0:N])
                    last.then_inc(s("gT_ready"), 1)
                if t == 1:
                    moe_hot(dve, it + 1)
            dve.wait_ge(*after("moe_down", NT7 * it + NT7))
            if full:
                dve.tensor_copy(ye[:, 512:1024], B[YE + 1][:, :]).then_inc(s("ye_dve"), 1)
            else:
                dve.memset(small[:, 61:62], 0.0).then_inc(s("ye_dve"), 1)
            dve.wait_ge(*after("comb_added", DC * it))
            for j in range(DC):
                dve.wait_ge(*after("comb_mm", DC * it + j + 1))
                dve.tensor_tensor(yT[:, j, :], yT[:, j, :], B[TURN + j % 2][:, 0:N], ALU.add).then_inc(s("comb_added"), 1)

        def moe_sync_item(sp, it, e, first=False):
            wg, wu, wd = (a[f"moe_w_{k}"][0, bass.ds(e, 1)] for k in ("gate", "up", "down"))
            for t in range(NT7):
                n = NT7 * it + t
                for kind, w in enumerate((wg, wu, wd)):
                    if first and t < 2:
                        sp.wait_ge(*used(max(g for g in range(len(TILES)) if g % SLOTS == 3 * t + kind)))
                    elif kind == 0:
                        sp.wait_ge(s("moe_up"), n - 1)
                    elif kind == 2:
                        sp.wait_ge(*after("moe_down", n - 1))
                    dst = ring[:, bass.ds(moe_tile(it, t, kind), SLOT)]
                    if kind < 2:
                        sp.dma_start(dst.rearrange("p (c f) -> p c f", c=DC),
                                     w.rearrange("o (c p) f -> p (o c) f", p=P)[:, :, 512 * t:512 * (t + 1)])\
                            .then_inc(s(f"moe_gu{t}"), 16)
                    else:
                        sp.dma_start(dst.rearrange("p (c f) -> p c f", c=4),
                                     w.rearrange("o f d -> (o f) d")[512 * t:512 * (t + 1), :].rearrange("(c p) d -> p c d", p=P))\
                            .then_inc(s(f"moe_d{t}"), 16)

        def items(engine, step):
            engine.wait_ge(*once("planned"))
            with engine.Fori(0, ITEMS // 2) as pair:
                for odd in range(2):
                    it = 2 * pair + odd
                    kind = engine.value_load(plan[0:1, bass.ds(it, 1)], min_val=0, max_val=NONE)
                    with engine.If(kind == HALF_ONLY):
                        step(it, odd, False, True)
                    with engine.If(kind == FULL_ONLY):
                        step(it, odd, True, False)
                    with engine.If(kind == BOTH):
                        step(it, odd, True, True)

        def moe_tensor(pe, mm):
            pe.wait_ge(s("ranked"), 3)
            pe.wait_ge(s("htok_ready"), 6)
            moe_gather(pe, mm, 0, PRIMED["pe"])
            items(pe, lambda *item: moe_tensor_item(pe, mm, *item))

        def moe_scalar(act):
            for i, name in enumerate(PRIMED["act"]):
                act.activation(small[:, 44 + i:45 + i], ident[:, 0:1], ACT.Copy).then_inc(s(name), 1)
            moe_gathered(act, 0)
            items(act, lambda it, odd, full, half: moe_scalar_item(act, it, full, half))

        def moe_plan(dve, do):
            counts = small[:, 48:48 + NE]
            TS, TT = dve.tensor_scalar, dve.tensor_tensor
            do(TS(wanted, counts, float(CAP), None, ALU.is_gt))
            do(dve.tensor_tensor_scan(ordinal, K("ones")[:, 0:NE], wanted, 0.0, ALU.mult, ALU.add))
            for r in range(MORE):
                do(dve.scalar_tensor_tensor(which[:, r, :], ordinal, float(r + 1), wanted, ALU.is_equal, ALU.mult))
            do(TT(chosen, spread(later, 2, MORE), spread(which, 1, 3), ALU.mult))
            do(dve.tensor_reduce(slot_at[:, :, NE:ITEMS], chosen, AX.X, ALU.add))
            do(TT(chosen, spread(comb[:, :, 0:NE], 2, MORE), spread(which, 1, 3), ALU.mult))
            do(dve.tensor_reduce(comb[:, :, NE:ITEMS], chosen, AX.X, ALU.add))
            do(TT(chosen[:, 0], which, spread(K("iota")[:, 0:NE], 1, MORE), ALU.mult))
            do(dve.tensor_reduce(planf[:, ITEMS:ITEMS + MORE], chosen[:, 0], AX.X, ALU.add))
            do(TS(load[:, 0:NE], counts, float(CAP), None, ALU.min))
            do(TS(wanted, counts, -float(CAP), None, ALU.add))
            do(TT(chosen[:, 0], which, spread(wanted, 1, MORE), ALU.mult))
            do(dve.tensor_reduce(load[:, NE:ITEMS], chosen[:, 0], AX.X, ALU.add))
            do(TS(small_item, load, float(HALF), None, ALU.is_le))
            do(dve.scalar_tensor_tensor(slot_at[:, :, 0:ITEMS], spread(small_item, 1, 3), float(P), slot_at[:, :, 0:ITEMS],
                                        ALU.mult, ALU.add))
            do(TS(planf[:, 0:ITEMS], load, float(P), None, ALU.is_gt))
            do(TT(planf[:, 0:ITEMS], planf[:, 0:ITEMS], small_item, ALU.subtract))
            do(TS(planf[:, 0:ITEMS], planf[:, 0:ITEMS], 1.0, None, ALU.add))
            do(TS(small_item[:, NE:ITEMS], load[:, NE:ITEMS], 0.0, float(NONE), ALU.is_equal, ALU.mult))
            do(TT(planf[:, NE:ITEMS], planf[:, NE:ITEMS], small_item[:, NE:ITEMS], ALU.add))
            do(TS(planf[:, ITEMS + MORE:], ordinal[:, NE - 1:NE], float(NE), None, ALU.add))
            do(dve.tensor_copy(plan[:, :], planf[0:1, :]), once.give("planned"))

        def moe_vector(dve, do):
            moe_plan(dve, do)
            for i, name in enumerate(PRIMED["dve"]):
                dve.memset(small[:, 32 + i:33 + i], 0.0).then_inc(s(name), 1)
            moe_hot(dve, 0)
            items(dve, lambda it, odd, full, half: moe_vector_item(dve, it, full, half))
            return dve.value_load(plan[0:1, ITEMS + MORE:ITEMS + MORE + 1], min_val=NE, max_val=ITEMS)

        def moe_sync(sp):
            moe_sync_item(sp, 0, 0, first=True)
            with sp.Fori(1, NE) as it:
                moe_sync_item(sp, it, it)
            sp.wait_ge(*once("planned"))
            with sp.Fori(NE, ITEMS) as it:
                kind = sp.value_load(plan[0:1, bass.ds(it, 1)], min_val=0, max_val=NONE)
                with sp.If(kind < NONE):
                    e = sp.value_load(plan[0:1, bass.ds(it + (ITEMS - NE), 1)], min_val=0, max_val=NE - 1)
                    moe_sync_item(sp, it, e)

        block = ctx.enter_context(nc.Block())

        @block.tensor
        def _(pe):
            def mm(out, lhsT, rhs, start, stop):
                return pe.matmul(out, lhsT, rhs, start=start, stop=stop, skip_group_check=True)

            pe.wait_ge(s("const_loaded"), 16)
            pe.wait_ge(*once("siluc"))
            b = banks.open(pe, "c", once("c_copied"))
            for c in range(DC):
                last = pe.transpose(b[:, 9 * c:9 * c + 9], scrow[0:9, P * c:P * (c + 1)], ident[0:9, 0:9])
            last.then_inc(once.give("c_turned"), 1)
            pe.wait_ge(s("x_loaded"), 48)
            for n, (blk, c0, nc_) in enumerate(XJOBS):
                w = BLK[blk][1]
                b = banks.open(pe, f"x{n}", (s("x_copied"), n + 1))
                for c in range(nc_):
                    last = pe.transpose(b[:, w * c:w * (c + 1)], xrow[0:w, blk, P * (c0 + c):P * (c0 + c + 1)],
                                        ident[0:w, 0:w])
                last.then_inc(s("x_turned"), 1)

            def mean_square(i):
                pe.wait_ge(s("squared"), i + 1)
                b = banks.open(pe, f"ms{i}", (s("ms_read"), i + 1))
                for c in range(DC):
                    last = mm(b[:, 0:N], K("ones"), tmpT[:, c, :], c == 0, c == DC - 1)
                last.then_inc(s("ms_ready"), 1)

            mean_square(0)

            def tile(g):
                pe.wait_ge(s(f"slot{g % SLOTS}"), 16 * (g // SLOTS + 1))
                return slot(g)

            def ada(layer, i):
                w = tile(TILES.index((f"ada{layer}", i))).rearrange("p (c f) -> p c f", c=DC)
                b = banks.open(pe, f"ada{layer}_{i}", (s("ada_copied"), 12 * layer + i + 1))
                for c in range(DC):
                    last = mm(b[32 * (c % 4):32 * (c % 4) + 32, :], silucT[:, c, :], w[:, c, :], c < 4, c >= 4)
                last.then_inc(s("ada_mm"), 1)

            def fold(layer, i):
                k = 12 * layer + i
                b = banks.open(pe, f"fold{layer}_{i}", (s("mod_ready"), k + 1))
                pe.wait_ge(s("ada_copied"), k + 1)
                for j in range(4):
                    last = mm(b[:, 9 * j:9 * j + 9], adap[layer][:, k % 2, P * j:P * (j + 1)], K("fold"), True, True)
                last.then_inc(s("folded"), 1)

            pe.wait_ge(*once("c_copied"))
            ada(0, 0)
            first, others = vector_rows()
            pe.wait_ge(s("vec_loaded"), 16 * len(first))
            b = banks.open(pe, "vec", once("vec_copied"))
            pe.transpose(b[:, 0:P], vrow[:, 0, :], ident).then_inc(once.give("vec_turned"), 1)
            for i in range(1, 4):
                ada(0, i)
                fold(0, i - 1)
            fold(0, 3)

            pe.wait_ge(s("h_ready"), 1)
            n = 0
            for i, (_, wd, chunks) in enumerate(WIN):
                w = tile(TILES.index(("win", i)))[:, 0:DC * wd].rearrange("p (c f) -> p c f", c=DC)
                for kind, idx, off, m in chunks:
                    b = banks.open(pe, f"win{n}", (s("win_act" if n % 2 else "win_dve"), n // 2 + 1))
                    for c in range(DC):
                        last = mm(b[0:m, 0:N], w[:, c, off:off + m], hT[:, c, :], c == 0, c == DC - 1)
                    last.then_inc(s("win_mm"), 1)
                    n += 1
                if i == 2:
                    pe.wait_ge(s("vec2_loaded"), 16 * len(others))
                    b = banks.open(pe, "vec2", once("vec2_copied"))
                    for k in range(2):
                        last = pe.transpose(b[:, P * k:P * (k + 1)], vrow[:, 1 + k, :], ident)
                    last.then_inc(once.give("vec2_turned"), 1)
                if i:
                    fold(0, 3 + i)
                ada(0, 4 + i)
            fold(0, 11)

            pe.wait_ge(*once("qk_squared"))
            for i in range(6):
                b = banks.open(pe, f"qkms{i}", (s("qkms_read"), i + 1))
                mm(b[:, 0:384], K("pairs"), flat(tmpT)[:, 384 * i:384 * (i + 1)], True, True).then_inc(s("qkms"), 1)
            pe.wait_ge(*once("k_ready"))
            for n in range(6):
                which, blk = n // 3, n % 3
                t0, w = BLK[blk]
                b = banks.open(pe, f"kv{n}", (s("kv_copied"), n + 1))
                for c in range(HC):
                    last = pe.transpose(b[0:w, P * c:P * (c + 1)], fqkv[:, HC * (1 + which) + c, t0:t0 + w], ident)
                last.then_inc(s("kv_turned"), 1)
            pe.wait_ge(*once("logf_ready"))
            b = banks.open(pe, "lf", (s("lf_copied"), 3))
            for blk, (t0, w) in enumerate(BLK):
                last = pe.transpose(b[0:w, H * blk:H * (blk + 1)], logf[:, t0:t0 + w], ident[0:H, 0:H])
            last.then_inc(once.give("lf_turned"), 1)
            pe.wait_ge(*once("last_ready"))
            b = banks.open(pe, "last", (s("last_copied"), 2))
            pe.transpose(b[0:NPC * 8, 0:P], lastS.rearrange("p a b -> p (a b)"), ident)
            pe.transpose(b[0:NPC, P:2 * P], lastP, ident).then_inc(once.give("last_turned"), 1)

            def scores(c, qb):
                nk = P * (qb + 1)
                for par in range(2):
                    p0 = DH * par
                    b = banks.open(pe, f"s{c}{qb}{par}", (s("scored"), 4 * c + 2 * qb + par + 1))
                    mm(b[:, 0:nk], fqkv[p0:p0 + DH, c, P * qb:P * (qb + 1)], fqkv[p0:p0 + DH, HC + c, 0:nk], True, False)
                    h = 2 * c + par
                    mm(b[:, 0:nk], ident[0:H, h:h + 1].to_broadcast([H, P]), negF[0:H, 0:nk], False, True)\
                        .then_inc(s("s_mm"), 1)

            def turn_probs(c, qb):
                k = 2 * c + qb
                pe.wait_ge(s("probs"), k + 1)
                b = banks.open(pe, f"pt{c}{qb}", (s("probsT"), k + 1))
                for par in range(2):
                    for j in range(qb + 1):
                        o = P * ((qb + 1) * par + j)
                        last = pe.transpose(b[:, o:o + P], pr[:, k % 2, par, P * j:P * (j + 1)], ident)
                last.then_inc(s("pt_mm"), 1)

            def attend(c, qb):
                k = 2 * c + qb
                pe.wait_ge(s("probsT"), k + 1)
                b = banks.open(pe, f"o{c}{qb}", (s("o_copied"), k + 1))
                for par in range(2):
                    h = 2 * c + par
                    for j in range(qb + 1):
                        last = mm(b[DH * par:DH * par + DH, 0:P], kvrow[:, 1, j, DH * h:DH * (h + 1)],
                                  prT[:, k % 2, par, j, :], j == 0, j == qb)
                last.then_inc(s("o_mm"), 1)

            pe.wait_ge(*once("q_ready"))
            pe.wait_ge(*once("negF_ready"))
            pe.wait_ge(s("kv_copied"), 6)
            tasks = [(c, qb) for c in range(HC) for qb in range(2)]
            scores(*tasks[0])
            for k, t in enumerate(tasks):
                if k + 1 < len(tasks):
                    scores(*tasks[k + 1])
                turn_probs(*t)
                attend(*t)

            pe.wait_ge(s("qbd_ready"), 2 * HC)
            for q in range(NB):
                pe.wait_ge(s(f"k_page{q % 2}"), 64 * (q // 2 + 1))
                for half in range(2):
                    b = banks.open(pe, f"kt{q}{half}", (s("kt_copied"), 3 * q + half + 1))
                    for cc in range(2):
                        for j in range(NPG):
                            o = 256 * cc + P * j
                            last = pe.transpose(b[:, o:o + P], ksamp[:, q % 2, j, P * (2 * half + cc):P * (2 * half + cc + 1)], ident)
                    last.then_inc(s("kt_mm"), 1)
                pe.wait_ge(s("kt_copied"), 3 * q + 3)
                b = banks.open(pe, f"ss{q}", (s("ss_copied"), q + 1))
                o = b[0:32, 0:PAST + NT]
                for c in range(HC):
                    mm(o, qbd[:, q, c, :], ktb[:, q % 2, c, :], c == 0, False)
                pe.wait_ge(s("lf_spread"), q + 1)
                for j in range(NPG):
                    mm(o, pastlf4[:, q, j, :], K(f"suffix{j}"), False, False)
                mm(b[0:32, PAST:PAST + NT], K("heads", H), negF[0:H, NP + NT * q:NP + NT * (q + 1)],
                   False, True).then_inc(s("ss_mm"), 1)
            pe.wait_ge(*once("psm_ready"))
            for g in range(2):
                b = banks.open(pe, f"pst{g}", (s("psT_ready"), 2 * g + 2))
                for j in range(NPG):
                    pe.transpose(b[:, P * j:P * (j + 1)], psm[:, g, P * j:P * (j + 1)], ident)
                last = pe.transpose(b[0:32, 2 * P:3 * P], pnew[:, g, :, :].rearrange("p a b -> p (a b)"), ident)
                last.then_inc(s("pst_mm"), 1)
            pe.wait_ge(s("psT_ready"), 4)
            pe.wait_ge(s("v_pages"), 32 * NB)
            b = banks.open(pe, "so", once("so_copied"))
            so = b[:, 0:HC * NS].rearrange("p (c t) -> p c t", c=HC)
            for h in range(H):
                p0, c = DH * (h % 2), h // 2
                for g in range(2):
                    new = psT[0:32, g, 2, :].rearrange("p (s h t) -> p s h t", s=4, h=H)[:, :, h, :]
                    mm(so[p0:p0 + DH, c, 16 * g:16 * g + 16], kvrow[0:NS, 1, 2, DH * h:DH * (h + 1)], new,
                       h < 2 and g == 0, False)
            for q in range(NB):
                for h in range(H):
                    p0, c = DH * (h % 2), h // 2
                    for j in range(NPG):
                        at = 32 * (q % 4) + NT * h
                        last = mm(so[p0:p0 + DH, c, NT * q:NT * (q + 1)], vsamp[:, q, j, DH * h:DH * (h + 1)],
                                  psT[:, q // 4, j, at:at + NT], False, q == NB - 1 and j == NPG - 1)
            last.then_inc(once.give("so_mm"), 1)

            def lowrank(name, weights, src, need):
                pe.wait_ge(*once(need))
                for c in range(HC):
                    b = banks.open(pe, f"{name}{c}", lora(name, "ready", c + 1))
                    mm(b[:, 0:N], weights[:, P * c:P * (c + 1)], src, True, True).then_inc(s("lora_mm"), 1)

            lowrank("dec", w2[:, :], rp[0:LORA, PWL, :], "wl_tanh")
            lowrank("icl", a2[:, :], rp[0:LORA, PAL, :], "rp_mixed")
            lowrank("gat", g2[:, :], rp[:, PGL, :], "gl_sigmoid")

            def head_sums(name, src, n=3):
                for i in range(n):
                    b = banks.open(pe, f"{name}{i}", sums(name, "read", i + 1))
                    mm(b[:, 0:384], K("pairs"), src[:, 384 * i:384 * (i + 1)], True, True).then_inc(s("sums_mm"), 1)

            pe.wait_ge(*once("kk_squared"))
            head_sums("kks", flat(tmpT)[:, 0:HC * N])
            pe.wait_ge(*once("rk_ready"))
            head_sums("bon", flat(tmpT)[:, HC * N:2 * HC * N])
            pe.wait_ge(*once("delta_ops"))
            for i, src in enumerate(sample_operands()):
                b = banks.open(pe, f"sr{i}", (s("srow_copied"), i + 1))
                for c in range(HC):
                    last = pe.transpose(b[0:NS, P * c:P * (c + 1)], src[:, c, NP:N], ident)
                last.then_inc(s("sr_mm"), 1)

            pe.wait_ge(*once("packed"))
            for c in range(HC):
                b = banks.open(pe, f"odd{c}", (s("odd_copied"), 2 * c + 2))
                mm(b[0:L, :], ident[:, DH:P], ar[:, c].rearrange("p n a t -> p (n a t)"), True, True).then_inc(s("odd_mm"), 1)
            b = banks.open(pe, "oddw", once("oddw_copied"))
            mm(b[0:L, 0:HC * NCH].rearrange("p (c n) -> p c n", c=HC), ident[:, DH:P],
               wdec.rearrange("p c (n t) -> p c n t", t=L)[:, :, :, L - 1], True, True).then_inc(once.give("oddw_mm"), 1)

            def products(n):
                for par in range(2):
                    b = banks.open(pe, f"gt{n}{par}", (s("gt_ready"), 2 * n + par + 1))
                    for c in range(HC):
                        last = mm(b[:, P * c:P * (c + 1)], bk[DH * par:DH * par + DH, c, n].rearrange("p a t -> p (a t)"),
                                  ar[DH * par:DH * par + DH, c, n].rearrange("p a t -> p (a t)"), True, True)
                    last.then_inc(s("gt_mm"), 1)
                for src, nm_ in ((bk, "bkt"), (zv, "vt")):
                    b = banks.open(pe, f"{nm_}{n}", (s(f"{nm_}_ready"), n + 1))
                    for c in range(HC):
                        last = pe.transpose(b[:, P * c:P * (c + 1)], src[:, c, n].rearrange("p a t -> p (a t)"), ident)
                    last.then_inc(s(f"{nm_}_mm"), 1)

            def invert(pair):
                for lv in range(LEVELS):
                    for i in range(2):
                        n = 2 * pair + i
                        k = LEVELS * n + lv
                        pe.wait_ge(s("nm_ready"), kth(n, lv) + 1)
                        if lv:
                            pe.wait_ge(s("t_ready"), t_count(n, lv - 1))
                        b = banks.open(pe, f"x_{k}", (s("xb_ready"), kth(n, lv) + 1))
                        for h in range(H):
                            rhs = ident[0:L, 0:L] if lv == 0 else tb[:, i, h, :]
                            last = mm(b[0:L, L * h:L * (h + 1)], nm[:, i, h, :], rhs, True, True)
                        last.then_inc(s("x_mm"), 1)
                    for i in range(2):
                        n = 2 * pair + i
                        if lv == 0:
                            continue
                        pe.wait_ge(s("xb_ready"), kth(n, lv) + 1)
                        if lv < LEVELS - 1:
                            b = banks.open(pe, f"t_{n}{lv}", (s("t_ready"), t_count(n, lv) - 1))
                            for h in range(H):
                                last = mm(b[0:L, L * h:L * (h + 1)], tt[:, i, h, :], xb[:, i, h, :], True, True)
                            last.then_inc(s("t_mm"), 1)
                        b = banks.open(pe, f"tt_{n}{lv}", (s("t_ready"), t_count(n, lv)))
                        for h in range(H):
                            last = mm(b[0:L, L * h:L * (h + 1)], xb[:, i, h, :], tt[:, i, h, :], True, True)
                        last.then_inc(s("t_mm"), 1)

            def advance(n):
                i = n % 2
                pe.wait_ge(s("su_ready"), n + 1)
                pe.wait_ge(s("lu_ready"), n + 1)
                pe.wait_ge(s("odd_copied"), 2 * HC)
                pe.wait_ge(s("even_copied"), 2)
                pe.wait_ge(s("vt_ready"), n + 1)
                b = banks.open(pe, f"u{n}", (s("u_ready"), n + 1))
                for h in range(H):
                    last = mm(b[0:L, DH * h:DH * (h + 1)], lu[:, n, h, :], su[:, i, h, :], True, True)
                last.then_inc(s("u_mm"), 1)
                pe.wait_ge(s("u_ready"), n + 1)
                pe.wait_ge(s("t_ready"), t_count(n, LEVELS - 1))
                b = banks.open(pe, f"sa{n}", (s("sa_ready"), n + 1))
                for h in range(H):
                    last = mm(b[0:L, DH * h:DH * (h + 1)], tt[:, i, h, :], ub[:, i, h, :], True, True)
                last.then_inc(s("sa_mm"), 1)
                pe.wait_ge(s("sa_ready"), n + 1)
                pe.wait_ge(s("bkt_ready"), n + 1)
                b = banks.open(pe, f"st{n}", (s("state_read"), n + 1))
                for h in range(H):
                    last = mm(b[0:L, DH * h:DH * (h + 1)], bkt[:, i, h, :], sav[:, i, h, :], True, True)
                last.then_inc(s("st_mm"), 1)
                b = banks.open(pe, f"y{n}", (s("yc_copied"), n + 1))
                for h in range(H):
                    o = b[DH * (h % 2):DH * (h % 2) + DH, L * (h // 2):L * (h // 2 + 1)]
                    mm(o, su[0:L, i, h, :], rt[:, n, h, :], True, False)
                    last = mm(o, sav[:, i, h, :], gt[:, i, h, L:2 * L], False, True)
                last.then_inc(s("y_mm"), 1)

            for pair in range(NCH // 2):
                products(2 * pair)
                products(2 * pair + 1)
                invert(pair)
                advance(2 * pair)
                advance(2 * pair + 1)
            pe.wait_ge(*once("final_state"))
            b = banks.open(pe, "fst", once("fst_copied"))
            for c in range(HC):
                last = pe.transpose(b[:, DH * c:DH * (c + 1)], su[0:L, 0, 2 * c:2 * c + 2, :].rearrange("p h v -> p (h v)"),
                                    ident[0:L, 0:L])
            last.then_inc(once.give("fst_mm"), 1)
            pe.wait_ge(s("syrow_loaded"), 16)
            b = banks.open(pe, "syt", once("syt_copied"))
            for c in range(HC):
                last = pe.transpose(b[:, NS * c:NS * (c + 1)], syrow[:, P * c:P * (c + 1)], ident[0:NS, 0:NS])
            last.then_inc(once.give("syt_mm"), 1)
            pe.wait_ge(*once("syt_copied"))
            pe.wait_ge(s("yc_copied"), NCH)
            head_sums("gnm", flat(yT)[:, HC * N:2 * HC * N])
            pe.wait_ge(*once("gn_squared"))
            head_sums("gnv", flat(tmpT)[:, 0:HC * N])

            pe.wait_ge(*once("mix_ready"))
            pe.wait_ge(s("o_copied"), 2 * HC)
            pe.wait_ge(*once("so_copied"))
            for j in range(DC):
                w = tile(MIX_TILE + j // 4).rearrange("p (c f) -> p c f", c=DC)
                b = banks.open(pe, f"wo{j}", (s("res1"), j + 1))
                for c in range(DC):
                    last = mm(b[:, 0:N], w[:, c, P * (j % 4):P * (j % 4 + 1)], yT[:, c, :], c == 0, c == DC - 1)
                last.then_inc(s("wo_mm"), 1)
            mean_square(1)

            pe.wait_ge(s("h_ready"), 2)

            def hidden(i):
                nf = FGRP[i][1]
                for j in range(nf // P):
                    for kind in ("gate", "up"):
                        w = tile(TILES.index((kind, i)))[:, 0:DC * nf].rearrange("p (c f) -> p c f", c=DC)
                        n = 4 * i + j
                        b = banks.open(pe, f"{kind}{n}", (s("act_ready"), n + 1))
                        for c in range(DC):
                            last = mm(b[:, 0:N], w[:, c, P * j:P * (j + 1)], hT[:, c, :], c == 0, c == DC - 1)
                        last.then_inc(s(f"{kind}_mm"), 1)

            def down(i):
                nf = FGRP[i][1]
                w = tile(TILES.index(("down", i)))[:, 0:nf // P * D].rearrange("p (c f) -> p c f", f=D)
                pe.wait_ge(s("act_ready"), FGRP[i][0] // P + nf // P)
                for j in range(DC):
                    b = banks.open(pe, f"down{i}_{j}", (s("ff_added"), DC * i + j + 1))
                    for c in range(nf // P):
                        last = mm(b[:, 0:N], w[:, c, P * j:P * (j + 1)], ffact[:, i % 2, c, :], c == 0, c == nf // P - 1)
                    last.then_inc(s("down_mm"), 1)

            hidden(0)
            for i in range(6):
                if i < 5:
                    hidden(i + 1)
                ada(1, 2 * i)
                ada(1, 2 * i + 1)
                down(i)
                fold(1, 2 * i)
                fold(1, 2 * i + 1)

            mean_square(2)
            pe.wait_ge(s("pool_rows"), 16)
            b = banks.open(pe, "pb0", (s("pbuf_copied"), 1))
            for c in range(4):
                last = pe.transpose(b[:, 120 * c:120 * (c + 1)], prow[0:120, P * c:P * (c + 1)], ident[0:120, 0:120])
            last.then_inc(s("pb_mm"), 1)
            b = banks.open(pe, "pb1", (s("pbuf_copied"), 2))
            for c in range(4):
                last = pe.transpose(b[:, 120 * c:120 * (c + 1)], prow[0:120, P * (4 + c):P * (5 + c)], ident[0:120, 0:120])
            last.then_inc(s("pb_mm"), 1)
            pe.wait_ge(s("h_ready"), 3)
            for half in range(2):
                b = banks.open(pe, f"hl{half}", (s("hl_copied"), half + 1))
                for c in range(4):
                    last = pe.transpose(b[0:NS + 16, P * c:P * (c + 1)], hT[:, 4 * half + c, NP - 16:N], ident)
                last.then_inc(s("hl_mm"), 1)
            pe.wait_ge(*once("z_ready"))
            pe.wait_ge(s("poolw_loaded"), 16)
            for j in range(DC):
                b = banks.open(pe, f"pool{j}", (s("res3"), j + 1))
                for c in range(2):
                    last = mm(b[:, 0:N], poolw[:, j // 2, c, P * (j % 2):P * (j % 2 + 1)], yT[:, 2 * (j // 2) + c, :],
                              c == 0, c == 1)
                last.then_inc(s("pool_mm"), 1)
            mean_square(3)

            pe.wait_ge(s("h_ready"), 4)
            b = banks.open(pe, "route", (s("logits"), 3))
            for blk, (t0, w) in enumerate(BLK):
                for c in range(DC):
                    last = mm(b[0:w, NE * blk:NE * (blk + 1)], hT[:, c, t0:t0 + w], routerw[:, c, :], c == 0, c == DC - 1)
            last.then_inc(once.give("route_mm"), 1)
            for n in range(6):
                t0, w = BLK[n // 2]
                b = banks.open(pe, f"ht{n}", (s("htok_ready"), n + 1))
                for c in range(4):
                    last = pe.transpose(b[0:w, P * c:P * (c + 1)], hT[:, 4 * (n % 2) + c, t0:t0 + w], ident)
                last.then_inc(s("ht_mm"), 1)
            pe.wait_ge(*once("picked"))
            b = banks.open(pe, "rank", (s("ranked"), 3))
            for blk, (t0, w) in enumerate(BLK):
                for e in range(blk + 1):
                    we = BLK[e][1]
                    tri = K("before")[0:we, 0:w] if e == blk else K("ones")[0:we, 0:w]
                    mm(b[0:w, NE * blk:NE * (blk + 1)], tri, pick[0:we, e, :], e == 0, e == blk)
            for e in range(3):
                we = BLK[e][1]
                last = mm(b[0:P, 3 * NE:4 * NE], K("ones")[0:we, 0:P], pick[0:we, e, :], e == 0, e == 2)
            last.then_inc(once.give("rank_mm"), 1)
            moe_tensor(pe, mm)

            pe.wait_ge(*once("res4"))
            for n in range(6):
                t0, w = BLK[n // 2]
                b = banks.open(pe, f"out{n}", (s("out_copied"), n + 1))
                for c in range(4):
                    last = pe.transpose(b[0:w, P * c:P * (c + 1)], xT[:, 4 * (n % 2) + c, t0:t0 + w], ident)
                last.then_inc(s("out_mm"), 1)

        @block.scalar
        def _(act):
            me = Counted(act)
            chain = s("act_chain")

            def copy(out, in_, sem):
                me.give(act.activation(out, in_, ACT.Copy), sem)

            for dst, src in vector_rows()[0]:
                act.dma_start(dst, src).then_inc(s("vec_loaded"), 16)
            act.wait_ge(s("c_loaded"), 32)
            me.step(act.activation(scrow[0:9, :], crow[0:9, :], ACT.Silu), once.give("siluc"))
            act.wait_ge(*once("c_turned"))
            act.wait_ge(*once("silucT_zero"))
            me.give(act.activation(silucT[:, :, 0:9], banks["c"][:, 0:72].rearrange("p (c j) -> p c j", c=DC),
                                   ACT.Copy), once.give("c_copied"))
            act.wait_ge(s("x_copied"), 5)

            def square_all(i):
                if i:
                    act.wait_ge(s("res"), i)
                me.give(act.activation(flat(tmpT), flat(xT), ACT.Square), s("squared"))

            def root(i):
                act.wait_ge(s("ms_read"), i + 1)
                me.give(act.activation(rstd[:, :], rstd[:, :], ACT.Sqrt), s("rooted"))

            square_all(0)
            root(0)

            def ada(layer, i):
                k = 12 * layer + i
                act.wait_ge(s("ada_mm"), k + 1)
                if k >= 2:
                    act.wait_ge(s("folded"), k - 1)
                copy(adap[layer][:, k % 2, :], banks[f"ada{layer}_{i}"][:, :], s("ada_copied"))

            for i in range(4):
                ada(0, i)

            def proj_chunk(n):
                kind, idx, _, m = WCHUNKS[n]
                dst = {"f": fqkv, "r": rp}[kind]
                return dst[0:m, idx, :], banks[f"win{n}"][0:m, 0:N]

            act.wait_ge(*once("last_zero"))
            n = 0
            for i, (_, _, cs) in enumerate(WIN):
                for _ in cs:
                    if n % 2:
                        act.wait_ge(s("win_mm"), n + 1)
                        copy(*proj_chunk(n), s("win_act"))
                    n += 1
                ada(0, 4 + i)
            act.wait_ge(s("win_dve"), (len(WCHUNKS) + 1) // 2)
            act.wait_ge(s("win_act"), len(WCHUNKS) // 2)
            me.give(act.activation(flat(tmpT), fqkv[:, 0:2 * HC, :].rearrange("p a b -> p (a b)"), ACT.Square), once.give("qk_squared"))
            act.wait_ge(*once("lf_abs"))
            me.step(act.activation(lftmp[:, 0, :], lftmp[:, 0, :], ACT.Exp), once.give("lf_exp"))
            act.wait_ge(*once("lf_one"))
            me.give(act.activation(lftmp[:, 0, :], lftmp[:, 0, :], ACT.Ln), once.give("lf_ln"))
            act.wait_ge(s("qkms_read"), 6)
            me.give(act.activation(flat(tmpT), flat(tmpT), ACT.Sqrt), once.give("qk_rooted"))
            for n in range(6):
                act.wait_ge(s("kv_turned"), n + 1)
                w = BLK[n % 3][1]
                copy(kvrow[0:w, n // 3, n % 3, :], banks[f"kv{n}"][0:w, :], s("kv_copied"))
            act.wait_ge(*once("lf_turned"))
            for blk, (t0, w) in enumerate(BLK):
                copy(lfrow[0:w, blk, :], banks["lf"][0:w, H * blk:H * (blk + 1)], s("lf_copied"))
            act.wait_ge(*once("last_turned"))
            copy(lastrow[0:NPC * 8, 0, :], banks["last"][0:NPC * 8, 0:P], s("last_copied"))
            copy(lastrow[0:NPC, 1, :], banks["last"][0:NPC, P:2 * P], s("last_copied"))

            for k in range(8):
                nk = P * (k % 2 + 1)
                act.wait_ge(s("shifted"), k + 1)
                v = pr[:, k % 2, :, 0:nk]
                me.give(act.activation(v, v, ACT.Exp), s("exped"))
                act.wait_ge(s("pt_mm"), k + 1)
                if k >= 2:
                    act.wait_ge(s("o_mm"), k - 1)
                nb = k % 2 + 1
                copy(prT[:, k % 2, :, 0:nb, :],
                     banks[f"pt{k // 2}{k % 2}"][:, 0:2 * nb * P].rearrange("p (h j q) -> p h j q", h=2, j=nb), s("probsT"))
                act.wait_ge(s("o_mm"), k + 1)
                copy(yT[:, k // 2, P * (k % 2):P * (k % 2 + 1)], banks[f"o{k // 2}{k % 2}"][:, 0:P], s("o_copied"))
            for q in range(NB):
                for half in range(2):
                    act.wait_ge(s("kt_mm"), 2 * q + half + 1)
                    if q >= 2:
                        act.wait_ge(s("ss_mm"), q - 1)
                    copy(ktb[:, q % 2, 2 * half:2 * half + 2, 0:PAST],
                         banks[f"kt{q}{half}"][:, :].rearrange("p (c k) -> p c k", c=2), s("kt_copied"))
                copy(ktb[:, q % 2, :, PAST:PAST + NT], fqkv[:, HC:2 * HC, NP + NT * q:NP + NT * (q + 1)], s("kt_copied"))
            act.wait_ge(*once("psm_shifted"))
            me.give(act.activation(psm, psm, ACT.Exp), once.give("psm_exped"))
            for g in range(2):
                act.wait_ge(s("pst_mm"), g + 1)
                copy(psT[:, g, 0:2, :], banks[f"pst{g}"][:, 0:2 * P].rearrange("p (j q) -> p j q", j=2), s("psT_ready"))
                copy(psT[0:32, g, 2, :], banks[f"pst{g}"][0:32, 2 * P:3 * P], s("psT_ready"))
            act.wait_ge(*once("so_mm"))
            copy(yT[:, 0:HC, NP:N], banks["so"][:, 0:HC * NS].rearrange("p (c t) -> p c t", c=HC), once.give("so_copied"))

            act.wait_ge(*once("rp_mixed"))
            me.give(act.activation(rp[0:LORA, PWL, :], rp[0:LORA, PWL, :], ACT.Tanh), once.give("wl_tanh"))
            me.give(act.activation(rp[:, PGL, :], rp[:, PGL, :], ACT.Sigmoid), once.give("gl_sigmoid"))
            for name, dst, col in (("dec", lw, VB_W0), ("icl", icl, VB_A0)):
                for c in range(HC):
                    act.wait_ge(*lora(name, "mm", c + 1))
                    me.give(act.activation(dst[:, c, :], banks[f"{name}{c}"][:, 0:N], ACT.Sigmoid,
                                           bias=vT[:, 1, col + c:col + c + 1]), s("lora_ready"))
            for c in range(HC):
                act.wait_ge(*lora("gat", "mm", c + 1))
                copy(gate[:, c, :], banks[f"gat{c}"][:, 0:N], s("lora_ready"))
            act.wait_ge(*once("kk_scaled"))
            me.give(act.activation(flat(tmpT)[:, 0:HC * N], kkT.rearrange("p a b -> p (a b)"), ACT.Square), once.give("kk_squared"))
            act.wait_ge(*sums("kks", "read", 3))
            me.give(act.activation(flat(tmpT)[:, 0:HC * N], flat(tmpT)[:, 0:HC * N], ACT.Sqrt), once.give("kk_rooted"))
            act.wait_ge(*once("cum_ready"))
            me.give(act.activation(lw[:, :, NP:N], lw[:, :, NP:N], ACT.Exp), s("decay_exp"))
            me.give(act.activation(wdec, cumv, ACT.Exp), s("decay_exp"))
            me.give(act.activation(winv, cumv, ACT.Exp, scale=-1.0), s("decay_exp"))
            me.give(act.activation(wprev, wprev, ACT.Exp), s("decay_exp"))
            act.wait_ge(s("mix_stored"), 16 * CACHE_STORES)
            for i in range(6):
                act.wait_ge(s("sr_mm"), i + 1)
                copy(srow[:, i, :], banks[f"sr{i}"][0:NS, :], s("srow_copied"))
            for c in range(HC):
                act.wait_ge(s("odd_mm"), c + 1)
                v = banks[f"odd{c}"][0:L, :].rearrange("p (n a t) -> p n a t", n=NCH, a=2)
                copy(lu[0:L, :, 2 * c + 1, :], v[:, :, 0, :], s("odd_copied"))
                copy(rt[:, :, 2 * c + 1, :], v[:, :, 1, :], s("odd_copied"))
            for pair in range(NCH // 2):
                for n in (2 * pair, 2 * pair + 1):
                    act.wait_ge(s("bkt_mm"), n + 1)
                    copy(bkt[:, n % 2].rearrange("p h k -> p (h k)"), banks[f"bkt{n}"][:, :], s("bkt_ready"))
                    act.wait_ge(s("vt_mm"), n + 1)
                    me.give(act.activation(sav[L:P, n % 2].rearrange("p h k -> p (h k)"), banks[f"vt{n}"][L:P, :], ACT.Copy), chain)
                    me.give(act.activation(su[L:P, n % 2].rearrange("p h k -> p (h k)"), banks[f"vt{n}"][L:P, :], ACT.Copy), s("vt_ready"))
                for lv in range(LEVELS):
                    for n in (2 * pair, 2 * pair + 1):
                        act.wait_ge(s("x_mm"), kth(n, lv) + 1)
                        copy(xb[:, n % 2].rearrange("p h k -> p (h k)"), banks[f"x_{LEVELS * n + lv}"][0:L, :], s("xb_ready"))
                for n in (2 * pair, 2 * pair + 1):
                    act.wait_ge(s("u_mm"), n + 1)
                    copy(ub[:, n % 2].rearrange("p h k -> p (h k)"), banks[f"u{n}"][0:L, :], s("u_ready"))
                    act.wait_ge(s("sa_mm"), n + 1)
                    copy(sav[0:L, n % 2].rearrange("p h k -> p (h k)"), banks[f"sa{n}"][0:L, :], s("sa_ready"))
                    act.wait_ge(s("y_mm"), n + 1)
                    copy(yT[:, HC:2 * HC, L * n:L * (n + 1)], banks[f"y{n}"][:, 0:HC * L].rearrange("p (c t) -> p c t", c=HC),
                         s("yc_copied"))
            act.wait_ge(*once("fst_mm"))
            copy(bkt[:, 0, 0:HC, :], banks["fst"][:, 0:HC * DH].rearrange("p (c k) -> p c k", c=HC), once.give("fst_copied"))
            act.wait_ge(*once("syt_mm"))
            copy(yT[:, HC:2 * HC, NP:N], banks["syt"][:, 0:HC * NS].rearrange("p (c t) -> p c t", c=HC), once.give("syt_copied"))
            act.wait_ge(*once("gn_centred"))
            me.give(act.activation(flat(tmpT)[:, 0:HC * N], flat(yT)[:, HC * N:2 * HC * N], ACT.Square), once.give("gn_squared"))
            act.wait_ge(*sums("gnv", "read", 3))
            me.give(act.activation(flat(tmpT)[:, 0:HC * N], flat(tmpT)[:, 0:HC * N], ACT.Sqrt), once.give("gn_rooted"))

            square_all(1)
            root(1)
            for n in range(FF // P):
                act.wait_ge(s("gate_mm"), n + 1)
                if n >= 2:
                    act.wait_ge(s("act_ready"), n - 1)
                me.give(act.activation(ffsilu[:, n % 2, :], banks[f"gate{n}"][:, 0:N], ACT.Silu), s("silu_ready"))
                if n >= 4 and (n % 4 == 3 or n == FF // P - 1):
                    ada(1, 2 * (n // 4) - 2)
                    ada(1, 2 * (n // 4) - 1)
            ada(1, 10)
            ada(1, 11)
            square_all(2)
            root(2)
            for half in range(2):
                act.wait_ge(s("pb_mm"), half + 1)
                act.wait_ge(*once("exts_zero"))
                me.give(act.activation(exts[:, 4 * half:4 * half + 4, :, 1:16],
                                       banks[f"pb{half}"][:, 0:480].rearrange("p (c b r) -> p c b r", c=4, r=PBUF),
                                       ACT.Copy), s("pbuf_copied"))
            for half in range(2):
                act.wait_ge(s("hl_mm"), half + 1)
                copy(hlast[0:NS + 16, 512 * half:512 * (half + 1)], banks[f"hl{half}"][0:NS + 16, :], s("hl_copied"))
            square_all(3)
            root(3)
            act.wait_ge(*once("z_used"))
            for n in range(6):
                w = BLK[n // 2][1]
                act.wait_ge(s("ht_mm"), n + 1)
                copy(htok[0:w, n // 2, 512 * (n % 2):512 * (n % 2 + 1)], banks[f"ht{n}"][0:w, :], s("htok_ready"))
            act.wait_ge(*once("top_ready"))
            me.give(act.activation(gate2[:, :, 0], gate2[:, :, 0], ACT.Exp), once.give("top_exped"))
            moe_scalar(act)
            for n in range(6):
                w = BLK[n // 2][1]
                act.wait_ge(s("out_mm"), n + 1)
                copy(outrow[0:w, n // 2, 512 * (n % 2):512 * (n % 2 + 1)], banks[f"out{n}"][0:w, :], s("out_copied"))

        @block.vector
        def _(dve):
            me = Counted(dve)
            chain = s("dve_chain")
            TT, TS, STT = dve.tensor_tensor, dve.tensor_scalar, dve.scalar_tensor_tensor

            def do(ins, sem=None):
                me.step(ins, sem or chain)

            dve.wait_ge(s("const_loaded"), 16)
            for n, (blk, c0, nc_) in enumerate(XJOBS):
                t0, w = BLK[blk]
                dve.wait_ge(s("x_turned"), n + 1)
                do(dve.tensor_copy(xT[:, c0:c0 + nc_, t0:t0 + w],
                                   banks[f"x{n}"][:, 0:nc_ * w].rearrange("p (c t) -> p c t", c=nc_)), s("x_copied"))

            def mod_tile(layer, i):
                dve.wait_ge(s("folded"), 12 * layer + i + 1)
                bias = vT[:, 0, 48 * layer + 4 * i:48 * layer + 4 * i + 4]
                do(TT(modT[layer][:, 4 * i:4 * i + 4, :], banks[f"fold{layer}_{i}"][:, 0:36].rearrange("p (j m) -> p j m", j=4),
                      spread(bias, 2, 9), ALU.add), s("mod_ready"))

            def mod(i, part):
                at = 24 * (i % 2) + 8 * part
                return modT[i // 2][:, at:at + 8, :]

            def gains(i):
                g = spread(vT[:, 0, VA_NORM[i]:VA_NORM[i] + 8], 2, 9)
                do(TS(gainT[i][:, :, :], mod(i, 1), 1.0, None, ALU.add))
                do(TT(gainT[i][:, :, :], gainT[i][:, :, :], g, ALU.mult))

            def mean_of(i):
                dve.wait_ge(s("ms_ready"), i + 1)
                do(TS(rstd[:, :], banks[f"ms{i}"][:, 0:N], 1.0 / D, RMS_EPS, ALU.mult, ALU.add), s("ms_read"))
                dve.wait_ge(s("rooted"), i + 1)
                do(dve.reciprocal(rstd[:, :], rstd[:, :]))

            def by_seq(ap):
                return ap.rearrange("p c (b t) -> p c b t", t=NT)

            def modulated(i):
                do(TT(hT[:, :, :], xT[:, :, :], spread(rstd[:, :], 1, DC), ALU.mult))
                hs = by_seq(hT[:, :, NP:N])
                do(TT(hs, hs, spread(gainT[i][:, :, 1:9], 3, NT), ALU.mult))
                do(TT(hs, hs, spread(mod(i, 0)[:, :, 1:9], 3, NT), ALU.add))
                for c in range(DC):
                    v = hT[:, c, 0:NP]
                    me.give(TS(v, v, gainT[i][:, c, 0:1], mod(i, 0)[:, c, 0:1], ALU.mult, ALU.add), chain)
                dve.wait_ge(chain, me.n[chain.name])
                do(dve.memset(small[:, 60:61], 0.0), s("h_ready"))

            def residual(src, gate_, j):
                do(STT(xT[:, j, 0:NP], src[:, 0:NP], gate_[:, j, 0:1], xT[:, j, 0:NP], ALU.mult, ALU.add))

            def residual_samples(src, gate_, j, sem):
                t = small[:, 0:NS]
                do(TT(t.rearrange("p (b t) -> p b t", t=NT), src[:, NP:N].rearrange("p (b t) -> p b t", t=NT),
                      spread(gate_[:, j, 1:9], 2, NT), ALU.mult), sem)
                do(TT(xT[:, j, NP:N], xT[:, j, NP:N], t, ALU.add))

            mean_of(0)
            dve.wait_ge(*once("vec_turned"))
            do(dve.tensor_copy(vT[:, 0, :], banks["vec"][:, 0:P]), once.give("vec_copied"))
            for i in range(4):
                mod_tile(0, i)
            gains(0)
            modulated(0)

            dve.wait_ge(*once("last_zero"))
            n = 0
            for i, (_, _, cs) in enumerate(WIN):
                for kind, idx, _, m in cs:
                    if n % 2 == 0:
                        dve.wait_ge(s("win_mm"), n + 1)
                        src = banks[f"win{n}"][0:m, 0:N]
                        if kind == "l":
                            do(TS(rstd[0:H, :], src, fbias[:, 0:1], None, ALU.add), s("win_dve"))
                        else:
                            do(dve.tensor_copy({"f": fqkv, "r": rp}[kind][0:m, idx, :], src), s("win_dve"))
                    n += 1
                if i == 2:
                    dve.wait_ge(*once("vec2_turned"))
                    do(dve.tensor_copy(vT[:, 1:3, :], banks["vec2"][:, 0:2 * P].rearrange("p (i f) -> p i f", i=2)),
                       once.give("vec2_copied"))
                    qg = vT[:, 1, VB_QG:VB_QG + 1]
                    do(TS(qg, qg, DH ** -0.5, None, ALU.mult))
                if i:
                    mod_tile(0, 3 + i)
            mod_tile(0, 11)
            gains(1)

            z = rstd[0:H, :]
            t0, t1 = lftmp[:, 0, :], lftmp[:, 1, :]
            dve.wait_ge(s("ada_mm"), 12)
            do(TS(t1, z, -1.0, None, ALU.mult))
            do(TT(t0, z, t1, ALU.min), once.give("lf_abs"))
            dve.wait_ge(*once("lf_exp"))
            do(TS(t0, t0, 1.0, None, ALU.add), once.give("lf_one"))
            do(TS(t1, z, 0.0, None, ALU.min))
            for i in range(6):
                dve.wait_ge(s("qkms"), i + 1)
                do(TS(flat(tmpT)[:, 384 * i:384 * (i + 1)], banks[f"qkms{i}"][:, 0:384], 1.0 / DH, RMS_EPS, ALU.mult, ALU.add),
                   s("qkms_read"))
            dve.wait_ge(*once("lf_ln"))
            do(TT(logf, t1, t0, ALU.subtract), once.give("logf_ready"))
            do(dve.tensor_tensor_scan(negF, K("restart", H), logf, 0.0, ALU.mult, ALU.add))
            do(TS(negF, negF, -1.0, None, ALU.mult), once.give("negF_ready"))
            dve.wait_ge(*once("qk_rooted"))
            do(dve.reciprocal(flat(tmpT), flat(tmpT)))
            dve.wait_ge(s("win_act"), len(WCHUNKS) // 2)
            for part, g, sem in ((1, VB_KG, "k_ready"), (0, VB_QG, "q_ready")):
                v = fqkv[:, HC * part:HC * (part + 1), :].rearrange("p a b -> p (a b)")
                r = flat(tmpT)[:, HC * N * part:HC * N * (part + 1)]
                do(STT(v, v, vT[:, 1, g:g + 1], r, ALU.mult, ALU.mult), once.give(sem))
            do(dve.tensor_copy(lastP, rp[:, :, NP - 1]))
            do(dve.tensor_copy(lastS, rp[:, :, NP + NT - 1:N:NT]), once.give("last_ready"))
            do(TT(diff[:, :, 1:NP], rp[:, :, 0:NP - 1], rp[:, :, 1:NP], ALU.subtract))
            do(TS(diff[:, :, 0], rp[:, :, 0], -1.0, None, ALU.mult))
            rs, ds_ = by_seq(rp[:, :, NP:N]), by_seq(diff[:, :, NP:N])
            do(TT(ds_[:, :, :, 1:NT], rs[:, :, :, 0:NT - 1], rs[:, :, :, 1:NT], ALU.subtract))
            prev = vT[:, 2, 0:NPC * NB].rearrange("p (c b) -> p c b", c=NPC)
            do(TT(ds_[:, :, :, 0], prev, rs[:, :, :, 0], ALU.subtract))
            do(TT(diff, diff, spread(vT[:, 1, VB_MU:VB_MU + NPC], 2, N), ALU.mult))
            do(TT(rp, rp, diff, ALU.add), once.give("rp_mixed"))

            for k in range(8):
                qb = k % 2
                nk = P * (qb + 1)
                if k >= 2:
                    dve.wait_ge(s("pt_mm"), k - 1)
                for par in range(2):
                    dve.wait_ge(s("s_mm"), 2 * k + par + 1)
                    do(TT(pr[:, k % 2, par, 0:nk], banks[f"s{k // 2}{qb}{par}"][:, 0:nk], K("causal")[:, 256 - nk:256], ALU.add),
                       s("scored"))
                v, m = pr[:, k % 2, :, 0:nk], small[:, 40:42]
                do(dve.tensor_reduce(m, v, AX.X, ALU.max))
                do(TT(v, v, spread(m, 2, nk), ALU.subtract), s("shifted"))
                dve.wait_ge(s("exped"), k + 1)
                do(dve.tensor_reduce(m, v, AX.X, ALU.add))
                do(dve.reciprocal(m, m))
                do(TT(v, v, spread(m, 2, nk), ALU.mult), s("probs"))
            for q in range(NB):
                dve.wait_ge(s("ss_mm"), q + 1)
                do(dve.tensor_copy(psm[32 * (q % 4):32 * (q % 4) + 32, q // 4, :], banks[f"ss{q}"][0:32, 0:PAST + NT]), s("ss_copied"))
            do(TT(psm[:, :, PAST:PAST + NT], psm[:, :, PAST:PAST + NT], spread(K("newmask"), 1, 2), ALU.add))
            m = small[:, 42:44]
            do(dve.tensor_reduce(m, psm, AX.X, ALU.max))
            do(TT(psm, psm, spread(m, 2, PAST + NT), ALU.subtract), once.give("psm_shifted"))
            dve.wait_ge(*once("psm_exped"))
            do(dve.tensor_reduce(m, psm, AX.X, ALU.add))
            do(dve.reciprocal(m, m))
            do(TT(psm, psm, spread(m, 2, PAST + NT), ALU.mult))
            for g in range(2):
                do(TT(pnew[:, g, :, :], spread(psm[:, g, PAST:PAST + NT], 1, NB),
                      spread(K("seqmask")[:, 8 * g:8 * g + 8], 2, NT), ALU.mult), chain if g == 0 else once.give("psm_ready"))

            kx, rx, vx = rp[:, PK:PK + HC, :], rp[:, PR:PR + HC, :], rp[:, PV:PV + HC, :]

            def fl(t):
                return t.rearrange("p a b -> p (a b)")

            dve.wait_ge(*once("so_mm"))
            dve.wait_ge(s("mix_stored"), 16 * CACHE_STORES)
            for c in range(HC):
                do(TS(kkT[:, c, :], kx[:, c, :], vT[:, 1, VB_KK + c:VB_KK + c + 1], None, ALU.mult),
                   once.give("kk_scaled") if c == HC - 1 else chain)
            dve.wait_ge(*lora("icl", "ready", HC))
            dve.wait_ge(*lora("dec", "ready", HC))
            for c in range(HC):
                t = flat(tmpT)[:, HC * N + N * c:HC * N + N * (c + 1)]
                do(TS(t, icl[:, c, :], -1.0, vT[:, 1, VB_KA + c:VB_KA + c + 1], ALU.add, ALU.mult))
                do(STT(kx[:, c, :], t, 1.0, kx[:, c, :], ALU.add, ALU.mult))
                do(STT(t, rx[:, c, :], vT[:, 1, VB_RK + c:VB_RK + c + 1], kx[:, c, :], ALU.mult, ALU.mult),
                   once.give("rk_ready") if c == HC - 1 else chain)
            for i in range(3):
                dve.wait_ge(*sums("kks", "mm", i + 1))
                do(TS(flat(tmpT)[:, 384 * i:384 * (i + 1)], banks[f"kks{i}"][:, 0:384], 1e-24, None, ALU.max), s("sums_read"))
            dve.wait_ge(*once("kk_rooted"))
            r = flat(tmpT)[:, 0:HC * N]
            do(dve.reciprocal(r, r))
            do(TT(fl(kkT), fl(kkT), r, ALU.mult))
            do(TT(fl(bT), fl(kkT), fl(icl), ALU.mult))
            do(TS(fl(kkT), fl(kkT), -1.0, None, ALU.mult))
            for i in range(3):
                dve.wait_ge(*sums("bon", "mm", i + 1))
                o = slice(384 * i, 384 * (i + 1))
                do(TT(fl(icl)[:, o], banks[f"bon{i}"][:, 0:384], fl(vx)[:, o], ALU.mult), s("sums_read"))
            do(TS(fl(lw), fl(lw), -DECAY, None, ALU.mult))
            for c in range(HC):
                do(dve.tensor_tensor_scan(cumv[:, c, :], K("reset"), lw[:, c, 0:NP], 0.0, ALU.mult, ALU.add))
            do(TT(wprev, cumv, lw[:, :, 0:NP], ALU.subtract), once.give("cum_ready"))
            dve.wait_ge(s("decay_exp"), 4)
            do(dve.memset(small[:, 61:62], 0.0), once.give("delta_ops"))

            def chunks(ap):
                return ap[:, :, 0:NP].rearrange("p c (n t) -> p c n t", t=L)

            do(TT(ar[:, :, :, 0, :], chunks(kkT), chunks(wprev), ALU.mult))
            do(TT(ar[:, :, :, 1, :], chunks(rx), chunks(wdec), ALU.mult))
            do(TT(bk[:, :, :, 0, :], chunks(bT), chunks(winv), ALU.mult))
            do(TT(bk[:, :, :, 1, :], chunks(kx), chunks(winv), ALU.mult))
            do(dve.tensor_copy(zv[:, :, :, 1, :], chunks(vx)))
            do(dve.memset(zv[:, :, :, 0, :], 0.0), once.give("packed"))
            dve.wait_ge(*once("oddw_mm"))
            do(dve.tensor_copy(wlx.rearrange("p (c a) n -> p c a n", a=2)[:, :, 1, :],
                               banks["oddw"][0:L, 0:HC * NCH].rearrange("p (c n) -> p c n", c=HC)), once.give("oddw_copied"))
            do(dve.tensor_copy(wlx.rearrange("p (c a) n -> p c a n", a=2)[:, :, 0, :],
                               wdec[0:L].rearrange("p c (n t) -> p c n t", t=L)[:, :, :, L - 1]))
            do(dve.memset(su[0:L, 0], 0.0), s("su_ready"))

            def rows(t, i):
                return spread(svec[:, t, i, :], 1, 32)

            def sample_ops():
                dve.wait_ge(s("svec_loaded"), 16 * 3 * NB)
                dve.wait_ge(s("sst_loaded"), 16)
                for t in range(NT):
                    yield lambda t=t: do(TT(sprod, sst, rows(t, 1), ALU.mult))
                    yield lambda t=t: do(dve.tensor_reduce(ssa, sprod, AX.X, ALU.add))
                    yield lambda t=t: do(TT(sst, sst, rows(t, 0), ALU.mult))
                    yield lambda t=t: do(TT(sprod, spread(ssa, 2, DH), rows(t, 2), ALU.mult))
                    yield lambda t=t: do(TT(sst, sst, sprod, ALU.add))
                    yield lambda t=t: do(TT(sprod, spread(sval[:, t, :], 2, DH), rows(t, 3), ALU.mult))
                    yield lambda t=t: do(TT(sst, sst, sprod, ALU.add))
                    yield lambda t=t: do(TT(sprod, sst, rows(t, 4), ALU.mult))
                    yield lambda t=t: do(dve.tensor_reduce(sy[:, t, :], sprod, AX.X, ALU.add), s("sy_ready"))

            pending = sample_ops()

            def some(k):
                for _, op in zip(range(k), pending):
                    op()

            def fh(ap):
                return ap.rearrange("p h k -> p (h k)")

            for pair in range(NCH // 2):
                for n in (2 * pair, 2 * pair + 1):
                    for par in range(2):
                        dve.wait_ge(s("gt_mm"), 2 * n + par + 1)
                        do(TT(gt[:, n % 2].rearrange("p (c a) t -> p c a t", a=2)[:, :, par, :],
                              banks[f"gt{n}{par}"][:, :].rearrange("p (c t) -> p c t", c=HC),
                              spread(K("chunk"), 1, HC), ALU.mult), s("gt_ready"))
                for lv in range(LEVELS):
                    for n in (2 * pair, 2 * pair + 1):
                        i = n % 2
                        if lv == 0:
                            dve.wait_ge(s("x_mm"), kth(n, lv) + 1)
                            dve.wait_ge(s("xb_ready"), kth(n, lv) + 1)
                            idb = spread(K("ident")[0:L, 0:L], 1, H)
                            do(TT(tb[:, i], xb[:, i], idb, ALU.add), s("t_ready"))
                            do(TT(tt[:, i], nm[:, i], idb, ALU.add), s("t_ready"))
                            continue
                        if lv < LEVELS - 1:
                            dve.wait_ge(s("t_mm"), t_mms(n, lv) - 1)
                            do(TT(fh(tb[:, i]), fh(tb[:, i]), banks[f"t_{n}{lv}"][0:L, :], ALU.add), s("t_ready"))
                        dve.wait_ge(s("t_mm"), t_mms(n, lv))
                        do(TT(fh(tt[:, i]), fh(tt[:, i]), banks[f"tt_{n}{lv}"][0:L, :], ALU.add), s("t_ready"))
                    some(3)
                for n in (2 * pair, 2 * pair + 1):
                    i = n % 2
                    dve.wait_ge(s("st_mm"), n + 1)
                    nxt = su[0:L, (n + 1) % 2]
                    do(TT(fh(nxt), fh(su[0:L, i]), banks[f"st{n}"][0:L, :], ALU.add), s("state_read"))
                    do(TT(nxt, nxt, spread(wlx[:, :, n], 2, DH), ALU.mult), s("su_ready") if n < NCH - 1 else once.give("final_state"))
            some(36)

            y2 = flat(yT)[:, HC * N:2 * HC * N]
            for i in range(3):
                o = slice(384 * i, 384 * (i + 1))
                dve.wait_ge(*sums("gnm", "mm", 3 if i == 0 else i + 1))
                do(STT(y2[:, o], banks[f"gnm{i}"][:, 0:384], -1.0 / DH, y2[:, o], ALU.mult, ALU.add), s("sums_read"))
            do(dve.memset(small[:, 62:63], 0.0), once.give("gn_centred"))
            for i in range(3):
                dve.wait_ge(*sums("gnv", "mm", i + 1))
                do(TS(flat(tmpT)[:, 384 * i:384 * (i + 1)], banks[f"gnv{i}"][:, 0:384], 1.0 / DH, GN_EPS, ALU.mult, ALU.add),
                   s("sums_read"))
            dve.wait_ge(*once("gn_rooted"))
            do(dve.reciprocal(r, r))
            do(TT(y2, y2, r, ALU.mult))
            for c in range(HC):
                v = yT[:, HC + c, :]
                do(TS(v, v, vT[:, 1, VB_LNW + c:VB_LNW + c + 1], vT[:, 1, VB_LNB + c:VB_LNB + c + 1], ALU.mult, ALU.add))
            do(TT(y2, y2, fl(icl), ALU.add))
            dve.wait_ge(*lora("gat", "ready", HC))
            do(TT(y2, y2, fl(gate), ALU.mult), once.give("mix_ready"))

            for j in range(DC):
                dve.wait_ge(s("wo_mm"), j + 1)
                src = banks[f"wo{j}"]
                residual(src, mod(0, 2), j)
                residual_samples(src, mod(0, 2), j, s("res1"))
            do(dve.memset(small[:, 63:64], 0.0), s("res"))
            mean_of(1)
            modulated(1)

            def hidden(i):
                for n in range(4 * i, min(4 * i + 4, FF // P)):
                    dve.wait_ge(s("silu_ready"), n + 1)
                    dve.wait_ge(s("up_mm"), n + 1)
                    if i >= 2:
                        dve.wait_ge(s("down_mm"), DC * (i - 1))
                    do(TT(ffact[:, i % 2, n % 4, :], ffsilu[:, n % 2, :], banks[f"up{n}"][:, 0:N], ALU.mult), s("act_ready"))

            def down(i):
                for j in range(DC):
                    dve.wait_ge(s("down_mm"), DC * i + j + 1)
                    src = banks[f"down{i}_{j}"][:, 0:N]
                    if i == 0:
                        do(dve.tensor_copy(yT[:, j, :], src), s("ff_added"))
                    else:
                        do(TT(yT[:, j, :], yT[:, j, :], src, ALU.add), s("ff_added"))

            hidden(0)
            for i in range(6):
                if i < 5:
                    hidden(i + 1)
                down(i)
                mod_tile(1, 2 * i)
                mod_tile(1, 2 * i + 1)
            gains(2)
            gains(3)
            gp = mod(2, 2)
            do(TT(gp, gp, spread(vT[:, 1, VB_PS:VB_PS + 8], 2, 9), ALU.mult))
            for j in range(DC):
                residual(yT[:, j, :], mod(1, 2), j)
                residual_samples(yT[:, j, :], mod(1, 2), j, chain)
            do(dve.memset(small[:, 59:60], 0.0), s("res"))

            do(dve.memset(exts[:, :, :, 0], 0.0), once.give("exts_zero"))
            do(dve.memset(ext[:, :, 0:16], 0.0))
            mean_of(2)
            modulated(2)
            do(dve.tensor_copy(ext[:, :, 16:16 + NP], hT[:, :, 0:NP]))
            dve.wait_ge(s("pbuf_copied"), 2)
            hs = by_seq(hT[:, :, NP:N])
            do(dve.tensor_copy(exts[:, :, :, 16:20], hs))
            ext2 = flat(tmpT)[:, 0:DC * (16 + NP)].rearrange("p (c t) -> p c t", c=DC)
            exts2 = other[:, 0:DC * NB * 20].rearrange("p (c b t) -> p c b t", c=DC, b=NB)
            pair_ = [(ext, exts), (ext2, exts2)]
            for lv in range(4):
                (a0, b0), (a1, b1) = pair_[lv % 2], pair_[1 - lv % 2]
                sh, c0, lo = 1 << lv, 2 * lv, (2 << lv) - 1
                do(TT(a1[:, c0:DC, lo:], a0[:, c0:DC, lo:], a0[:, c0:DC, lo - sh:16 + NP - sh], ALU.add))
                do(TT(b1[:, c0:DC, :, lo:], b0[:, c0:DC, :, lo:], b0[:, c0:DC, :, lo - sh:20 - sh], ALU.add))
                g = slice(c0, c0 + 2)
                do(STT(yT[:, g, 0:NP], a1[:, g, 16:16 + NP], 1.0 / WINS[lv], hT[:, g, 0:NP], ALU.mult, ALU.subtract))
                head = yT[:, g, 0:16]
                cnt = K("count").rearrange("p (g t) -> p g t", g=4)[:, lv, :]
                do(TT(head, a1[:, g, 16:32], spread(cnt, 1, 2), ALU.mult))
                do(TT(head, head, hT[:, g, 0:16], ALU.subtract))
                for c in (c0, c0 + 1):
                    do(STT(by_seq(yT[:, :, NP:N])[:, c], b1[:, c, :, 16:20], 1.0 / WINS[lv], hs[:, c], ALU.mult, ALU.subtract))
            do(dve.memset(small[:, 58:59], 0.0), once.give("z_ready"))
            for j in range(DC):
                dve.wait_ge(s("pool_mm"), j + 1)
                src = banks[f"pool{j}"]
                residual(src, mod(2, 2), j)
                residual_samples(src, mod(2, 2), j, s("res3"))
            do(dve.memset(small[:, 57:58], 0.0), s("res"))
            mean_of(3)
            modulated(3)
            dve.wait_ge(s("pool_stored"), 16 * (2 + NB))
            for table in (comb, slot_at, later):
                do(dve.memset(table, 0.0))
            do(dve.memset(flat(yT), 0.0), once.give("z_used"))

            dve.wait_ge(*once("route_mm"))
            for blk, (t0_, w) in enumerate(BLK):
                lg = logit[0:w, blk, :]
                do(TT(lg, banks["route"][0:w, NE * blk:NE * (blk + 1)], routerb[0:w, :], ALU.add), s("logits"))
                do(dve.max(top[0:w, blk, :], lg))
                do(dve.max_index(topi[0:w, blk, :].bitcast(U32), top[0:w, blk, :], lg))
                do(dve.tensor_copy(logit[0:w, blk, 0:2], topi[0:w, blk, 0:2].bitcast(U32)))
                for k, dst in enumerate((pick, comb)):
                    do(TS(dst[0:w, blk, 0:NE], K("iota")[0:w, 0:NE], logit[0:w, blk, k:k + 1], None, ALU.is_equal))
                do(TT(gate2[0:w, blk, 0:1], top[0:w, blk, 1:2], top[0:w, blk, 0:1], ALU.subtract),
                   once.give("top_ready") if blk == 2 else chain)
            dve.wait_ge(*once("top_exped"))
            for blk, (t0_, w) in enumerate(BLK):
                e, one, lo_, hi_ = (gate2[0:w, blk, i:i + 1] for i in range(4))
                do(TS(one, e, 1.0, None, ALU.add))
                do(dve.reciprocal(hi_, one))
                do(TT(lo_, e, hi_, ALU.mult))
                first, second = pick[0:w, blk, :], comb[0:w, blk, 0:NE]
                do(TT(logit[0:w, blk, :], first, second, ALU.add))
                do(TS(first, first, hi_, None, ALU.mult))
                do(STT(second, second, lo_, first, ALU.mult, ALU.add))
                do(dve.tensor_copy(first, logit[0:w, blk, :]), once.give("picked") if blk == 2 else chain)
            dve.wait_ge(*once("rank_mm"))
            do(dve.tensor_copy(small[:, 48:56], banks["rank"][:, 3 * NE:4 * NE]))
            for blk, (t0_, w) in enumerate(BLK):
                sl = slot_at[0:w, blk, 0:NE]
                do(STT(sl, banks["rank"][0:w, NE * blk:NE * (blk + 1)], 1.0, pick[0:w, blk, :], ALU.add, ALU.mult),
                   s("ranked"))
                do(TS(sl, sl, -1.0, None, ALU.add))
                do(TS(later[0:w, blk, :], sl, -float(CAP), None, ALU.add))
            count = moe_vector(dve, do)
            dve.wait_ge(*after("comb_added", count * DC))
            for j in range(DC):
                residual(yT[:, j, :], mod(3, 2), j)
                residual_samples(yT[:, j, :], mod(3, 2), j, chain)
            do(dve.memset(small[:, 56:57], 0.0), once.give("res4"))

        @block.gpsimd
        def _(pool):
            me = Counted(pool)
            me.step(pool.memset(vrow[:, 1:3, :], 0.0), once.give("vrow_zero"))
            me.step(pool.memset(silucT[:, :, :], 0.0), once.give("silucT_zero"))
            for dst, src in vector_rows()[1]:
                pool.dma_start(dst, src).then_inc(s("vec2_loaded"), 16)
            pool.wait_ge(s("x_turned"), len(XJOBS))
            me.step(pool.memset(rp[LORA:P, PWL, :], 0.0), s("pool_chain"))
            me.step(pool.memset(rp[LORA:P, PAL, :], 0.0), once.give("last_zero"))
            pool.wait_ge(s("ada_mm"), 12)
            me.step(pool.memset(qbd, 0.0), s("pool_chain"))
            pool.wait_ge(*once("q_ready"))
            for c in range(HC):
                for par in range(2):
                    p0, at = DH * par, NT * (2 * c + par)
                    me.step(pool.tensor_copy(qbd[p0:p0 + DH, :, c, at:at + NT],
                                             fqkv[p0:p0 + DH, c, NP:N].rearrange("p (q t) -> p q t", t=NT)), s("qbd_ready"))
            stores = []

            def store(dst, src):
                pool.dma_start(dst, src).then_inc(s("mix_stored"), 16)
                stores.append(1)

            pool.wait_ge(s("kv_copied"), 6)
            for i, (dp, dsm) in enumerate(((k_p, k_s), (v_p, v_s))):
                store(dp[0, 0].rearrange("(b p) h d -> p b (h d)", p=P), kvrow[:, i, 0:2, :])
                store(dsm[0].rearrange("b t h d -> (b t) (h d)"), kvrow[0:NS, i, 2, :])
            pool.wait_ge(s("lf_copied"), 3)
            store(lf_p[0, 0].rearrange("(b p) h -> p b h", p=P), lfrow[:, 0:2, :])
            store(lf_s[0].rearrange("b t h -> (b t) h"), lfrow[0:NS, 2, :])
            pool.wait_ge(s("last_copied"), 2)
            for i, (at, w) in enumerate(PIECES):
                store(sh_s[0][:, at:at + w], lastrow[NB * i:NB * (i + 1), 0, 0:w])
                store(sh_p[0][:, at:at + w], lastrow[i:i + 1, 1, 0:w])
            assert len(stores) == CACHE_STORES
            for q in range(NB):
                pool.wait_ge(s(f"k_page{q % 2}"), 64 * (q // 2 + 1))
                me.step(pool.tensor_copy(pastlf4[:, q].rearrange("p j (h t) -> p j h t", t=NT),
                                         spread(pastlf[:, q], 3, NT)), s("lf_spread"))
            pool.wait_ge(*once("packed"))
            lu5 = lu[0:L].rearrange("p n (c a) t -> p n c a t", a=2)
            rt5 = rt.rearrange("p n (c a) t -> p n c a t", a=2)
            for c in range(HC):
                me.step(pool.tensor_copy(lu5[:, :, c, 0, :], ar[0:L, c, :, 0, :]), s("even_copied") if c == HC - 1 else s("pool_chain"))
            for c in range(HC):
                me.step(pool.tensor_copy(rt5[:, :, c, 0, :], ar[0:L, c, :, 1, :]), s("even_copied") if c == HC - 1 else s("pool_chain"))

            def level(n, lv):
                mask = spread(K("levels")[0:L, L * lv:L * (lv + 1)], 1, H)
                me.step(pool.tensor_tensor(nm[:, n % 2], gt[0:L, n % 2, :, 0:L], mask, ALU.mult), s("nm_ready"))

            for pair in range(NCH // 2):
                both = (2 * pair, 2 * pair + 1)
                for n in both:
                    pool.wait_ge(s("gt_ready"), 2 * n + 2)
                    level(n, 0)
                for n in both:
                    me.step(pool.tensor_copy(lu[L:P, n], gt[L:P, n % 2, :, 0:L]), s("lu_ready"))
                for lv in range(1, LEVELS):
                    for n in both:
                        pool.wait_ge(s("x_mm"), kth(n, lv - 1) + 1)
                        if lv == 1:
                            pool.wait_ge(s("t_ready"), t_count(n, 0))
                        level(n, lv)
            pool.wait_ge(*once("fst_copied"))
            store(st_p[0, 0].rearrange("(c a) v k -> (a v) c k", a=2), bkt[:, 0, 0:HC, :])
            pool.wait_ge(s("sy_ready"), NT)
            store(st_s[0].rearrange("b h (f v) k -> (b h f) (v k)", f=2), sst.rearrange("p v k -> p (v k)"))
            mix_stores[0] = len(stores)
            pool.wait_ge(s("mix_stored"), 16 * len(stores))
            pool.dma_start(pool_s[0][:, 0:PBUF - NT, :], a["state_pool"][0][:, NT:PBUF, :]).then_inc(s("pool_stored"), 16)
            pool.wait_ge(s("hl_copied"), 2)
            pool.dma_start(pool_p[0, 0], hlast[1:16, :]).then_inc(s("pool_stored"), 16)
            for q in range(NB):
                pool.dma_start(pool_s[0, q, PBUF - NT:PBUF, :], hlast[16 + NT * q:16 + NT * (q + 1), :]).then_inc(s("pool_stored"), 16)
            pool.wait_ge(s("pool_stored"), 16 * (2 + NB))

        @block.sync
        def _(sp):
            sp.dma_start(const[:, :], a["constants"]).then_inc(s("const_loaded"), 16)
            sp.dma_start(crow[0:1, :], a["c_prompt"]).then_inc(s("c_loaded"), 16)
            sp.dma_start(crow[1:9, :], a["c_sample"]).then_inc(s("c_loaded"), 16)
            for blk in range(2):
                sp.dma_start(xrow[:, blk, :], a["x_prompt"][0, P * blk:P * (blk + 1), :]).then_inc(s("x_loaded"), 16)
            sp.dma_start(xrow[0:NS, 2, :], a["x_sample"].rearrange("b t d -> (b t) d")).then_inc(s("x_loaded"), 16)

            def load(g):
                if g >= SLOTS:
                    sp.wait_ge(*used(g - SLOTS))
                dst, src = tile_source(g)
                sp.dma_start(dst, src).then_inc(s(f"slot{g % SLOTS}"), 16)

            for g in range(4):
                load(g)
            small_loads = [(w2[:, :], a["rwkv_w2"][0]), (a2[:, :], a["rwkv_a2"][0]), (g2[:, :], a["rwkv_g2"][0]),
                           (fbias[:, :], a["fox_f_bias"].rearrange("o h -> h o")),
                           (routerw[:, :, :], a["moe_router_w"][0].rearrange("(c p) e -> p c e", p=P)),
                           (routerb[:, :], a["moe_router_b"].to_broadcast([P, NE])),
                           (pages[:, :], a["page_table"].rearrange("b j -> (b j)").unsqueeze(0))]
            for dst, src in small_loads:
                sp.dma_start(dst, src).then_inc(s("small_loaded"), 16)
            for g in range(4, MIX_TILE):
                load(g)
            sp.wait_ge(s("ada_mm"), 12)
            sp.dma_start(sst.rearrange("p v k -> p (v k)"),
                         a["state_rwkv"][0].rearrange("b h (f v) k -> (b h f) (v k)", f=2)).then_inc(s("sst_loaded"), 16)
            sp.wait_ge(s("small_loaded"), 16 * len(small_loads))
            for q in range(NB):
                if q >= 2:
                    sp.wait_ge(s("kt_mm"), 2 * (q - 1))
                for j in range(NPG):
                    page = sp.value_load(pages[0:1, NPG * q + j:NPG * q + j + 1], min_val=0,
                                         max_val=a["cache_fox_k"].shape[1] - 1)
                    for dst, name, sem in ((ksamp[:, q % 2, j, :], "cache_fox_k", f"k_page{q % 2}"),
                                           (vsamp[:, q, j, :], "cache_fox_v", "v_pages")):
                        sp.dma_start(dst, a[name][0, bass.ds(page, 1)].rearrange("o p h d -> (o p) (h d)")).then_inc(s(sem), 16)
                    sp.dma_start(pastlf[:, q, j, :], a["cache_fox_logf"][0, bass.ds(page, 1)].rearrange("o p h -> (o p) h"))\
                        .then_inc(s(f"k_page{q % 2}"), 16)
            sp.wait_ge(s("srow_copied"), 6)
            sp.dma_start(scratch.rearrange("b t q h k -> (b t) (q h k)"), srow.rearrange("p q k -> p (q k)")).then_inc(s("srow_stored"), 16)
            sp.wait_ge(s("srow_stored"), 16)
            for q in range(NB):
                for f in range(2):
                    sp.dma_start(svec[2 * H * q + f:2 * H * (q + 1):2].rearrange("p t i k -> p (t i) k"),
                                 scratch[q].rearrange("t i h k -> h (t i) k")).then_inc(s("svec_loaded"), 16)
                sp.dma_start(sval[2 * H * q:2 * H * (q + 1)], scratch[q, :, 5].rearrange("t h (f k) -> (h f) t k", f=2))\
                    .then_inc(s("svec_loaded"), 16)
            sp.wait_ge(s("sy_ready"), NT)
            for q in range(NB):
                sp.dma_start(scratch_y[q].rearrange("t f k -> f t k"), sy[2 * H * q:2 * H * (q + 1)]).then_inc(s("sy_stored"), 16)
            sp.wait_ge(s("sy_stored"), 16 * NB)
            sp.dma_start(syrow, scratch_y.rearrange("b t f k -> (b t) (f k)")).then_inc(s("syrow_loaded"), 16)
            sp.wait_ge(*once("mix_ready"))
            sp.wait_ge(s("mix_stored"), 16 * mix_stores[0])
            sp.dma_start(prow[0:NB * PBUF, :], a["state_pool"][0].rearrange("b r d -> (b r) d")).then_inc(s("pool_rows"), 16)
            sp.dma_start(poolw, a["pool_w"][0].rearrange("g (c p) f -> p g c f", p=P)).then_inc(s("poolw_loaded"), 16)
            for g in range(MIX_TILE, len(TILES)):
                load(g)
            moe_sync(sp)
            sp.wait_ge(s("out_copied"), 6)
            sp.dma_start(y_p[0].rearrange("(b p) d -> p b d", p=P), outrow[:, 0:2, :]).then_inc(s("y_stored"), 16)
            sp.dma_start(y_s.rearrange("b t d -> (b t) d"), outrow[0:NS, 2, :]).then_inc(s("y_stored"), 16)
            sp.wait_ge(s("y_stored"), 32)


INPUTS = ["x_prompt", "x_sample", "c_prompt", "c_sample", "cache_fox_k", "cache_fox_v", "cache_fox_logf", "page_table",
          "state_rwkv", "state_rwkv_shift", "state_pool", "norm1_g", "norm2_g", "ada_w", "ada_b", "w_in", "w_out",
          "fox_q_gain", "fox_k_gain", "fox_f_bias", "rwkv_mu", "rwkv_w0", "rwkv_w2", "rwkv_a0", "rwkv_a2", "rwkv_g2",
          "rwkv_k_k", "rwkv_k_a", "rwkv_r_k", "rwkv_ln_w", "rwkv_ln_b", "ffn_w_gate", "ffn_w_up", "ffn_w_down",
          "pool_w", "pool_scale", "moe_router_w", "moe_router_b", "moe_w_gate", "moe_w_up", "moe_w_down"]
OUTPUTS = [(1, NP, D), (NB, NT, D), (1, 1, NP, H, DH), (1, NB, NT, H, DH), (1, 1, NP, H, DH), (1, NB, NT, H, DH),
           (1, 1, NP, H), (1, NB, NT, H), (1, 1, H, DH, DH), (1, NB, H, DH, DH), (1, 1, RW_IN), (1, NB, RW_IN),
           (1, 1, PBUF, D), (1, NB, PBUF, D)]


def kernel(**inputs):
    import concourse.bacc as bacc
    from concourse.bass_utils import run_bass_kernel_spmd

    nc = bacc.Bacc("TRN2", target_bir_lowering=False, num_devices=1)
    arrays, args = {}, {}
    for name in INPUTS + ["constants"]:
        x = constants() if name == "constants" else np.ascontiguousarray(inputs[name])
        arrays[f"in_{name}"] = x
        args[name] = nc.dram_tensor(f"in_{name}", x.shape, mybir.dt.from_np(x.dtype), kind="ExternalInput").ap()
    outs = [nc.dram_tensor(f"out_{i}", shape, F32, kind="ExternalOutput").ap() for i, shape in enumerate(OUTPUTS)]
    build_program(nc, args, *outs)
    r = run_bass_kernel_spmd(nc, [arrays], core_ids=[0])
    return tuple(r.results[0][f"out_{i}"] for i in range(len(OUTPUTS)))
```

```python
from contextlib import ExitStack

import numpy as np

import concourse.bass as bass
from concourse import mybir

F32 = mybir.dt.float32
I32 = mybir.dt.int32
U32 = mybir.dt.uint32
ALU = mybir.AluOpType
ACT = mybir.ActivationFunctionType
AX = mybir.AxisListType

P = 128
D = 1024
DC = D // P
NP, NB, NT = 256, 8, 4
NS = NB * NT
N = NP + NS
BLK = [(0, 128), (128, 128), (256, 32)]
H, DH = 8, 64
HW = H * DH
HC = HW // P
LORA, GLORA = 64, 128
FOX_IN = 3 * HW + H
RW_IN = 3 * HW + 2 * LORA + GLORA
IN_W = FOX_IN + RW_IN
PAGE, NPG, PAST = 128, 2, 256
FF = 2816
NE, FE = 8, 3584
CAP, HALF = 192, 64
MORE = (2 * N - 1) // CAP
ITEMS = NE + MORE
PBUF = 15
WINS = (2, 4, 8, 16)
RMS_EPS, GN_EPS, NEG = 1e-6, 64e-5, -1e30
DECAY = float(np.exp(-0.5))
L = 64
NCH = NP // L
LEVELS = 6

PIECES = ([(P * i, P) for i in range(HC)] + [(HW, LORA)] + [(HW + LORA + P * i, P) for i in range(HC)]
          + [(2 * HW + LORA + P * i, P) for i in range(HC)] + [(3 * HW + LORA, LORA), (3 * HW + 2 * LORA, GLORA)])
NPC = len(PIECES)
PR, PWL, PK, PV, PAL, PGL = 0, 4, 5, 9, 13, 14

CONST = {}
_at = 0
for _name, _n in [("ident", 128), ("before", 128), ("suffix0", 260), ("suffix1", 260),
                  ("causal", 256), ("pairs", 128), ("chunk", 128), ("levels", 64 * LEVELS), ("eyes", 64), ("fold", 9),
                  ("heads", 32), ("newmask", 4), ("seqmask", 16), ("headof", 8), ("tokenof", 16), ("turns", NE), ("iota", CAP + HALF), ("count", 64), ("reset", 256),
                  ("restart", 288)]:
    CONST[_name] = (_at, _n)
    _at += _n
NCONST = _at
CONST["ones"] = (CONST["suffix1"][0], P)


def constants():
    c = np.zeros((P, NCONST), np.float32)
    p = np.arange(P)[:, None]

    def put(name, a):
        at, n = CONST[name]
        c[:a.shape[0], at:at + n] = a.reshape(a.shape[0], n)

    j = np.arange(P)[None, :]
    put("ident", (p == j) * 1.0)
    put("before", (p < j) * 1.0)
    later, z = (p > j) * 1.0, np.zeros((P, 4))
    put("suffix0", np.concatenate([later, 0 * later, z], 1))
    put("suffix1", np.concatenate([np.ones((P, P)), later, z], 1))
    put("causal", np.concatenate([np.zeros((P, P)), np.where(j <= p, 0.0, NEG)], 1))
    put("pairs", (p // DH == j // DH) * 1.0)
    s, t = p % L, np.arange(2 * L)[None, :]
    put("chunk", np.where(t < L, s < t, s <= t - L) * 1.0)
    s, t = p % L, np.arange(L)[None, :]
    put("eyes", (s == t) * 1.0)
    put("levels", np.concatenate([((s // (2 * m) == t // (2 * m)) & (s // m % 2 == 0) & (t // m % 2 == 1)) * 1.0
                                  for m in (1 << i for i in range(LEVELS))], 1))
    put("fold", (p % 32 == np.arange(9)[None, :]) * 1.0)
    put("heads", (np.arange(H)[:, None] == np.arange(32)[None, :] // NT) * 1.0)
    put("newmask", np.where(np.arange(NT)[None, :] <= p % NT, 0.0, NEG))
    put("seqmask", (np.arange(16)[None, :] // 8 * 4 + p // 32 == np.arange(16)[None, :] % 8) * 1.0)
    r = np.arange(CAP + HALF)[None, :]
    put("headof", (p // NT % H == np.arange(H)[None, :]) * 1.0)
    put("turns", np.broadcast_to(np.array([0] + [i // 2 + (1 if i % 2 == 0 else NE // 2 + 1) for i in range(NE - 1)])[None], (P, NE)) * 1.0)
    put("tokenof", (p // 32 * NT + p % NT == np.arange(16)[None, :]) * 1.0)
    put("iota", np.broadcast_to(np.where(r < CAP, r, r - HALF), (P, CAP + HALF)) * 1.0)
    cnt = np.stack([1.0 / np.minimum(np.arange(16) + 1, w) for w in WINS])
    put("count", np.broadcast_to(cnt[None], (P, 4, 16)).copy())
    put("reset", np.broadcast_to((np.arange(NP) % L != 0)[None] * 1.0, (P, NP)).copy())
    t = np.arange(N)
    put("restart", np.broadcast_to(((t != 0) & ((t < NP) | (t % NT != 0)))[None] * 1.0, (P, N)).copy())
    return c


def weight_tiles():
    tiles = [("ada0", i) for i in range(4)]
    for i in range(8):
        tiles += [("win", i), ("ada0", 4 + i)]
    tiles += [("wout", i) for i in range(1, 3)]
    tiles += [("gate", 0), ("up", 0)]
    for i in range(6):
        tiles += [("gate", i + 1), ("up", i + 1)] if i < 5 else []
        tiles += [("ada1", 2 * i), ("ada1", 2 * i + 1), ("down", i)]
    return tiles


TILES = weight_tiles()
SLOTS, SLOT = 6, 4096
MIX_TILE = TILES.index(("wout", 1))
WOUT = [(0, 3 * P), (3 * P, 3 * P), (6 * P, 2 * P)]
FGRP = [(512 * i, min(512, FF - 512 * i)) for i in range(6)]
WIN = [
    (0, 512, [("f", i, P * i, P) for i in range(4)]),
    (512, 512, [("f", 4 + i, P * i, P) for i in range(4)]),
    (1024, 512, [("f", 8 + i, P * i, P) for i in range(4)]),
    (1536, 8, [("l", 0, 0, 8)]),
    (1544, 512, [("r", i, P * i, P) for i in range(4)]),
    (2056, 448, [("r", PWL, 0, 64)] + [("r", PK + i, 64 + P * i, P) for i in range(3)]),
    (2504, 512, [("r", PK + 3, 0, P)] + [("r", PV + i, P + P * i, P) for i in range(3)]),
    (3016, 320, [("r", PV + 3, 0, P), ("r", PAL, P, 64), ("r", PGL, 192, P)]),
]
WCHUNKS = [c for _, _, cs in WIN for c in cs]


class Banks:

    def __init__(self, tiles):
        self.tiles, self.n, self.owner, self.at = tiles, 0, [None] * len(tiles), {}

    def open(self, pe, name, freed):
        b = self.n % len(self.tiles)
        self.n += 1
        if self.owner[b] is not None:
            pe.wait_ge(*self.owner[b])
        self.owner[b] = freed
        self.at[name] = b
        return self.tiles[b]

    def __getitem__(self, name):
        return self.tiles[self.at[name]]


class Named:

    def __init__(self, nc, ctx):
        self.nc, self.ctx, self.made = nc, ctx, {}

    def __call__(self, name):
        if name not in self.made:
            self.made[name] = self.ctx.enter_context(self.nc.semaphore(name))
        return self.made[name]


ONCE = {
    "vector": ("vec_copied vec2_copied lf_abs lf_one logf_ready negF_ready k_ready q_ready last_ready "
              "kk_scaled rk_ready cum_ready psm_shifted psm_ready delta_ops packed "
              "final_state gn_centred mix_ready exts_zero z_ready z_used top_ready picked planned"),
    "scalar": ("siluc c_copied qk_squared lf_exp lf_ln qk_rooted wl_tanh gl_sigmoid kk_squared kk_rooted "
              "psm_exped so_copied fst_copied syt_copied gn_squared gn_rooted top_exped"),
    "tensor": ("c_turned vec_turned vec2_turned lf_turned last_turned so_mm fst_mm syt_mm route_mm "
              "rank_mm"),
    "gpsimd": ("vrow_zero silucT_zero last_zero rp_mixed zv_ready"),
}


class Once:

    def __init__(self, s):
        self.s, self.given = s, {e: 0 for e in ONCE}
        self.place = {name: (e, i + 1) for e, names in ONCE.items() for i, name in enumerate(names.split())}

    def __call__(self, name):
        engine, value = self.place[name]
        return self.s(f"{engine}_once"), value

    def give(self, name):
        engine, value = self.place[name]
        self.given[engine] += 1
        assert self.given[engine] == value, name
        return self.s(f"{engine}_once")


class Counted:

    def __init__(self, eng):
        self.eng, self.n = eng, {}

    def give(self, ins, sem):
        ins.then_inc(sem, 1)
        self.n[sem.name] = self.n.get(sem.name, 0) + 1

    def step(self, ins, sem):
        self.give(ins, sem)
        self.eng.wait_ge(sem, self.n[sem.name])


def spread(ap, axis, n):
    ap = ap.unsqueeze(axis)
    shape = list(ap.shape)
    shape[axis] = n
    return ap.to_broadcast(shape)


def flat(t):
    return t[:, :, :].rearrange("p a b -> p (a b)")


def own(a):
    return slice(DH * a, DH * (a + 1))


XJOBS = [(0, 0, 4), (0, 4, 4), (1, 0, 4), (1, 4, 4), (2, 0, 8)]


def kth(n, lv):
    return 2 * LEVELS * (n // 2) + 2 * lv + n % 2


def t_count(n, lv):
    per_pair = 2 * (2 * (LEVELS - 1) + 1)
    base = per_pair * (n // 2)
    return base + (4 * lv + 2 * (n % 2) + 2 if lv < LEVELS - 1 else 4 * lv + n % 2 + 1)


HALF_ONLY, FULL_ONLY, BOTH, NONE = range(4)
CACHE_STORES = 6 + 2 * NPC

VB_MU, VB_W0, VB_A0, VB_KK, VB_KA, VB_RK, VB_LNW, VB_LNB, VB_PS, VB_QG, VB_KG = 0, 15, 19, 23, 27, 31, 35, 39, 43, 51, 52
VA_ADA, VA_NORM = 0, (96, 112, 104, 120)



def t_mms(n, lv):
    per_pair = 2 * (2 * (LEVELS - 2) + 1)
    base = per_pair * (n // 2)
    return base + (4 * (lv - 1) + 2 * (n % 2) + 2 if lv < LEVELS - 1 else 4 * (lv - 1) + n % 2 + 1)


def build_program(nc, a, y_p, y_s, k_p, k_s, v_p, v_s, lf_p, lf_s, st_p, st_s, sh_p, sh_s, pool_p, pool_s):
    ctx = ExitStack()
    with ctx:
        def sb(name, shape, dt=F32):
            return ctx.enter_context(nc.sbuf_tensor(name, shape, dt))

        s = Named(nc, ctx)
        once = Once(s)

        def sums(name, which, n):
            return s(f"sums_{which}"), 3 * ("kks", "bon", "gnm", "gnv").index(name) + n

        def lora(name, which, n):
            return s(f"lora_{which}"), HC * ("dec", "icl", "gat").index(name) + n

        banks = Banks([ctx.enter_context(nc.psum_tensor(f"bank{i}", [P, 512], F32)) for i in range(8)])

        const = sb("const", [P, NCONST])

        def K(name, rows=P):
            at, n = CONST[name]
            return const[0:rows, at:at + n]

        ident = K("ident")
        xT = sb("xT", [P, DC, N])
        hT = sb("hT", [P, DC, N])
        tmpT = sb("tmpT", [P, DC, N])
        yT = sb("yT", [P, DC, N])
        modT = [sb(f"modT{i}", [P, 48, 9]) for i in range(2)]
        gainT = [sb(f"gainT{i}", [P, DC, 9]) for i in range(4)]
        silucT = sb("silucT", [P, DC, 32])
        vT = sb("vT", [P, 3, P])
        rstd = sb("rstd", [P, N])
        w2 = sb("w2", [LORA, HW])
        a2 = sb("a2", [LORA, HW])
        g2 = sb("g2", [GLORA, HW])
        fbias = sb("fbias", [H, 1])
        routerw = sb("routerw", [P, DC, NE])
        routerb = sb("routerb", [P, NE])
        pages = sb("pages", [1, NB * NPG], I32)
        ring = sb("ring", [P, SLOTS * SLOT])
        other = sb("other", [P, 12672])

        def slot(g):
            return ring[:, (g % SLOTS) * SLOT:(g % SLOTS + 1) * SLOT]

        class Region:
            def __init__(self, tensor, at=0):
                self.tensor, self.at = tensor, at

            def cut(self, *shape, rows=P):
                n = int(np.prod(shape))
                ap = self.tensor[0:rows, self.at:self.at + n]
                self.at += n
                names = "abcd"[:len(shape)]
                if len(shape) == 1:
                    return ap
                return ap.rearrange(f"p ({' '.join(names)}) -> p {' '.join(names)}",
                                    **dict(zip(names[1:], shape[1:])))

        vrow = Region(other, 12672 - 3 * P).cut(3, P)
        R = Region(other)
        rp = R.cut(NPC, N)
        diff = R.cut(NPC, N)
        fqkv = R.cut(3 * HC, N)
        pastlf4 = R.cut(NB, NPG, H * NT)
        D2 = Region(other, PGL * N)
        bonus = D2.cut(HC, N)
        lw = D2.cut(HC, N)
        icl = D2.cut(HC, N)
        gate = D2.cut(HC, N)
        R = Region(ring)
        X = Region(other)
        xrow = X.cut(3, D)
        crow = X.cut(D)
        scrow = X.cut(D)
        adap = [Region(flat(yT), HC * N).cut(2, 512)]
        R = Region(ring)
        ksamp = R.cut(2, NPG, HW)
        vsamp = R.cut(NB, NPG, HW)
        ktb = R.cut(2, HC, PAST + NT)
        qbd = R.cut(NB, HC, 32)
        pr = R.cut(2, 2, 256)
        prT = R.cut(2, 2, 2, P)
        psm = R.cut(2, PAST + NT)
        pnew = R.cut(2, NB, NT)
        psT = R.cut(2, 3, P)
        pastlf = R.cut(NB, NPG, H)
        logf = R.cut(N, rows=H)
        negF = R.cut(N, rows=H)
        lftmp = R.cut(2, N, rows=H)
        kvrow = R.cut(2, 3, HW)
        lfrow = R.cut(3, H)
        lastS = R.cut(NPC, NB)
        lastP = R.cut(NPC)
        lastrow = R.cut(2, P)
        ATT_END = R.at
        avm = ring[:, 0:2 * HW].rearrange("p (g f) -> p g f", g=2)
        wo_first = other[:, 0:DC * WOUT[0][1]]
        sst = R.cut(32, DH)
        sval = R.cut(NT, 32)
        ssa = R.cut(32)
        sy = R.cut(NT, 32)
        syrow = R.cut(HW, rows=NS)
        assert R.at <= SLOTS * SLOT, R.at
        R = Region(ring)
        kkT = yT[:, HC:2 * HC, :]
        bT = R.cut(HC, N)
        ar = R.cut(HC, NCH, 2, L)
        bk = R.cut(HC, NCH, 2, L)
        zv = R.cut(HC, NCH, 2, L)
        gt = R.cut(2, H, 2 * L)
        bkt = R.cut(2, H, DH)
        sav = R.cut(2, H, DH)
        su = R.cut(2, H, DH)
        lu = R.cut(NCH, H, L)
        assert R.at <= ATT_END, (R.at, ATT_END)
        Q = Region(other, 2 * NPC * N)
        tb = Q.cut(2, HC, L)
        assert Q.at <= 12672, Q.at
        Q = Region(flat(tmpT))
        wdec = Q.cut(HC, NP)
        winv = Q.cut(HC, NP)
        Q = Region(flat(hT))
        wprev = Q.cut(HC, NP)
        tt = Q.cut(2, HC, L)
        Q = Region(ring, R.at)
        xb = Q.cut(2, HC, L)
        nm = Q.cut(2, HC, L)
        ub = xb
        srow = Region(ring, Q.at).cut(6, HW, rows=NS)
        svec = Q.cut(NT, 6, DH)
        sprod = Q.cut(32, DH)
        assert Q.at <= ATT_END, (Q.at, ATT_END)

        def by_sequence(ap):
            return ap.rearrange("p c (b t) -> p c b t", t=NT)

        def of(t, a):
            return t.rearrange("p (c a) k -> p c a k", a=2)[:, :, a, :]

        small = sb("small", [P, 64])
        plan = sb("plan", [1, 2 * ITEMS + 1], I32)
        mix_stores = [0]

        R = Region(other)
        ffact = R.cut(2, 4, N)
        ffsilu = R.cut(2, N)
        prow = R.cut(D)
        poolw = R.cut(4, 2, 256)
        ext = R.cut(DC, 16 + NP)
        exts = R.cut(DC, NB, 20)
        hlast = R.cut(D)
        adap.append(R.cut(2, 512))
        assert R.at <= 12672, R.at
        R = Region(other)
        htok = R.cut(3, D)
        outrow = Region(other).cut(3, D)
        xe = R.cut(DC, CAP)
        sg = R.cut(2, 512)
        ea = R.cut(2, 512)
        eaT = R.cut(2, 4, CAP)
        ye = R.cut(D)
        yeh = R.cut(512)
        hot = R.cut(3, CAP)
        hotw = R.cut(3, CAP + HALF)
        gT = R.cut(2, N)
        pick = R.cut(3, NE)
        logit = R.cut(3, NE)
        comb = R.cut(3, ITEMS + 1)
        slot_at = R.cut(3, ITEMS + 1)
        later = R.cut(3, NE)
        top = R.cut(3, 8)
        topi = R.cut(3, 8)
        gate2 = R.cut(3, 4)
        wanted = R.cut(NE)
        ordinal = R.cut(NE)
        which = R.cut(MORE, NE)
        chosen = R.cut(3, NE, NE)
        gate_e = R.cut(3, NE)
        slot_e = R.cut(3, NE)
        heavier = R.cut(NE, NE)
        rank = R.cut(NE)
        turn_of = R.cut(NE, NE)
        load = R.cut(ITEMS)
        small_item = R.cut(ITEMS)
        planf = R.cut(2 * ITEMS + 1)
        assert R.at <= 12672, R.at

        def vector_rows():
            out = [(vrow[48 * l:48 * l + 48, 0, :], a["ada_b"][l].rearrange("(r p) -> r p", p=P)) for l in range(2)]
            for i, name in enumerate(("norm1_g", "norm2_g")):
                out.append((vrow[96 + 16 * i:112 + 16 * i, 0, :], a[name].rearrange("l (r p) -> (l r) p", p=P)))
            first, out = out, []
            for i, (at, w) in enumerate(PIECES):
                out.append((vrow[VB_MU + i:VB_MU + i + 1, 1, 0:w], a["rwkv_mu"][:, at:at + w]))
                out.append((vrow[NB * i:NB * i + NB, 2, 0:w], a["state_rwkv_shift"][0, :, at:at + w]))
            for name, row in (("rwkv_w0", VB_W0), ("rwkv_a0", VB_A0), ("rwkv_k_k", VB_KK), ("rwkv_k_a", VB_KA),
                              ("rwkv_ln_w", VB_LNW), ("rwkv_ln_b", VB_LNB)):
                out.append((vrow[row:row + HC, 1, :], a[name][0].rearrange("(r p) -> r p", p=P)))
            out.append((vrow[VB_RK:VB_RK + HC, 1, :], a["rwkv_r_k"][0].rearrange("(c a) k -> c (a k)", a=2)))
            out.append((vrow[VB_PS:VB_PS + DC, 1, :], a["pool_scale"][0].rearrange("(r p) -> r p", p=P)))
            for name, row in (("fox_q_gain", VB_QG), ("fox_k_gain", VB_KG)):
                for par in range(2):
                    out.append((vrow[row:row + 1, 1, DH * par:DH * (par + 1)], a[name]))
            return first, out

        cumv = winv

        def sample_operands():
            return [lw, kkT, bT, rp[:, PK:PK + HC, :], rp[:, PR:PR + HC, :], rp[:, PV:PV + HC, :]]

        scratch = nc.dram_tensor("sample_operands", [NB, NT, 6, H, DH], F32, kind="Internal").ap()
        scratch_y = nc.dram_tensor("sample_outputs", [NB, NT, 2 * H, 32], F32, kind="Internal").ap()

        def used(g):
            kind, i = TILES[g]
            if kind[:3] == "ada":
                return s("ada_mm"), 12 * int(kind[3]) + i + 1
            if kind == "win":
                return s("win_mm"), sum(len(c) for _, _, c in WIN[:i + 1])
            if kind == "wout":
                return s("wo_mm"), sum(WOUT[i]) // P
            if kind == "down":
                return s("down_mm"), DC * (i + 1)
            return s(f"{kind}_mm"), 4 * i + FGRP[i][1] // P

        def tile_source(g):
            kind, i = TILES[g]

            def cols(w, at, n):
                return (slot(g)[:, 0:DC * n].rearrange("p (c f) -> p c f", c=DC),
                        w.rearrange("(c p) f -> p c f", p=P)[:, :, at:at + n])

            if kind[:3] == "ada":
                return cols(a["ada_w"][int(kind[3])], 512 * i, 512)
            if kind == "win":
                return cols(a["w_in"][0], WIN[i][0], WIN[i][1])
            if kind == "wout":
                return cols(a["w_out"][0], *WOUT[i])
            at, n = FGRP[i]
            if kind == "down":
                return (slot(g)[:, 0:n // P * D].rearrange("p (c f) -> p c f", f=D),
                        a["ffn_w_down"][0, at:at + n, :].rearrange("(c p) f -> p c f", p=P))
            return cols(a[f"ffn_w_{kind}"][0], at, n)

        NT7 = FE // 512
        GRP = 3 * SLOT

        def moe_tile(it, t, kind):
            return ((it + t) % 2) * GRP + kind * SLOT

        PRIMED = {"pe": ("moe_down", "moe_turn", "comb_mm"), "act": ("moe_silu", "ye_act"),
                  "dve": ("moe_act", "ye_dve", "comb_added")}

        def after(name, n):
            assert any(name in names for names in PRIMED.values())
            return s(name), n + 1

        GATE, UP, GU, TURNH, TURN, YEH, YE = range(7)

        def moe_gather(pe, mm, k, prime=()):
            pe.wait_ge(s("hot_ready"), k + 1)
            for q in range(4):
                for c in range(2):
                    for blk, (_, w) in enumerate(BLK):
                        o = P * (2 * q + c)
                        last = mm(banks.tiles[q][:, CAP * c:CAP * (c + 1)], htok[0:w, blk, o:o + P], hot[0:w, blk, :],
                                  blk == 0, blk == 2)
                    if c == 0 and q < len(prime):
                        last.then_inc(s(prime[q]), 1)
                last.then_inc(s("gather_mm"), 1)

        def moe_tensor_item(pe, mm, it, odd, full, half):
            B = banks.tiles

            def hidden(t):
                n = NT7 * it + t
                pe.wait_ge(*after("moe_silu", n))
                pe.wait_ge(*after("moe_act", n))
                pe.wait_ge(s(f"moe_gu{t}"), 32 * it + 32)
                gate, up = moe_tile(odd, t, 0), moe_tile(odd, t, 1)
                if full:
                    for c in range(DC):
                        last = mm(B[GATE][:, :], xe[:, c, 0:P], ring[:, gate + 512 * c:gate + 512 * (c + 1)], c == 0, c == DC - 1)
                    last.then_inc(s("moe_gate"), 1)
                if half:
                    for c in range(DC):
                        last = mm(B[GU][0:HALF, :], xe[:, c, P:CAP], ring[:, gate + 512 * c:gate + 512 * (c + 1)], c == 0, c == DC - 1)
                        if c == DC - 1 and not full:
                            last.then_inc(s("moe_gate"), 1)
                        last = mm(B[GU][HALF:P, :], xe[:, c, P:CAP], ring[:, up + 512 * c:up + 512 * (c + 1)], c == 0, c == DC - 1)
                if full:
                    for c in range(DC):
                        last = mm(B[UP][:, :], xe[:, c, 0:P], ring[:, up + 512 * c:up + 512 * (c + 1)], c == 0, c == DC - 1)
                last.then_inc(s("moe_up"), 1)

            def turn(t):
                n = NT7 * it + t
                pe.wait_ge(*after("moe_act", n + 1))
                if t == 0:
                    pe.wait_ge(s("gT_ready"), it + 1)
                else:
                    pe.wait_ge(s("eaT_ready"), n)
                for j in range(4):
                    if full:
                        last = pe.transpose(B[TURN][:, P * j:P * (j + 1)], ea[:, 0, P * j:P * (j + 1)], ident)
                    if half:
                        last = mm(B[TURNH][:, HALF * j:HALF * (j + 1)], ea[HALF:P, 1, P * j:P * (j + 1)],
                                  ident[HALF:P, HALF:P], True, True)
                last.then_inc(s("moe_turn"), 1)

            def down(t):
                n = NT7 * it + t
                pe.wait_ge(s("eaT_ready"), n + 1)
                if t == 0:
                    pe.wait_ge(*after("ye_act", it))
                    pe.wait_ge(*after("ye_dve", it))
                    pe.wait_ge(*after("comb_added", DC * it))
                pe.wait_ge(s(f"moe_d{t}"), 16 * it + 16)
                at = moe_tile(odd, t, 2)
                for j in range(4):
                    start, stop = t == 0 and j == 0, t == NT7 - 1 and j == 3
                    for p in range(2):
                        w = ring[:, at + D * j + 512 * p:at + D * j + 512 * (p + 1)]
                        if full:
                            last = mm(B[YE + p][:, :], eaT[:, t % 2, j, 0:P], w, start, stop)
                    for p in range(2):
                        w = ring[:, at + D * j + 512 * p:at + D * j + 512 * (p + 1)]
                        if half:
                            last = mm(B[YEH][HALF * p:HALF * (p + 1), :], eaT[:, t % 2, j, P:CAP], w, start, stop)
                last.then_inc(s("moe_down"), 1)

            pe.wait_ge(s("xe_ready"), 4 * it + 4)
            hidden(0)
            pe.wait_ge(*after("comb_added", DC * it))
            for blk, (t0, w) in enumerate(BLK):
                if full:
                    last = pe.transpose(B[TURN][:, t0:t0 + w], hotw[0:w, blk, 0:P], ident[0:w, 0:w])
                if half:
                    last = pe.transpose(B[TURNH][:, t0:t0 + w], hotw[0:w, blk, P:2 * P], ident[0:w, 0:w])
            last.then_inc(s("g_mm"), 1)
            for t in range(1, NT7):
                hidden(t)
                turn(t - 1)
                down(t - 1)
            turn(NT7 - 1)
            pe.wait_ge(s("eaT_ready"), NT7 * it + NT7)
            moe_gather(pe, mm, it + 1)
            down(NT7 - 1)
            pe.wait_ge(*after("ye_act", it + 1))
            pe.wait_ge(*after("ye_dve", it + 1))
            for j in range(DC):
                if j >= 2:
                    pe.wait_ge(*after("comb_added", DC * it + j - 1))
                o = B[TURN + j % 2][:, 0:N]
                if full:
                    last = mm(o, ye[:, P * j:P * (j + 1)], gT[:, 0, :], True, not half)
                if half:
                    p = HALF * (j // 4)
                    last = mm(o, yeh[p:p + HALF, P * (j % 4):P * (j % 4 + 1)], gT[p:p + HALF, 1, :], not full, True)
                last.then_inc(s("comb_mm"), 1)

        def moe_scalar_item(act, it, full, half):
            B = banks.tiles

            def turned(t):
                n = NT7 * it + t
                act.wait_ge(*after("moe_turn", n + 1))
                act.wait_ge(*after("moe_down", n if t == 0 else n - 1))
                if full:
                    last = act.activation(eaT[:, t % 2, :, 0:P], B[TURN][:, :].rearrange("p (j q) -> p j q", j=4), ACT.Copy)
                if half:
                    last = act.activation(eaT[:, t % 2, :, P:CAP],
                                          B[TURNH][:, 0:4 * HALF].rearrange("p (j q) -> p j q", j=4), ACT.Copy)
                last.then_inc(s("eaT_ready"), 1)

            for t in range(NT7):
                n = NT7 * it + t
                act.wait_ge(s("moe_gate"), n + 1)
                act.wait_ge(*after("moe_act", n))
                if full:
                    last = act.activation(sg[:, 0, :], B[GATE][:, :], ACT.Silu)
                if half:
                    if full:
                        act.wait_ge(s("moe_up"), n + 1)
                    last = act.activation(sg[HALF:P, 1, :], B[GU][0:HALF, :], ACT.Silu)
                last.then_inc(s("moe_silu"), 1)
                if t:
                    turned(t - 1)
            turned(NT7 - 1)
            moe_gathered(act, it + 1)
            act.wait_ge(*after("moe_down", NT7 * it + NT7))
            act.wait_ge(*after("comb_mm", DC * it))
            if full:
                last = act.activation(ye[:, 0:512], B[YE][:, :], ACT.Copy)
            if half:
                last = act.activation(yeh, B[YEH][:, :], ACT.Copy)
            last.then_inc(s("ye_act"), 1)

        def moe_gathered(act, k):
            for q in range(4):
                act.wait_ge(s("gather_mm"), 4 * k + q + 1)
                act.activation(xe[:, 2 * q:2 * q + 2, :].rearrange("p c s -> p (c s)"), banks.tiles[q][:, 0:2 * CAP], ACT.Copy)\
                    .then_inc(s("xe_ready"), 1)

        def moe_hot(dve, it):
            for blk, (_, w) in enumerate(BLK):
                at = slot_at[0:w, blk, bass.ds(it, 1)]
                dve.tensor_scalar(hot[0:w, blk, :], K("iota")[0:w, 0:CAP], at, None, ALU.is_equal)
                last = dve.tensor_scalar(hotw[0:w, blk, :], K("iota")[0:w, :], at, comb[0:w, blk, bass.ds(it, 1)],
                                         ALU.is_equal, ALU.mult)
            last.then_inc(s("hot_ready"), 1)

        def moe_vector_item(dve, it, full, half):
            B = banks.tiles
            for t in range(NT7):
                n = NT7 * it + t
                dve.wait_ge(*after("moe_silu", n + 1))
                dve.wait_ge(s("moe_up"), n + 1)
                dve.wait_ge(*after("moe_turn", n))
                if full:
                    last = dve.tensor_tensor(ea[:, 0, :], sg[:, 0, :], B[UP][:, :], ALU.mult)
                if half:
                    last = dve.tensor_tensor(ea[HALF:P, 1, :], sg[HALF:P, 1, :], B[GU][HALF:P, :], ALU.mult)
                last.then_inc(s("moe_act"), 1)
                if t == 0:
                    dve.wait_ge(s("g_mm"), it + 1)
                    dve.wait_ge(*after("comb_mm", DC * it))
                    if full:
                        last = dve.tensor_copy(gT[:, 0, :], B[TURN][:, 0:N])
                    if half:
                        last = dve.tensor_copy(gT[:, 1, :], B[TURNH][:, 0:N])
                    last.then_inc(s("gT_ready"), 1)
                if t == 1:
                    moe_hot(dve, it + 1)
            dve.wait_ge(*after("moe_down", NT7 * it + NT7))
            if full:
                dve.tensor_copy(ye[:, 512:1024], B[YE + 1][:, :]).then_inc(s("ye_dve"), 1)
            else:
                dve.memset(small[:, 61:62], 0.0).then_inc(s("ye_dve"), 1)
            dve.wait_ge(*after("comb_added", DC * it))
            for j in range(DC):
                dve.wait_ge(*after("comb_mm", DC * it + j + 1))
                dve.tensor_tensor(yT[:, j, :], yT[:, j, :], B[TURN + j % 2][:, 0:N], ALU.add).then_inc(s("comb_added"), 1)

        def moe_sync_item(sp, it, e, first=False):
            wg, wu, wd = (a[f"moe_w_{k}"][0, bass.ds(e, 1)] for k in ("gate", "up", "down"))
            order = [(t, kind) for t in range(NT7) for kind in (0, 1)]
            for t in range(NT7):
                order.insert(3 * t + 4 if t < NT7 - 1 else len(order), (t, 2))
            for t, kind in order:
                w = (wg, wu, wd)[kind]
                n = NT7 * it + t
                if first and t < 2:
                    sp.wait_ge(*used(max(g for g in range(len(TILES)) if g % SLOTS == 3 * t + kind)))
                elif kind == 0:
                    sp.wait_ge(s("moe_up"), n - 1)
                elif kind == 2:
                    sp.wait_ge(*after("moe_down", n - 1))
                dst = ring[:, bass.ds(moe_tile(it, t, kind), SLOT)]
                if kind < 2:
                    sp.dma_start(dst.rearrange("p (c f) -> p c f", c=DC),
                                 w.rearrange("o (c p) f -> p (o c) f", p=P)[:, :, 512 * t:512 * (t + 1)])\
                        .then_inc(s(f"moe_gu{t}"), 16)
                else:
                    sp.dma_start(dst.rearrange("p (c f) -> p c f", c=4),
                                 w.rearrange("o f d -> (o f) d")[512 * t:512 * (t + 1), :].rearrange("(c p) d -> p c d", p=P))\
                        .then_inc(s(f"moe_d{t}"), 16)

        def items(engine, step):
            engine.wait_ge(*once("planned"))
            with engine.Fori(0, ITEMS // 2) as pair:
                for odd in range(2):
                    it = 2 * pair + odd
                    kind = engine.value_load(plan[0:1, bass.ds(it, 1)], min_val=0, max_val=NONE)
                    with engine.If(kind == HALF_ONLY):
                        step(it, odd, False, True)
                    with engine.If(kind == FULL_ONLY):
                        step(it, odd, True, False)
                    with engine.If(kind == BOTH):
                        step(it, odd, True, True)

        def moe_tensor(pe, mm):
            pe.wait_ge(s("ranked"), 3)
            pe.wait_ge(s("htok_ready"), 6)
            moe_gather(pe, mm, 0, PRIMED["pe"])
            items(pe, lambda *item: moe_tensor_item(pe, mm, *item))

        def moe_scalar(act):
            for i, name in enumerate(PRIMED["act"]):
                act.activation(small[:, 44 + i:45 + i], ident[:, 0:1], ACT.Copy).then_inc(s(name), 1)
            moe_gathered(act, 0)
            items(act, lambda it, odd, full, half: moe_scalar_item(act, it, full, half))

        def moe_plan(dve, do):
            counts = small[:, 48:48 + NE]
            TS, TT, STT = dve.tensor_scalar, dve.tensor_tensor, dve.scalar_tensor_tensor
            number = K("iota")[:, 0:NE]

            def chosen_by(choice, n, src, dst):
                v = chosen[:, :, 0:n, :]
                do(TT(v, spread(src, 2, n), spread(choice, 1, 3), ALU.mult))
                do(dve.tensor_reduce(dst, v, AX.X, ALU.add))

            def one_chosen(choice, n, src, dst):
                v = chosen[:, 0, 0:n, :]
                do(TT(v, choice, spread(src, 1, n), ALU.mult))
                do(dve.tensor_reduce(dst, v, AX.X, ALU.add))

            do(STT(rank, number, -1.0 / 16, counts, ALU.mult, ALU.add))
            do(dve.memset(rank[:, 0:1], 2.0 * N))
            do(TT(heavier, spread(rank, 1, NE), spread(rank, 2, NE), ALU.is_gt))
            do(dve.tensor_reduce(rank, heavier, AX.X, ALU.add))
            do(TT(turn_of, spread(rank, 1, NE), spread(K("turns"), 2, NE), ALU.is_equal))
            chosen_by(turn_of, NE, slot_e, slot_at[:, :, 0:NE])
            chosen_by(turn_of, NE, gate_e, comb[:, :, 0:NE])
            one_chosen(turn_of, NE, number, planf[:, ITEMS:ITEMS + NE])
            do(TS(wanted, counts, float(CAP), None, ALU.is_gt))
            do(dve.tensor_tensor_scan(ordinal, K("ones")[:, 0:NE], wanted, 0.0, ALU.mult, ALU.add))
            for r in range(MORE):
                do(STT(which[:, r, :], ordinal, float(r + 1), wanted, ALU.is_equal, ALU.mult))
            chosen_by(which, MORE, later, slot_at[:, :, NE:ITEMS])
            chosen_by(which, MORE, gate_e, comb[:, :, NE:ITEMS])
            one_chosen(which, MORE, number, planf[:, ITEMS + NE:2 * ITEMS])
            do(TS(wanted, counts, float(CAP), None, ALU.min))
            one_chosen(turn_of, NE, wanted, load[:, 0:NE])
            do(TS(wanted, counts, -float(CAP), None, ALU.add))
            one_chosen(which, MORE, wanted, load[:, NE:ITEMS])
            do(TS(small_item, load, float(HALF), None, ALU.is_le))
            do(dve.scalar_tensor_tensor(slot_at[:, :, 0:ITEMS], spread(small_item, 1, 3), float(P), slot_at[:, :, 0:ITEMS],
                                        ALU.mult, ALU.add))
            do(TS(planf[:, 0:ITEMS], load, float(P), None, ALU.is_gt))
            do(TT(planf[:, 0:ITEMS], planf[:, 0:ITEMS], small_item, ALU.subtract))
            do(TS(planf[:, 0:ITEMS], planf[:, 0:ITEMS], 1.0, None, ALU.add))
            do(TS(small_item[:, NE:ITEMS], load[:, NE:ITEMS], 0.0, float(NONE), ALU.is_equal, ALU.mult))
            do(TT(planf[:, NE:ITEMS], planf[:, NE:ITEMS], small_item[:, NE:ITEMS], ALU.add))
            do(TS(planf[:, 2 * ITEMS:], ordinal[:, NE - 1:NE], float(NE), None, ALU.add))
            do(dve.tensor_copy(plan[:, :], planf[0:1, :]), once.give("planned"))

        def moe_vector(dve, do):
            moe_plan(dve, do)
            for i, name in enumerate(PRIMED["dve"]):
                dve.memset(small[:, 32 + i:33 + i], 0.0).then_inc(s(name), 1)
            moe_hot(dve, 0)
            items(dve, lambda it, odd, full, half: moe_vector_item(dve, it, full, half))
            return dve.value_load(plan[0:1, 2 * ITEMS:2 * ITEMS + 1], min_val=NE, max_val=ITEMS)

        def moe_sync(sp):
            moe_sync_item(sp, 0, 0, first=True)
            sp.wait_ge(*once("planned"))
            with sp.Fori(1, ITEMS) as it:
                kind = sp.value_load(plan[0:1, bass.ds(it, 1)], min_val=0, max_val=NONE)
                with sp.If(kind < NONE):
                    e = sp.value_load(plan[0:1, bass.ds(it + ITEMS, 1)], min_val=0, max_val=NE - 1)
                    moe_sync_item(sp, it, e)

        block = ctx.enter_context(nc.Block())

        @block.tensor
        def _(pe):
            def mm(out, lhsT, rhs, start, stop):
                return pe.matmul(out, lhsT, rhs, start=start, stop=stop, skip_group_check=True)

            pe.wait_ge(s("const_loaded"), 16)
            pe.wait_ge(*once("siluc"))
            b = banks.open(pe, "c", once("c_copied"))
            for c in range(DC):
                last = pe.transpose(b[:, 9 * c:9 * c + 9], scrow[0:9, P * c:P * (c + 1)], ident[0:9, 0:9])
            last.then_inc(once.give("c_turned"), 1)
            pe.wait_ge(s("x_loaded"), 48)
            for n, (blk, c0, nc_) in enumerate(XJOBS):
                w = BLK[blk][1]
                b = banks.open(pe, f"x{n}", (s("x_copied"), n + 1))
                for c in range(nc_):
                    last = pe.transpose(b[:, w * c:w * (c + 1)], xrow[0:w, blk, P * (c0 + c):P * (c0 + c + 1)],
                                        ident[0:w, 0:w])
                last.then_inc(s("x_turned"), 1)

            def mean_square(i):
                b = banks.open(pe, f"ms{i}", (s("ms_read"), i + 1))
                for c in range(DC):
                    pe.wait_ge(s("squared"), DC * i + c + 1)
                    last = mm(b[:, 0:N], K("ones"), tmpT[:, c, :], c == 0, c == DC - 1)
                last.then_inc(s("ms_ready"), 1)

            mean_square(0)

            def tile(g):
                pe.wait_ge(s(f"slot{g % SLOTS}"), 16 * (g // SLOTS + 1))
                return slot(g)

            def ada(layer, i):
                w = tile(TILES.index((f"ada{layer}", i))).rearrange("p (c f) -> p c f", c=DC)
                b = banks.open(pe, f"ada{layer}_{i}", (s("ada_copied"), 12 * layer + i + 1))
                for c in range(DC):
                    last = mm(b[32 * (c % 4):32 * (c % 4) + 32, :], silucT[:, c, :], w[:, c, :], c < 4, c >= 4)
                last.then_inc(s("ada_mm"), 1)

            def fold(layer, i):
                k = 12 * layer + i
                b = banks.open(pe, f"fold{layer}_{i}", (s("mod_ready"), k + 1))
                pe.wait_ge(s("ada_copied"), k + 1)
                for j in range(4):
                    last = mm(b[:, 9 * j:9 * j + 9], adap[layer][:, k % 2, P * j:P * (j + 1)], K("fold"), True, True)
                last.then_inc(s("folded"), 1)

            pe.wait_ge(*once("c_copied"))
            ada(0, 0)
            first, others = vector_rows()
            pe.wait_ge(s("vec_loaded"), 16 * len(first))
            b = banks.open(pe, "vec", once("vec_copied"))
            pe.transpose(b[:, 0:P], vrow[:, 0, :], ident).then_inc(once.give("vec_turned"), 1)
            for i in range(1, 4):
                ada(0, i)
                fold(0, i - 1)
            fold(0, 3)

            n = 0
            for i, (_, wd, chunks) in enumerate(WIN):
                w = tile(TILES.index(("win", i)))[:, 0:DC * wd].rearrange("p (c f) -> p c f", c=DC)
                for kind, idx, off, m in chunks:
                    b = banks.open(pe, f"win{n}", (s("win_act" if n % 2 else "win_dve"), n // 2 + 1))
                    for c in range(DC):
                        if n == 0:
                            pe.wait_ge(s("h_ready"), c + 1)
                        last = mm(b[0:m, 0:N], w[:, c, off:off + m], hT[:, c, :], c == 0, c == DC - 1)
                    last.then_inc(s("win_mm"), 1)
                    n += 1
                if i == 2:
                    pe.wait_ge(s("vec2_loaded"), 16 * len(others))
                    b = banks.open(pe, "vec2", once("vec2_copied"))
                    for k in range(2):
                        last = pe.transpose(b[:, P * k:P * (k + 1)], vrow[:, 1 + k, :], ident)
                    last.then_inc(once.give("vec2_turned"), 1)
                if i:
                    fold(0, 3 + i)
                ada(0, 4 + i)
            fold(0, 11)

            pe.wait_ge(*once("qk_squared"))
            for i in range(6):
                b = banks.open(pe, f"qkms{i}", (s("qkms_read"), i + 1))
                mm(b[:, 0:384], K("pairs"), flat(tmpT)[:, 384 * i:384 * (i + 1)], True, True).then_inc(s("qkms"), 1)
            pe.wait_ge(*once("k_ready"))
            for n in range(6):
                which, blk = n // 3, n % 3
                t0, w = BLK[blk]
                b = banks.open(pe, f"kv{n}", (s("kv_copied"), n + 1))
                for c in range(HC):
                    last = pe.transpose(b[0:w, P * c:P * (c + 1)], fqkv[:, HC * (1 + which) + c, t0:t0 + w], ident)
                last.then_inc(s("kv_turned"), 1)
            pe.wait_ge(*once("logf_ready"))
            b = banks.open(pe, "lf", (s("lf_copied"), 3))
            for blk, (t0, w) in enumerate(BLK):
                last = pe.transpose(b[0:w, H * blk:H * (blk + 1)], logf[:, t0:t0 + w], ident[0:H, 0:H])
            last.then_inc(once.give("lf_turned"), 1)
            pe.wait_ge(*once("last_ready"))
            b = banks.open(pe, "last", (s("last_copied"), 2))
            pe.transpose(b[0:NPC * 8, 0:P], lastS.rearrange("p a b -> p (a b)"), ident)
            pe.transpose(b[0:NPC, P:2 * P], lastP, ident).then_inc(once.give("last_turned"), 1)

            def scores(c, qb):
                nk = P * (qb + 1)
                for par in range(2):
                    p0 = DH * par
                    b = banks.open(pe, f"s{c}{qb}{par}", (s("scored"), 4 * c + 2 * qb + par + 1))
                    mm(b[:, 0:nk], fqkv[p0:p0 + DH, c, P * qb:P * (qb + 1)], fqkv[p0:p0 + DH, HC + c, 0:nk], True, False)
                    h = 2 * c + par
                    mm(b[:, 0:nk], ident[0:H, h:h + 1].to_broadcast([H, P]), negF[0:H, 0:nk], False, True)\
                        .then_inc(s("s_mm"), 1)

            def turn_probs(c, qb):
                k = 2 * c + qb
                pe.wait_ge(s("probs"), k + 1)
                b = banks.open(pe, f"pt{c}{qb}", (s("probsT"), k + 1))
                for par in range(2):
                    for j in range(qb + 1):
                        o = P * ((qb + 1) * par + j)
                        last = pe.transpose(b[:, o:o + P], pr[:, k % 2, par, P * j:P * (j + 1)], ident)
                last.then_inc(s("pt_mm"), 1)

            def attend(c, qb):
                k = 2 * c + qb
                pe.wait_ge(s("probsT"), k + 1)
                b = banks.open(pe, f"o{c}{qb}", (s("o_copied"), k + 1))
                for par in range(2):
                    h = 2 * c + par
                    for j in range(qb + 1):
                        last = mm(b[DH * par:DH * par + DH, 0:P], kvrow[:, 1, j, DH * h:DH * (h + 1)],
                                  prT[:, k % 2, par, j, :], j == 0, j == qb)
                last.then_inc(s("o_mm"), 1)

            pe.wait_ge(*once("q_ready"))
            pe.wait_ge(*once("negF_ready"))
            pe.wait_ge(s("kv_copied"), 6)
            tasks = [(c, qb) for c in range(HC) for qb in range(2)]
            scores(*tasks[0])
            scores(*tasks[1])
            for k, t in enumerate(tasks):
                if k + 2 < len(tasks):
                    scores(*tasks[k + 2])
                turn_probs(*t)
                attend(*t)

            def lowrank(name, weights, src, need):
                pe.wait_ge(*once(need))
                for c in range(HC):
                    b = banks.open(pe, f"{name}{c}", lora(name, "ready", c + 1))
                    mm(b[:, 0:N], weights[:, P * c:P * (c + 1)], src, True, True).then_inc(s("lora_mm"), 1)

            lowrank("dec", w2[:, :], rp[0:LORA, PWL, :], "wl_tanh")
            lowrank("icl", a2[:, :], rp[0:LORA, PAL, :], "rp_mixed")
            lowrank("gat", g2[:, :], rp[:, PGL, :], "gl_sigmoid")

            def head_sums(name, src, n=3):
                for i in range(n):
                    b = banks.open(pe, f"{name}{i}", sums(name, "read", i + 1))
                    mm(b[:, 0:384], K("pairs"), src[:, 384 * i:384 * (i + 1)], True, True).then_inc(s("sums_mm"), 1)

            pe.wait_ge(*once("kk_squared"))
            head_sums("kks", flat(tmpT)[:, 0:HC * N])
            def past_keys(q):
                pe.wait_ge(s(f"k_page{q % 2}"), 64 * (q // 2 + 1))
                for half in range(2):
                    b = banks.open(pe, f"kt{q}{half}", (s("kt_copied"), 3 * q + half + 1))
                    for cc in range(2):
                        for j in range(NPG):
                            o = 256 * cc + P * j
                            last = pe.transpose(b[:, o:o + P], ksamp[:, q % 2, j, P * (2 * half + cc):P * (2 * half + cc + 1)], ident)
                    last.then_inc(s("kt_mm"), 1)

            past_keys(0)
            pe.wait_ge(s("qbd_ready"), 2 * HC)
            for q in range(NB):
                if q < NB - 1:
                    past_keys(q + 1)
                pe.wait_ge(s("kt_copied"), 3 * q + 3)
                b = banks.open(pe, f"ss{q}", (s("ss_copied"), q + 1))
                o = b[0:32, 0:PAST + NT]
                for c in range(HC):
                    mm(o, qbd[:, q, c, :], ktb[:, q % 2, c, :], c == 0, False)
                pe.wait_ge(s("lf_spread"), q + 1)
                for j in range(NPG):
                    mm(o, pastlf4[:, q, j, :], K(f"suffix{j}"), False, False)
                mm(b[0:32, PAST:PAST + NT], K("heads", H), negF[0:H, NP + NT * q:NP + NT * (q + 1)],
                   False, True).then_inc(s("ss_mm"), 1)
                if q == 2:
                    pe.wait_ge(*once("rk_ready"))
                    head_sums("bon", flat(tmpT)[:, HC * N:2 * HC * N])
            pe.wait_ge(*once("psm_ready"))
            for g in range(2):
                b = banks.open(pe, f"pst{g}", (s("psT_ready"), 2 * g + 2))
                for j in range(NPG):
                    pe.transpose(b[:, P * j:P * (j + 1)], psm[:, g, P * j:P * (j + 1)], ident)
                last = pe.transpose(b[0:32, 2 * P:3 * P], pnew[:, g, :, :].rearrange("p a b -> p (a b)"), ident)
                last.then_inc(s("pst_mm"), 1)
            pe.wait_ge(s("psT_ready"), 4)
            pe.wait_ge(s("v_pages"), 32 * NB)
            for g in range(2):
                b = banks.open(pe, f"av{g}", (s("av_masked"), g + 1))
                mm(b[:, :], psT[0:32, g, 2, :], kvrow[0:NS, 1, 2, :], True, False)
                for j in range(NPG):
                    for q in range(4):
                        last = mm(b[32 * q:32 * q + 32, :], psT[:, g, j, 32 * q:32 * q + 32], vsamp[:, 4 * g + q, j, :],
                                  False, j == NPG - 1)
                last.then_inc(s("av_mm"), 1)
            b = banks.open(pe, "so", once("so_copied"))
            so = b[:, 0:HC * NS].rearrange("p (c t) -> p c t", c=HC)
            for g in range(2):
                pe.wait_ge(s("av_masked"), g + 1)
                for c in range(HC):
                    last = mm(so[:, c, 16 * g:16 * g + 16], avm[:, g, P * c:P * (c + 1)], K("tokenof"), True, True)
            last.then_inc(once.give("so_mm"), 1)

            pe.wait_ge(*once("delta_ops"))
            for i, src in enumerate(sample_operands()):
                b = banks.open(pe, f"sr{i}", (s("srow_copied"), i + 1))
                for c in range(HC):
                    last = pe.transpose(b[0:NS, P * c:P * (c + 1)], src[:, c, NP:N], ident)
                last.then_inc(s("sr_mm"), 1)

            pe.wait_ge(*once("packed"))

            def products(n):
                for par in range(2):
                    b = banks.open(pe, f"gt{n}{par}", (s("gt_ready"), 2 * n + par + 1))
                    for c in range(HC):
                        last = mm(b[:, P * c:P * (c + 1)], bk[DH * par:DH * par + DH, c, n].rearrange("p a t -> p (a t)"),
                                  ar[DH * par:DH * par + DH, c, n].rearrange("p a t -> p (a t)"), True, True)
                    last.then_inc(s("gt_mm"), 1)
                pe.wait_ge(*once("zv_ready"))
                for src, nm_ in ((bk, "bkt"), (zv, "vt")):
                    b = banks.open(pe, f"{nm_}{n}", (s(f"{nm_}_ready"), n + 1))
                    for c in range(HC):
                        last = pe.transpose(b[:, P * c:P * (c + 1)], src[:, c, n].rearrange("p a t -> p (a t)"), ident)
                    last.then_inc(s(f"{nm_}_mm"), 1)

            def invert(pair):
                for lv in range(LEVELS):
                    for i in range(2):
                        n = 2 * pair + i
                        k = LEVELS * n + lv
                        pe.wait_ge(s("nm_ready"), kth(n, lv) + 1)
                        if lv:
                            pe.wait_ge(s("t_ready"), t_count(n, lv - 1))
                        b = banks.open(pe, f"x_{k}", (s("xb_ready"), kth(n, lv) + 1))
                        for h in range(H):
                            c, o = h // 2, own(h % 2)
                            rhs = K("eyes")[o] if lv == 0 else tb[o, i, c, :]
                            last = mm(b[o, L * c:L * (c + 1)], nm[o, i, c, :], rhs, True, True)
                        last.then_inc(s("x_mm"), 1)
                    for i in range(2):
                        n = 2 * pair + i
                        if lv == 0:
                            continue
                        pe.wait_ge(s("xb_ready"), kth(n, lv) + 1)
                        if lv < LEVELS - 1:
                            b = banks.open(pe, f"t_{n}{lv}", (s("t_ready"), t_count(n, lv) - 1))
                            for h in range(H):
                                c, o = h // 2, own(h % 2)
                                last = mm(b[o, L * c:L * (c + 1)], tt[o, i, c, :], xb[o, i, c, :], True, True)
                            last.then_inc(s("t_mm"), 1)
                        b = banks.open(pe, f"tt_{n}{lv}", (s("t_ready"), t_count(n, lv)))
                        for h in range(H):
                            c, o = h // 2, own(h % 2)
                            last = mm(b[o, L * c:L * (c + 1)], xb[o, i, c, :], tt[o, i, c, :], True, True)
                        last.then_inc(s("t_mm"), 1)

            def advance(n):
                i = n % 2
                pe.wait_ge(s("su_ready"), n + 1)
                pe.wait_ge(s("lu_ready"), n + 1)
                pe.wait_ge(s("lu_own"), H)
                pe.wait_ge(s("vt_ready"), n + 1)
                b = banks.open(pe, f"u{n}", (s("u_ready"), n + 1))
                for h in range(H):
                    c, o = h // 2, own(h % 2)
                    last = mm(b[o, DH * c:DH * (c + 1)], lu[:, n, h, :], su[:, i, h, :], True, True)
                last.then_inc(s("u_mm"), 1)
                pe.wait_ge(s("u_ready"), n + 1)
                pe.wait_ge(s("t_ready"), t_count(n, LEVELS - 1))
                b = banks.open(pe, f"sa{n}", (s("sa_ready"), n + 1))
                for h in range(H):
                    c, o = h // 2, own(h % 2)
                    last = mm(b[o, DH * c:DH * (c + 1)], tt[o, i, c, :], ub[o, i, c, :], True, True)
                last.then_inc(s("sa_mm"), 1)
                pe.wait_ge(s("sa_ready"), n + 1)
                pe.wait_ge(s("bkt_ready"), n + 1)
                b = banks.open(pe, f"st{n}", (s("state_read"), n + 1))
                for h in range(H):
                    c, o = h // 2, own(h % 2)
                    last = mm(b[o, DH * c:DH * (c + 1)], bkt[:, i, h, :], sav[:, i, h, :], True, True)
                last.then_inc(s("st_mm"), 1)
                b = banks.open(pe, f"y{n}", (s("yc_copied"), n + 1))
                for h in range(H):
                    c, o = h // 2, own(h % 2)
                    y = b[o, L * c:L * (c + 1)]
                    mm(y, su[o, i, h, :], ar[o, c, n, 1, :], True, False)
                    last = mm(y, sav[:, i, h, :], gt[:, i, h, L:2 * L], False, True)
                last.then_inc(s("y_mm"), 1)

            for pair in range(NCH // 2):
                products(2 * pair)
                products(2 * pair + 1)
                invert(pair)
                advance(2 * pair)
                advance(2 * pair + 1)
            pe.wait_ge(*once("final_state"))
            b = banks.open(pe, "fst", once("fst_copied"))
            for h in range(H):
                c, o = h // 2, own(h % 2)
                last = mm(b[o, DH * c:DH * (c + 1)], su[o, 0, h, :], K("eyes")[o], True, True)
            last.then_inc(once.give("fst_mm"), 1)
            pe.wait_ge(s("syrow_loaded"), 16)
            b = banks.open(pe, "syt", once("syt_copied"))
            for c in range(HC):
                last = pe.transpose(b[:, NS * c:NS * (c + 1)], syrow[:, P * c:P * (c + 1)], ident[0:NS, 0:NS])
            last.then_inc(once.give("syt_mm"), 1)
            pe.wait_ge(*once("syt_copied"))
            pe.wait_ge(s("yc_copied"), NCH)
            head_sums("gnm", flat(yT)[:, HC * N:2 * HC * N])
            pe.wait_ge(*once("gn_squared"))
            head_sums("gnv", flat(tmpT)[:, 0:HC * N])

            pe.wait_ge(*once("mix_ready"))
            pe.wait_ge(s("o_copied"), 2 * HC)
            pe.wait_ge(*once("so_copied"))
            pe.wait_ge(s("wo_first"), 16)
            for i, (at, wd) in enumerate(WOUT):
                w = (tile(MIX_TILE + i - 1) if i else wo_first)[:, 0:DC * wd].rearrange("p (c f) -> p c f", c=DC)
                for j in range(at // P, (at + wd) // P):
                    b = banks.open(pe, f"wo{j}", (s("res1"), j + 1))
                    for c in range(DC):
                        last = mm(b[:, 0:N], w[:, c, P * j - at:P * (j + 1) - at], yT[:, c, :], c == 0, c == DC - 1)
                    last.then_inc(s("wo_mm"), 1)
            mean_square(1)


            def hidden(i):
                nf = FGRP[i][1]
                for j in range(nf // P):
                    for kind in ("gate", "up"):
                        w = tile(TILES.index((kind, i)))[:, 0:DC * nf].rearrange("p (c f) -> p c f", c=DC)
                        n = 4 * i + j
                        b = banks.open(pe, f"{kind}{n}", (s("act_ready"), n + 1))
                        for c in range(DC):
                            if i + j == 0 and kind == "gate":
                                pe.wait_ge(s("h_ready"), DC + c + 1)
                            last = mm(b[:, 0:N], w[:, c, P * j:P * (j + 1)], hT[:, c, :], c == 0, c == DC - 1)
                        last.then_inc(s(f"{kind}_mm"), 1)

            def down(i):
                nf = FGRP[i][1]
                w = tile(TILES.index(("down", i)))[:, 0:nf // P * D].rearrange("p (c f) -> p c f", f=D)
                pe.wait_ge(s("act_ready"), FGRP[i][0] // P + nf // P)
                for j in range(DC):
                    b = banks.open(pe, f"down{i}_{j}", (s("ff_added"), DC * i + j + 1))
                    for c in range(nf // P):
                        last = mm(b[:, 0:N], w[:, c, P * j:P * (j + 1)], ffact[:, i % 2, c, :], c == 0, c == nf // P - 1)
                    last.then_inc(s("down_mm"), 1)

            hidden(0)
            for i in range(6):
                if i < 5:
                    hidden(i + 1)
                ada(1, 2 * i)
                ada(1, 2 * i + 1)
                down(i)
                fold(1, 2 * i)
                fold(1, 2 * i + 1)

            mean_square(2)
            pe.wait_ge(s("pool_rows"), 16)
            b = banks.open(pe, "pb0", (s("pbuf_copied"), 1))
            for c in range(4):
                last = pe.transpose(b[:, 120 * c:120 * (c + 1)], prow[0:120, P * c:P * (c + 1)], ident[0:120, 0:120])
            last.then_inc(s("pb_mm"), 1)
            b = banks.open(pe, "pb1", (s("pbuf_copied"), 2))
            for c in range(4):
                last = pe.transpose(b[:, 120 * c:120 * (c + 1)], prow[0:120, P * (4 + c):P * (5 + c)], ident[0:120, 0:120])
            last.then_inc(s("pb_mm"), 1)
            pe.wait_ge(s("h_ready"), 3 * DC)
            for half in range(2):
                b = banks.open(pe, f"hl{half}", (s("hl_copied"), half + 1))
                for c in range(4):
                    last = pe.transpose(b[0:NS + 16, P * c:P * (c + 1)], hT[:, 4 * half + c, NP - 16:N], ident)
                last.then_inc(s("hl_mm"), 1)
            pe.wait_ge(*once("z_ready"))
            pe.wait_ge(s("poolw_loaded"), 16)
            for j in range(DC):
                b = banks.open(pe, f"pool{j}", (s("res3"), j + 1))
                for c in range(2):
                    last = mm(b[:, 0:N], poolw[:, j // 2, c, P * (j % 2):P * (j % 2 + 1)], yT[:, 2 * (j // 2) + c, :],
                              c == 0, c == 1)
                last.then_inc(s("pool_mm"), 1)
            mean_square(3)

            b = banks.open(pe, "route", (s("logits"), 3))
            for blk, (t0, w) in enumerate(BLK):
                for c in range(DC):
                    if blk == 0:
                        pe.wait_ge(s("h_ready"), 3 * DC + c + 1)
                    last = mm(b[0:w, NE * blk:NE * (blk + 1)], hT[:, c, t0:t0 + w], routerw[:, c, :], c == 0, c == DC - 1)
            last.then_inc(once.give("route_mm"), 1)
            for n in range(6):
                t0, w = BLK[n // 2]
                b = banks.open(pe, f"ht{n}", (s("htok_ready"), n + 1))
                for c in range(4):
                    last = pe.transpose(b[0:w, P * c:P * (c + 1)], hT[:, 4 * (n % 2) + c, t0:t0 + w], ident)
                last.then_inc(s("ht_mm"), 1)
            pe.wait_ge(*once("picked"))
            b = banks.open(pe, "rank", (s("ranked"), 3))
            for blk, (t0, w) in enumerate(BLK):
                for e in range(blk + 1):
                    we = BLK[e][1]
                    tri = K("before")[0:we, 0:w] if e == blk else K("ones")[0:we, 0:w]
                    mm(b[0:w, NE * blk:NE * (blk + 1)], tri, pick[0:we, e, :], e == 0, e == blk)
            for e in range(3):
                we = BLK[e][1]
                last = mm(b[0:P, 3 * NE:4 * NE], K("ones")[0:we, 0:P], pick[0:we, e, :], e == 0, e == 2)
            last.then_inc(once.give("rank_mm"), 1)
            moe_tensor(pe, mm)

            for n in range(6):
                t0, w = BLK[n % 3]
                pe.wait_ge(s("res"), 3 * DC + 4 * (n // 3) + 4)
                b = banks.open(pe, f"out{n}", (s("out_copied"), n + 1))
                for c in range(4):
                    last = pe.transpose(b[0:w, P * c:P * (c + 1)], xT[:, 4 * (n // 3) + c, t0:t0 + w], ident)
                last.then_inc(s("out_mm"), 1)

        @block.scalar
        def _(act):
            me = Counted(act)
            chain = s("act_chain")

            def copy(out, in_, sem):
                me.give(act.activation(out, in_, ACT.Copy), sem)

            for dst, src in vector_rows()[0]:
                act.dma_start(dst, src).then_inc(s("vec_loaded"), 16)
            act.wait_ge(s("c_loaded"), 32)
            me.step(act.activation(scrow[0:9, :], crow[0:9, :], ACT.Silu), once.give("siluc"))
            act.wait_ge(*once("c_turned"))
            act.wait_ge(*once("silucT_zero"))
            me.give(act.activation(silucT[:, :, 0:9], banks["c"][:, 0:72].rearrange("p (c j) -> p c j", c=DC),
                                   ACT.Copy), once.give("c_copied"))
            act.wait_ge(s("x_copied"), 5)

            def square_all(i):
                for c in range(DC):
                    if i:
                        act.wait_ge(s("res"), DC * (i - 1) + c + 1)
                    me.give(act.activation(tmpT[:, c, :], xT[:, c, :], ACT.Square), s("squared"))

            def root(i):
                act.wait_ge(s("ms_read"), i + 1)
                me.give(act.activation(rstd[:, :], rstd[:, :], ACT.Sqrt), s("rooted"))

            square_all(0)
            root(0)

            def ada(layer, i):
                k = 12 * layer + i
                act.wait_ge(s("ada_mm"), k + 1)
                if k >= 2:
                    act.wait_ge(s("folded"), k - 1)
                copy(adap[layer][:, k % 2, :], banks[f"ada{layer}_{i}"][:, :], s("ada_copied"))

            for i in range(4):
                ada(0, i)

            def proj_chunk(n):
                kind, idx, _, m = WCHUNKS[n]
                dst = {"f": fqkv, "r": rp}[kind]
                return dst[0:m, idx, :], banks[f"win{n}"][0:m, 0:N]

            act.wait_ge(*once("last_zero"))
            n = 0
            for i, (_, _, cs) in enumerate(WIN):
                for _ in cs:
                    if n % 2:
                        act.wait_ge(s("win_mm"), n + 1)
                        copy(*proj_chunk(n), s("win_act"))
                    n += 1
                ada(0, 4 + i)
            act.wait_ge(s("win_dve"), (len(WCHUNKS) + 1) // 2)
            act.wait_ge(s("win_act"), len(WCHUNKS) // 2)
            me.give(act.activation(flat(tmpT), fqkv[:, 0:2 * HC, :].rearrange("p a b -> p (a b)"), ACT.Square), once.give("qk_squared"))
            act.wait_ge(*once("lf_abs"))
            me.step(act.activation(lftmp[:, 0, :], lftmp[:, 0, :], ACT.Exp), once.give("lf_exp"))
            act.wait_ge(*once("lf_one"))
            me.give(act.activation(lftmp[:, 0, :], lftmp[:, 0, :], ACT.Ln), once.give("lf_ln"))
            act.wait_ge(s("qkms_read"), 6)
            me.give(act.activation(flat(tmpT), flat(tmpT), ACT.Sqrt), once.give("qk_rooted"))
            for n in range(6):
                act.wait_ge(s("kv_turned"), n + 1)
                w = BLK[n % 3][1]
                copy(kvrow[0:w, n // 3, n % 3, :], banks[f"kv{n}"][0:w, :], s("kv_copied"))
            act.wait_ge(*once("lf_turned"))
            for blk, (t0, w) in enumerate(BLK):
                copy(lfrow[0:w, blk, :], banks["lf"][0:w, H * blk:H * (blk + 1)], s("lf_copied"))
            act.wait_ge(*once("last_turned"))
            copy(lastrow[0:NPC * 8, 0, :], banks["last"][0:NPC * 8, 0:P], s("last_copied"))
            copy(lastrow[0:NPC, 1, :], banks["last"][0:NPC, P:2 * P], s("last_copied"))

            def exponentials(k):
                act.wait_ge(s("shifted"), k + 1)
                v = pr[:, k % 2, :, 0:P * (k % 2 + 1)]
                me.give(act.activation(v, v, ACT.Exp), s("exped"))

            exponentials(0)
            for k in range(8):
                if k < 7:
                    exponentials(k + 1)
                act.wait_ge(s("pt_mm"), k + 1)
                if k >= 2:
                    act.wait_ge(s("o_mm"), k - 1)
                nb = k % 2 + 1
                copy(prT[:, k % 2, :, 0:nb, :],
                     banks[f"pt{k // 2}{k % 2}"][:, 0:2 * nb * P].rearrange("p (h j q) -> p h j q", h=2, j=nb), s("probsT"))
                act.wait_ge(s("o_mm"), k + 1)
                copy(yT[:, k // 2, P * (k % 2):P * (k % 2 + 1)], banks[f"o{k // 2}{k % 2}"][:, 0:P], s("o_copied"))
            act.wait_ge(*once("rp_mixed"))
            me.give(act.activation(rp[0:LORA, PWL, :], rp[0:LORA, PWL, :], ACT.Tanh), once.give("wl_tanh"))
            me.give(act.activation(rp[:, PGL, :], rp[:, PGL, :], ACT.Sigmoid), once.give("gl_sigmoid"))
            for name, dst, col in (("dec", lw, VB_W0), ("icl", icl, VB_A0)):
                for c in range(HC):
                    act.wait_ge(*lora(name, "mm", c + 1))
                    me.give(act.activation(dst[:, c, :], banks[f"{name}{c}"][:, 0:N], ACT.Sigmoid,
                                           bias=vT[:, 1, col + c:col + c + 1]), s("lora_ready"))
            for c in range(HC):
                act.wait_ge(*lora("gat", "mm", c + 1))
                copy(gate[:, c, :], banks[f"gat{c}"][:, 0:N], s("lora_ready"))
            act.wait_ge(*once("kk_scaled"))
            me.give(act.activation(flat(tmpT)[:, 0:HC * N], kkT.rearrange("p a b -> p (a b)"), ACT.Square), once.give("kk_squared"))
            def scores_of(q):
                act.wait_ge(s("ss_mm"), q + 1)
                copy(psm[32 * (q % 4):32 * (q % 4) + 32, q // 4, :], banks[f"ss{q}"][0:32, 0:PAST + NT], s("ss_copied"))

            for q in range(NB):
                for half in range(2):
                    act.wait_ge(s("kt_mm"), 2 * q + half + 1)
                    if q >= 2:
                        act.wait_ge(s("ss_mm"), q - 1)
                    copy(ktb[:, q % 2, 2 * half:2 * half + 2, 0:PAST],
                         banks[f"kt{q}{half}"][:, :].rearrange("p (c k) -> p c k", c=2), s("kt_copied"))
                copy(ktb[:, q % 2, :, PAST:PAST + NT], fqkv[:, HC:2 * HC, NP + NT * q:NP + NT * (q + 1)], s("kt_copied"))
                if q:
                    scores_of(q - 1)
                if q == 2:
                    act.wait_ge(*sums("kks", "read", 3))
                    me.give(act.activation(flat(tmpT)[:, 0:HC * N], flat(tmpT)[:, 0:HC * N], ACT.Sqrt), once.give("kk_rooted"))
            scores_of(NB - 1)
            act.wait_ge(*once("cum_ready"))
            me.give(act.activation(lw[:, :, NP:N], lw[:, :, NP:N], ACT.Exp), s("decay_exp"))
            me.give(act.activation(wdec, cumv, ACT.Exp), s("decay_exp"))
            me.give(act.activation(winv, cumv, ACT.Exp, scale=-1.0), s("decay_exp"))
            me.give(act.activation(wprev, wprev, ACT.Exp), s("decay_exp"))
            act.wait_ge(*once("psm_shifted"))
            me.give(act.activation(psm, psm, ACT.Exp), once.give("psm_exped"))
            for g in range(2):
                act.wait_ge(s("pst_mm"), g + 1)
                copy(psT[:, g, 0:2, :], banks[f"pst{g}"][:, 0:2 * P].rearrange("p (j q) -> p j q", j=2), s("psT_ready"))
                copy(psT[0:32, g, 2, :], banks[f"pst{g}"][0:32, 2 * P:3 * P], s("psT_ready"))
            act.wait_ge(*once("so_mm"))
            copy(yT[:, 0:HC, NP:N], banks["so"][:, 0:HC * NS].rearrange("p (c t) -> p c t", c=HC), once.give("so_copied"))

            act.wait_ge(s("mix_stored"), 16 * CACHE_STORES)
            for i in range(6):
                act.wait_ge(s("sr_mm"), i + 1)
                copy(srow[:, i, :], banks[f"sr{i}"][0:NS, :], s("srow_copied"))
            for pair in range(NCH // 2):
                for n in (2 * pair, 2 * pair + 1):
                    act.wait_ge(s("bkt_mm"), n + 1)
                    copy(bkt[:, n % 2].rearrange("p h k -> p (h k)"), banks[f"bkt{n}"][:, :], s("bkt_ready"))
                    act.wait_ge(s("vt_mm"), n + 1)
                    vt = banks[f"vt{n}"][:, :].rearrange("p (h k) -> p h k", h=H)
                    for a_ in range(2):
                        o = own(1 - a_)
                        for dst in (sav, su):
                            copy(of(dst[o, n % 2], a_), of(vt[o], a_), s("vt_ready") if a_ and dst is su else chain)
                for lv in range(LEVELS):
                    for n in (2 * pair, 2 * pair + 1):
                        act.wait_ge(s("x_mm"), kth(n, lv) + 1)
                        copy(xb[:, n % 2].rearrange("p h k -> p (h k)"), banks[f"x_{LEVELS * n + lv}"][:, 0:HC * L], s("xb_ready"))
                    if pair + lv == 0:
                        for a_ in range(2):
                            for c in range(HC):
                                copy(lu[own(a_), :, 2 * c + a_, :], ar[own(a_), c, :, 0, :], s("lu_own"))
                for n in (2 * pair, 2 * pair + 1):
                    act.wait_ge(s("u_mm"), n + 1)
                    copy(ub[:, n % 2].rearrange("p h k -> p (h k)"), banks[f"u{n}"][:, 0:HC * DH], s("u_ready"))
                    act.wait_ge(s("sa_mm"), n + 1)
                    for a_ in range(2):
                        copy(of(sav[own(a_), n % 2], a_), banks[f"sa{n}"][own(a_), 0:HC * DH].rearrange("p (c k) -> p c k", c=HC),
                             s("sa_ready") if a_ else chain)
                    act.wait_ge(s("y_mm"), n + 1)
                    copy(yT[:, HC:2 * HC, L * n:L * (n + 1)], banks[f"y{n}"][:, 0:HC * L].rearrange("p (c t) -> p c t", c=HC),
                         s("yc_copied"))
            act.wait_ge(*once("fst_mm"))
            copy(bkt[:, 0, 0:HC, :], banks["fst"][:, 0:HC * DH].rearrange("p (c k) -> p c k", c=HC), once.give("fst_copied"))
            act.wait_ge(*once("syt_mm"))
            copy(yT[:, HC:2 * HC, NP:N], banks["syt"][:, 0:HC * NS].rearrange("p (c t) -> p c t", c=HC), once.give("syt_copied"))
            act.wait_ge(*once("gn_centred"))
            me.give(act.activation(flat(tmpT)[:, 0:HC * N], flat(yT)[:, HC * N:2 * HC * N], ACT.Square), once.give("gn_squared"))
            act.wait_ge(*sums("gnv", "read", 3))
            me.give(act.activation(flat(tmpT)[:, 0:HC * N], flat(tmpT)[:, 0:HC * N], ACT.Sqrt), once.give("gn_rooted"))

            square_all(1)
            root(1)
            for n in range(FF // P):
                act.wait_ge(s("gate_mm"), n + 1)
                if n >= 2:
                    act.wait_ge(s("act_ready"), n - 1)
                me.give(act.activation(ffsilu[:, n % 2, :], banks[f"gate{n}"][:, 0:N], ACT.Silu), s("silu_ready"))
                if n >= 4 and (n % 4 == 3 or n == FF // P - 1):
                    ada(1, 2 * (n // 4) - 2)
                    ada(1, 2 * (n // 4) - 1)
            ada(1, 10)
            ada(1, 11)
            square_all(2)
            root(2)
            for half in range(2):
                act.wait_ge(s("pb_mm"), half + 1)
                act.wait_ge(*once("exts_zero"))
                me.give(act.activation(exts[:, 4 * half:4 * half + 4, :, 1:16],
                                       banks[f"pb{half}"][:, 0:480].rearrange("p (c b r) -> p c b r", c=4, r=PBUF),
                                       ACT.Copy), s("pbuf_copied"))
            for half in range(2):
                act.wait_ge(s("hl_mm"), half + 1)
                copy(hlast[0:NS + 16, 512 * half:512 * (half + 1)], banks[f"hl{half}"][0:NS + 16, :], s("hl_copied"))
            square_all(3)
            root(3)
            act.wait_ge(*once("z_used"))
            for n in range(6):
                w = BLK[n // 2][1]
                act.wait_ge(s("ht_mm"), n + 1)
                copy(htok[0:w, n // 2, 512 * (n % 2):512 * (n % 2 + 1)], banks[f"ht{n}"][0:w, :], s("htok_ready"))
                if n == 1:
                    act.wait_ge(*once("top_ready"))
                    me.give(act.activation(gate2[:, :, 0], gate2[:, :, 0], ACT.Exp), once.give("top_exped"))
            moe_scalar(act)
            for n in range(6):
                w = BLK[n % 3][1]
                act.wait_ge(s("out_mm"), n + 1)
                copy(outrow[0:w, n % 3, 512 * (n // 3):512 * (n // 3 + 1)], banks[f"out{n}"][0:w, :], s("out_copied"))

        @block.vector
        def _(dve):
            me = Counted(dve)
            chain = s("dve_chain")
            TT, TS, STT = dve.tensor_tensor, dve.tensor_scalar, dve.scalar_tensor_tensor

            def do(ins, sem=None):
                me.step(ins, sem or chain)

            dve.wait_ge(s("const_loaded"), 16)
            for n, (blk, c0, nc_) in enumerate(XJOBS):
                t0, w = BLK[blk]
                dve.wait_ge(s("x_turned"), n + 1)
                do(dve.tensor_copy(xT[:, c0:c0 + nc_, t0:t0 + w],
                                   banks[f"x{n}"][:, 0:nc_ * w].rearrange("p (c t) -> p c t", c=nc_)), s("x_copied"))

            def mod_tile(layer, i):
                dve.wait_ge(s("folded"), 12 * layer + i + 1)
                bias = vT[:, 0, 48 * layer + 4 * i:48 * layer + 4 * i + 4]
                do(TT(modT[layer][:, 4 * i:4 * i + 4, :], banks[f"fold{layer}_{i}"][:, 0:36].rearrange("p (j m) -> p j m", j=4),
                      spread(bias, 2, 9), ALU.add), s("mod_ready"))

            def mod(i, part):
                at = 24 * (i % 2) + 8 * part
                return modT[i // 2][:, at:at + 8, :]

            def gains(i):
                g = spread(vT[:, 0, VA_NORM[i]:VA_NORM[i] + 8], 2, 9)
                do(TS(gainT[i][:, :, :], mod(i, 1), 1.0, None, ALU.add))
                do(TT(gainT[i][:, :, :], gainT[i][:, :, :], g, ALU.mult))

            def mean_of(i):
                dve.wait_ge(s("ms_ready"), i + 1)
                do(TS(rstd[:, :], banks[f"ms{i}"][:, 0:N], 1.0 / D, RMS_EPS, ALU.mult, ALU.add), s("ms_read"))
                dve.wait_ge(s("rooted"), i + 1)
                do(dve.reciprocal(rstd[:, :], rstd[:, :]))

            def by_seq(ap):
                return ap.rearrange("p c (b t) -> p c b t", t=NT)

            def modulated(i):
                do(TT(hT[:, :, :], xT[:, :, :], spread(rstd[:, :], 1, DC), ALU.mult))
                hs = by_seq(hT[:, :, NP:N])
                do(TT(hs, hs, spread(gainT[i][:, :, 1:9], 3, NT), ALU.mult))
                do(TT(hs, hs, spread(mod(i, 0)[:, :, 1:9], 3, NT), ALU.add))
                for c in range(DC):
                    v = hT[:, c, 0:NP]
                    me.give(TS(v, v, gainT[i][:, c, 0:1], mod(i, 0)[:, c, 0:1], ALU.mult, ALU.add), s("h_ready"))

            def residual(src, gate_, j):
                do(STT(xT[:, j, 0:NP], src[:, 0:NP], gate_[:, j, 0:1], xT[:, j, 0:NP], ALU.mult, ALU.add))

            def residual_samples(src, gate_, j, sem, done=None):
                t = small[:, 0:NS]
                do(TT(t.rearrange("p (b t) -> p b t", t=NT), src[:, NP:N].rearrange("p (b t) -> p b t", t=NT),
                      spread(gate_[:, j, 1:9], 2, NT), ALU.mult), sem)
                do(TT(xT[:, j, NP:N], xT[:, j, NP:N], t, ALU.add), done or s("res"))

            mean_of(0)
            dve.wait_ge(*once("vec_turned"))
            do(dve.tensor_copy(vT[:, 0, :], banks["vec"][:, 0:P]), once.give("vec_copied"))
            for i in range(4):
                mod_tile(0, i)
            gains(0)
            modulated(0)

            dve.wait_ge(*once("last_zero"))
            n = 0
            for i, (_, _, cs) in enumerate(WIN):
                for kind, idx, _, m in cs:
                    if n % 2 == 0:
                        dve.wait_ge(s("win_mm"), n + 1)
                        src = banks[f"win{n}"][0:m, 0:N]
                        if kind == "l":
                            do(TS(rstd[0:H, :], src, fbias[:, 0:1], None, ALU.add), s("win_dve"))
                        else:
                            do(dve.tensor_copy({"f": fqkv, "r": rp}[kind][0:m, idx, :], src), s("win_dve"))
                    n += 1
                if i == 2:
                    dve.wait_ge(*once("vec2_turned"))
                    do(dve.tensor_copy(vT[:, 1:3, :], banks["vec2"][:, 0:2 * P].rearrange("p (i f) -> p i f", i=2)),
                       once.give("vec2_copied"))
                    qg = vT[:, 1, VB_QG:VB_QG + 1]
                    do(TS(qg, qg, DH ** -0.5, None, ALU.mult))
                if i:
                    mod_tile(0, 3 + i)
            mod_tile(0, 11)
            gains(1)

            z = rstd[0:H, :]
            t0, t1 = lftmp[:, 0, :], lftmp[:, 1, :]
            dve.wait_ge(s("ada_mm"), 12)
            do(TS(t1, z, -1.0, None, ALU.mult))
            do(TT(t0, z, t1, ALU.min), once.give("lf_abs"))
            dve.wait_ge(*once("lf_exp"))
            do(TS(t0, t0, 1.0, None, ALU.add), once.give("lf_one"))
            do(TS(t1, z, 0.0, None, ALU.min))
            for i in range(6):
                dve.wait_ge(s("qkms"), i + 1)
                do(TS(flat(tmpT)[:, 384 * i:384 * (i + 1)], banks[f"qkms{i}"][:, 0:384], 1.0 / DH, RMS_EPS, ALU.mult, ALU.add),
                   s("qkms_read"))
            dve.wait_ge(*once("lf_ln"))
            do(TT(logf, t1, t0, ALU.subtract), once.give("logf_ready"))
            do(dve.tensor_tensor_scan(negF, K("restart", H), logf, 0.0, ALU.mult, ALU.add))
            do(TS(negF, negF, -1.0, None, ALU.mult), once.give("negF_ready"))
            dve.wait_ge(*once("qk_rooted"))
            do(dve.reciprocal(flat(tmpT), flat(tmpT)))
            dve.wait_ge(s("win_act"), len(WCHUNKS) // 2)
            for part, g, sem in ((1, VB_KG, "k_ready"), (0, VB_QG, "q_ready")):
                v = fqkv[:, HC * part:HC * (part + 1), :].rearrange("p a b -> p (a b)")
                r = flat(tmpT)[:, HC * N * part:HC * N * (part + 1)]
                do(STT(v, v, vT[:, 1, g:g + 1], r, ALU.mult, ALU.mult), once.give(sem))
            do(dve.tensor_copy(lastP, rp[:, :, NP - 1]))
            do(dve.tensor_copy(lastS, rp[:, :, NP + NT - 1:N:NT]), once.give("last_ready"))
            def masked(k):
                qb = k % 2
                nk = P * (qb + 1)
                if k >= 2:
                    dve.wait_ge(s("pt_mm"), k - 1)
                for par in range(2):
                    dve.wait_ge(s("s_mm"), 2 * k + par + 1)
                    me.give(TT(pr[:, k % 2, par, 0:nk], banks[f"s{k // 2}{qb}{par}"][:, 0:nk], K("causal")[:, 256 - nk:256], ALU.add),
                            s("scored"))
                dve.wait_ge(s("scored"), 2 * k + 2)
                v, m = pr[:, k % 2, :, 0:nk], small[:, 36 + 2 * qb:38 + 2 * qb]
                do(dve.tensor_reduce(m, v, AX.X, ALU.max))
                do(TT(v, v, spread(m, 2, nk), ALU.subtract), s("shifted"))

            def normed(k):
                qb = k % 2
                nk = P * (qb + 1)
                v, m = pr[:, k % 2, :, 0:nk], small[:, 36 + 2 * qb:38 + 2 * qb]
                dve.wait_ge(s("exped"), k + 1)
                do(dve.tensor_reduce(m, v, AX.X, ALU.add))
                do(dve.reciprocal(m, m))
                do(TT(v, v, spread(m, 2, nk), ALU.mult), s("probs"))

            masked(0)
            for k in range(8):
                if k < 7:
                    masked(k + 1)
                normed(k)
            kx, rx, vx = rp[:, PK:PK + HC, :], rp[:, PR:PR + HC, :], rp[:, PV:PV + HC, :]

            def fl(t):
                return t.rearrange("p a b -> p (a b)")

            dve.wait_ge(*once("rp_mixed"))
            for c in range(HC):
                do(TS(kkT[:, c, :], kx[:, c, :], vT[:, 1, VB_KK + c:VB_KK + c + 1], None, ALU.mult),
                   once.give("kk_scaled") if c == HC - 1 else chain)
            dve.wait_ge(*lora("icl", "ready", HC))
            dve.wait_ge(*lora("dec", "ready", HC))
            for c in range(HC):
                t = flat(tmpT)[:, HC * N + N * c:HC * N + N * (c + 1)]
                do(TS(t, icl[:, c, :], -1.0, vT[:, 1, VB_KA + c:VB_KA + c + 1], ALU.add, ALU.mult))
                do(STT(kx[:, c, :], t, 1.0, kx[:, c, :], ALU.add, ALU.mult))
                do(STT(t, rx[:, c, :], vT[:, 1, VB_RK + c:VB_RK + c + 1], kx[:, c, :], ALU.mult, ALU.mult),
                   once.give("rk_ready") if c == HC - 1 else chain)
            for i in range(3):
                dve.wait_ge(*sums("kks", "mm", i + 1))
                do(TS(flat(tmpT)[:, 384 * i:384 * (i + 1)], banks[f"kks{i}"][:, 0:384], 1e-24, None, ALU.max), s("sums_read"))
            dve.wait_ge(*once("kk_rooted"))
            r = flat(tmpT)[:, 0:HC * N]
            do(dve.reciprocal(r, r))
            do(TT(fl(kkT), fl(kkT), r, ALU.mult))
            do(TS(fl(kkT), fl(kkT), -1.0, None, ALU.mult))
            for i in range(3):
                dve.wait_ge(*sums("bon", "mm", i + 1))
                o = slice(384 * i, 384 * (i + 1))
                do(TT(fl(bonus)[:, o], banks[f"bon{i}"][:, 0:384], fl(vx)[:, o], ALU.mult), s("sums_read"))
            do(TS(fl(lw), fl(lw), -DECAY, None, ALU.mult))
            for c in range(HC):
                do(dve.tensor_tensor_scan(cumv[:, c, :], K("reset"), lw[:, c, 0:NP], 0.0, ALU.mult, ALU.add))
            do(TT(wprev, cumv, lw[:, :, 0:NP], ALU.subtract), once.give("cum_ready"))
            dve.wait_ge(s("ss_copied"), NB)
            do(TT(psm[:, :, PAST:PAST + NT], psm[:, :, PAST:PAST + NT], spread(K("newmask"), 1, 2), ALU.add))
            m = small[:, 42:44]
            do(dve.tensor_reduce(m, psm, AX.X, ALU.max))
            do(TT(psm, psm, spread(m, 2, PAST + NT), ALU.subtract), once.give("psm_shifted"))
            dve.wait_ge(*once("psm_exped"))
            do(dve.tensor_reduce(m, psm, AX.X, ALU.add))
            do(dve.reciprocal(m, m))
            do(TT(psm, psm, spread(m, 2, PAST + NT), ALU.mult))
            for g in range(2):
                do(TT(pnew[:, g, :, :], spread(psm[:, g, PAST:PAST + NT], 1, NB),
                      spread(K("seqmask")[:, 8 * g:8 * g + 8], 2, NT), ALU.mult), chain if g == 0 else once.give("psm_ready"))

            for g in range(2):
                dve.wait_ge(s("av_mm"), g + 1)
                do(TT(avm[:, g, :].rearrange("p (h d) -> p h d", h=H), banks[f"av{g}"][:, :].rearrange("p (h d) -> p h d", h=H),
                      spread(K("headof"), 2, DH), ALU.mult), s("av_masked"))
            dve.wait_ge(*once("so_mm"))
            dve.wait_ge(s("mix_stored"), 16 * CACHE_STORES)
            dve.wait_ge(s("decay_exp"), 4)
            do(STT(fl(bT), fl(kkT), -1.0, fl(icl), ALU.mult, ALU.mult), once.give("delta_ops"))

            def chunks(ap):
                return ap[:, :, 0:NP].rearrange("p c (n t) -> p c n t", t=L)

            do(TT(ar[:, :, :, 0, :], chunks(kkT), chunks(wprev), ALU.mult))
            do(TT(ar[:, :, :, 1, :], chunks(rx), chunks(wdec), ALU.mult))
            for a_ in range(2):
                o = own(a_)
                do(TT(bk[o, :, :, a_, :], chunks(bT)[o], chunks(winv)[o], ALU.mult))
                do(TT(bk[o, :, :, 1 - a_, :], chunks(kx)[o], chunks(winv)[o], ALU.mult), once.give("packed") if a_ else chain)
            do(dve.memset(of(su[own(0), 0], 0), 0.0))
            do(dve.memset(of(su[own(1), 0], 1), 0.0), s("su_ready"))

            def rows(t, i):
                return spread(svec[:, t, i, :], 1, 32)

            def sample_ops():
                dve.wait_ge(s("svec_loaded"), 16 * 3 * NB)
                dve.wait_ge(s("sst_loaded"), 16)
                for t in range(NT):
                    yield lambda t=t: do(TT(sprod, sst, rows(t, 1), ALU.mult))
                    yield lambda t=t: do(dve.tensor_reduce(ssa, sprod, AX.X, ALU.add))
                    yield lambda t=t: do(TT(sst, sst, rows(t, 0), ALU.mult))
                    yield lambda t=t: do(TT(sprod, spread(ssa, 2, DH), rows(t, 2), ALU.mult))
                    yield lambda t=t: do(TT(sst, sst, sprod, ALU.add))
                    yield lambda t=t: do(TT(sprod, spread(sval[:, t, :], 2, DH), rows(t, 3), ALU.mult))
                    yield lambda t=t: do(TT(sst, sst, sprod, ALU.add))
                    yield lambda t=t: do(TT(sprod, sst, rows(t, 4), ALU.mult))
                    yield lambda t=t: do(dve.tensor_reduce(sy[:, t, :], sprod, AX.X, ALU.add), s("sy_ready"))

            pending = sample_ops()

            def some(k):
                for _, op in zip(range(k), pending):
                    op()

            def fh(ap):
                return ap.rearrange("p h k -> p (h k)")

            for pair in range(NCH // 2):
                for n in (2 * pair, 2 * pair + 1):
                    for par in range(2):
                        dve.wait_ge(s("gt_mm"), 2 * n + par + 1)
                        do(TT(gt[:, n % 2].rearrange("p (c a) t -> p c a t", a=2)[:, :, par, :],
                              banks[f"gt{n}{par}"][:, :].rearrange("p (c t) -> p c t", c=HC),
                              spread(K("chunk"), 1, HC), ALU.mult), s("gt_ready"))
                for lv in range(LEVELS):
                    for n in (2 * pair, 2 * pair + 1):
                        i = n % 2
                        if lv == 0:
                            dve.wait_ge(s("x_mm"), kth(n, lv) + 1)
                            dve.wait_ge(s("xb_ready"), kth(n, lv) + 1)
                            idb = spread(K("eyes"), 1, HC)
                            do(TT(tb[:, i], xb[:, i], idb, ALU.add), s("t_ready"))
                            do(TT(tt[:, i], nm[:, i], idb, ALU.add), s("t_ready"))
                            continue
                        if lv < LEVELS - 1:
                            dve.wait_ge(s("t_mm"), t_mms(n, lv) - 1)
                            do(TT(fh(tb[:, i]), fh(tb[:, i]), banks[f"t_{n}{lv}"][:, 0:HC * L], ALU.add), s("t_ready"))
                        dve.wait_ge(s("t_mm"), t_mms(n, lv))
                        do(TT(fh(tt[:, i]), fh(tt[:, i]), banks[f"tt_{n}{lv}"][:, 0:HC * L], ALU.add), s("t_ready"))
                    some(3)
                for n in (2 * pair, 2 * pair + 1):
                    i = n % 2
                    dve.wait_ge(s("st_mm"), n + 1)
                    for a_ in range(2):
                        o = own(a_)
                        nxt = of(su[o, (n + 1) % 2], a_)
                        st = banks[f"st{n}"][o, 0:HC * DH].rearrange("p (c k) -> p c k", c=HC)
                        do(TT(nxt, of(su[o, i], a_), st, ALU.add), s("state_read") if a_ else chain)
                    for a_ in range(2):
                        o = own(a_)
                        nxt = of(su[o, (n + 1) % 2], a_)
                        do(TT(nxt, nxt, spread(wdec[o, :, L * (n + 1) - 1], 2, DH), ALU.mult),
                           chain if a_ == 0 else s("su_ready") if n < NCH - 1 else once.give("final_state"))
            some(36)

            y2 = flat(yT)[:, HC * N:2 * HC * N]
            for i in range(3):
                o = slice(384 * i, 384 * (i + 1))
                dve.wait_ge(*sums("gnm", "mm", 3 if i == 0 else i + 1))
                do(STT(y2[:, o], banks[f"gnm{i}"][:, 0:384], -1.0 / DH, y2[:, o], ALU.mult, ALU.add), s("sums_read"))
            do(dve.memset(small[:, 62:63], 0.0), once.give("gn_centred"))
            for i in range(3):
                dve.wait_ge(*sums("gnv", "mm", i + 1))
                do(TS(flat(tmpT)[:, 384 * i:384 * (i + 1)], banks[f"gnv{i}"][:, 0:384], 1.0 / DH, GN_EPS, ALU.mult, ALU.add),
                   s("sums_read"))
            dve.wait_ge(*once("gn_rooted"))
            r = flat(tmpT)[:, 0:HC * N]
            do(dve.reciprocal(r, r))
            do(TT(y2, y2, r, ALU.mult))
            for c in range(HC):
                v = yT[:, HC + c, :]
                do(TS(v, v, vT[:, 1, VB_LNW + c:VB_LNW + c + 1], vT[:, 1, VB_LNB + c:VB_LNB + c + 1], ALU.mult, ALU.add))
            do(TT(y2, y2, fl(bonus), ALU.add))
            dve.wait_ge(*lora("gat", "ready", HC))
            do(TT(y2, y2, fl(gate), ALU.mult), once.give("mix_ready"))

            for j in range(DC):
                dve.wait_ge(s("wo_mm"), j + 1)
                src = banks[f"wo{j}"]
                residual(src, mod(0, 2), j)
                residual_samples(src, mod(0, 2), j, s("res1"))
            mean_of(1)
            modulated(1)

            def hidden(i):
                for n in range(4 * i, min(4 * i + 4, FF // P)):
                    dve.wait_ge(s("silu_ready"), n + 1)
                    dve.wait_ge(s("up_mm"), n + 1)
                    if i >= 2:
                        dve.wait_ge(s("down_mm"), DC * (i - 1))
                    do(TT(ffact[:, i % 2, n % 4, :], ffsilu[:, n % 2, :], banks[f"up{n}"][:, 0:N], ALU.mult), s("act_ready"))

            def down(i):
                for j in range(DC):
                    dve.wait_ge(s("down_mm"), DC * i + j + 1)
                    src = banks[f"down{i}_{j}"][:, 0:N]
                    if i == 0:
                        do(dve.tensor_copy(yT[:, j, :], src), s("ff_added"))
                    else:
                        do(TT(yT[:, j, :], yT[:, j, :], src, ALU.add), s("ff_added"))
                    if i == 5:
                        residual(yT[:, j, :], mod(1, 2), j)
                        residual_samples(yT[:, j, :], mod(1, 2), j, chain)

            hidden(0)
            for i in range(6):
                if i < 5:
                    hidden(i + 1)
                down(i)
                mod_tile(1, 2 * i)
                mod_tile(1, 2 * i + 1)
            gains(2)
            gains(3)
            gp = mod(2, 2)
            do(TT(gp, gp, spread(vT[:, 1, VB_PS:VB_PS + 8], 2, 9), ALU.mult))

            do(dve.memset(exts[:, :, :, 0], 0.0), once.give("exts_zero"))
            do(dve.memset(ext[:, :, 0:16], 0.0))
            mean_of(2)
            modulated(2)
            dve.wait_ge(s("h_ready"), 3 * DC)
            do(dve.tensor_copy(ext[:, :, 16:16 + NP], hT[:, :, 0:NP]))
            dve.wait_ge(s("pbuf_copied"), 2)
            hs = by_seq(hT[:, :, NP:N])
            do(dve.tensor_copy(exts[:, :, :, 16:20], hs))
            ext2 = flat(tmpT)[:, 0:DC * (16 + NP)].rearrange("p (c t) -> p c t", c=DC)
            exts2 = other[:, 0:DC * NB * 20].rearrange("p (c b t) -> p c b t", c=DC, b=NB)
            pair_ = [(ext, exts), (ext2, exts2)]
            for lv in range(4):
                (a0, b0), (a1, b1) = pair_[lv % 2], pair_[1 - lv % 2]
                sh, c0, lo = 1 << lv, 2 * lv, (2 << lv) - 1
                do(TT(a1[:, c0:DC, lo:], a0[:, c0:DC, lo:], a0[:, c0:DC, lo - sh:16 + NP - sh], ALU.add))
                do(TT(b1[:, c0:DC, :, lo:], b0[:, c0:DC, :, lo:], b0[:, c0:DC, :, lo - sh:20 - sh], ALU.add))
                g = slice(c0, c0 + 2)
                do(STT(yT[:, g, 0:NP], a1[:, g, 16:16 + NP], 1.0 / WINS[lv], hT[:, g, 0:NP], ALU.mult, ALU.subtract))
                head = yT[:, g, 0:16]
                cnt = K("count").rearrange("p (g t) -> p g t", g=4)[:, lv, :]
                do(TT(head, a1[:, g, 16:32], spread(cnt, 1, 2), ALU.mult))
                do(TT(head, head, hT[:, g, 0:16], ALU.subtract))
                for c in (c0, c0 + 1):
                    do(STT(by_seq(yT[:, :, NP:N])[:, c], b1[:, c, :, 16:20], 1.0 / WINS[lv], hs[:, c], ALU.mult, ALU.subtract))
            do(dve.memset(small[:, 58:59], 0.0), once.give("z_ready"))
            for j in range(DC):
                dve.wait_ge(s("pool_mm"), j + 1)
                src = banks[f"pool{j}"]
                residual(src, mod(2, 2), j)
                residual_samples(src, mod(2, 2), j, s("res3"))
            mean_of(3)
            modulated(3)
            dve.wait_ge(s("pool_stored"), 16 * (2 + NB))
            for table in (comb, slot_at, slot_e, logit, top, topi, gate2):
                do(dve.memset(table, 0.0))
            do(dve.memset(flat(yT), 0.0), once.give("z_used"))

            dve.wait_ge(*once("route_mm"))
            idx = gate2[:, :, 2:4]
            for blk, (_, w) in enumerate(BLK):
                me.give(TT(logit[0:w, blk, :], banks["route"][0:w, NE * blk:NE * (blk + 1)], routerb[0:w, :], ALU.add), s("logits"))
            dve.wait_ge(s("logits"), 3)
            for blk, (_, w) in enumerate(BLK):
                do(dve.max(top[0:w, blk, :], logit[0:w, blk, :]))
            do(TT(gate2[:, :, 0], top[:, :, 1], top[:, :, 0], ALU.subtract), once.give("top_ready"))
            for blk, (_, w) in enumerate(BLK):
                do(dve.max_index(topi[0:w, blk, :].bitcast(U32), top[0:w, blk, :], logit[0:w, blk, :]))
            do(dve.tensor_copy(idx, topi[:, :, 0:2].bitcast(U32)))
            first, second = logit, gate_e
            for k, dst in enumerate((first, second)):
                do(TT(dst, spread(K("iota")[:, 0:NE], 1, 3), spread(idx[:, :, k], 2, NE), ALU.is_equal))
            do(TT(pick, first, second, ALU.add), once.give("picked"))
            dve.wait_ge(*once("top_exped"))
            e, hi_ = gate2[:, :, 0], gate2[:, :, 1]
            do(TS(hi_, e, 1.0, None, ALU.add))
            do(dve.reciprocal(hi_, hi_))
            do(TT(e, e, hi_, ALU.mult))
            do(TT(first, first, spread(hi_, 2, NE), ALU.mult))
            do(TT(second, second, spread(e, 2, NE), ALU.mult))
            do(TT(second, second, first, ALU.add))
            dve.wait_ge(*once("rank_mm"))
            do(dve.tensor_copy(small[:, 48:48 + NE], banks["rank"][:, 3 * NE:4 * NE]))
            for blk, (_, w) in enumerate(BLK):
                me.give(STT(slot_e[0:w, blk, :], banks["rank"][0:w, NE * blk:NE * (blk + 1)], 1.0, pick[0:w, blk, :],
                            ALU.add, ALU.mult), s("ranked"))
            dve.wait_ge(s("ranked"), 3)
            do(TS(slot_e, slot_e, -1.0, None, ALU.add))
            do(TS(later, slot_e, -float(CAP), None, ALU.add))
            count = moe_vector(dve, do)
            dve.wait_ge(*after("comb_added", count * DC))
            for j in range(DC):
                residual(yT[:, j, :], mod(3, 2), j)
                residual_samples(yT[:, j, :], mod(3, 2), j, chain)

        @block.gpsimd
        def _(pool):
            me = Counted(pool)
            me.step(pool.memset(vrow[:, 1:3, :], 0.0), once.give("vrow_zero"))
            me.step(pool.memset(silucT[:, :, :], 0.0), once.give("silucT_zero"))
            for dst, src in vector_rows()[1]:
                pool.dma_start(dst, src).then_inc(s("vec2_loaded"), 16)
            pool.wait_ge(s("x_turned"), len(XJOBS))
            me.step(pool.memset(rp[LORA:P, PWL, :], 0.0), s("pool_chain"))
            me.step(pool.memset(rp[LORA:P, PAL, :], 0.0), once.give("last_zero"))
            pool.wait_ge(s("ada_mm"), 12)
            me.step(pool.memset(qbd, 0.0), s("pool_chain"))
            pool.wait_ge(*once("q_ready"))
            for c in range(HC):
                for par in range(2):
                    p0, at = DH * par, NT * (2 * c + par)
                    me.step(pool.tensor_copy(qbd[p0:p0 + DH, :, c, at:at + NT],
                                             fqkv[p0:p0 + DH, c, NP:N].rearrange("p (q t) -> p q t", t=NT)), s("qbd_ready"))
            pool.wait_ge(s("win_dve"), (len(WCHUNKS) + 1) // 2)
            pool.wait_ge(s("win_act"), len(WCHUNKS) // 2)
            pool.wait_ge(*once("last_ready"))
            me.step(pool.tensor_tensor(diff[:, :, 1:NP], rp[:, :, 0:NP - 1], rp[:, :, 1:NP], ALU.subtract), s("pool_chain"))
            me.step(pool.tensor_scalar(diff[:, :, 0], rp[:, :, 0], -1.0, None, ALU.mult), s("pool_chain"))
            rs, ds_ = by_sequence(rp[:, :, NP:N]), by_sequence(diff[:, :, NP:N])
            me.step(pool.tensor_tensor(ds_[:, :, :, 1:NT], rs[:, :, :, 0:NT - 1], rs[:, :, :, 1:NT], ALU.subtract), s("pool_chain"))
            prev = vT[:, 2, 0:NPC * NB].rearrange("p (c b) -> p c b", c=NPC)
            me.step(pool.tensor_tensor(ds_[:, :, :, 0], prev, rs[:, :, :, 0], ALU.subtract), s("pool_chain"))
            me.step(pool.tensor_tensor(diff, diff, spread(vT[:, 1, VB_MU:VB_MU + NPC], 2, N), ALU.mult), s("pool_chain"))
            me.step(pool.tensor_tensor(rp, rp, diff, ALU.add), once.give("rp_mixed"))

            stores = []

            def store(dst, src):
                pool.dma_start(dst, src).then_inc(s("mix_stored"), 16)
                stores.append(1)

            pool.wait_ge(s("kv_copied"), 6)
            for i, (dp, dsm) in enumerate(((k_p, k_s), (v_p, v_s))):
                store(dp[0, 0].rearrange("(b p) h d -> p b (h d)", p=P), kvrow[:, i, 0:2, :])
                store(dsm[0].rearrange("b t h d -> (b t) (h d)"), kvrow[0:NS, i, 2, :])
            pool.wait_ge(s("lf_copied"), 3)
            store(lf_p[0, 0].rearrange("(b p) h -> p b h", p=P), lfrow[:, 0:2, :])
            store(lf_s[0].rearrange("b t h -> (b t) h"), lfrow[0:NS, 2, :])
            pool.wait_ge(s("last_copied"), 2)
            for i, (at, w) in enumerate(PIECES):
                store(sh_s[0][:, at:at + w], lastrow[NB * i:NB * (i + 1), 0, 0:w])
                store(sh_p[0][:, at:at + w], lastrow[i:i + 1, 1, 0:w])
            assert len(stores) == CACHE_STORES
            for q in range(NB):
                pool.wait_ge(s(f"k_page{q % 2}"), 64 * (q // 2 + 1))
                me.step(pool.tensor_copy(pastlf4[:, q].rearrange("p j (h t) -> p j h t", t=NT),
                                         spread(pastlf[:, q], 3, NT)), s("lf_spread"))
            def by_chunk(ap):
                return ap[:, :, 0:NP].rearrange("p c (n t) -> p c n t", t=L)

            pool.wait_ge(*once("delta_ops"))
            for a_ in range(2):
                me.step(pool.memset(zv[own(a_), :, :, a_, :], 0.0), s("pool_chain"))
                me.step(pool.tensor_copy(zv[own(a_), :, :, 1 - a_, :], by_chunk(rp[:, PV:PV + HC, :])[own(a_)]),
                        once.give("zv_ready") if a_ else s("pool_chain"))

            def level(n, lv):
                for a_ in range(2):
                    o = own(a_)
                    mask = spread(K("levels")[o, L * lv:L * (lv + 1)], 1, HC)
                    me.step(pool.tensor_tensor(nm[o, n % 2], of(gt[o, n % 2], a_)[:, :, 0:L], mask, ALU.mult),
                            s("nm_ready") if a_ else s("pool_chain"))

            for pair in range(NCH // 2):
                both = (2 * pair, 2 * pair + 1)
                for n in both:
                    pool.wait_ge(s("gt_ready"), 2 * n + 2)
                    level(n, 0)
                for n in both:
                    for a_ in range(2):
                        o = own(1 - a_)
                        me.step(pool.tensor_copy(of(lu[o, n], a_), of(gt[o, n % 2], a_)[:, :, 0:L]),
                                s("lu_ready") if a_ else s("pool_chain"))
                for lv in range(1, LEVELS):
                    for n in both:
                        pool.wait_ge(s("x_mm"), kth(n, lv - 1) + 1)
                        if lv == 1:
                            pool.wait_ge(s("t_ready"), t_count(n, 0))
                        level(n, lv)
            pool.wait_ge(*once("fst_copied"))
            store(st_p[0, 0].rearrange("(c a) v k -> (a v) c k", a=2), bkt[:, 0, 0:HC, :])
            pool.wait_ge(s("sy_ready"), NT)
            store(st_s[0].rearrange("b h (f v) k -> (b h f) (v k)", f=2), sst.rearrange("p v k -> p (v k)"))
            mix_stores[0] = len(stores)
            pool.wait_ge(s("mix_stored"), 16 * len(stores))
            pool.dma_start(pool_s[0][:, 0:PBUF - NT, :], a["state_pool"][0][:, NT:PBUF, :]).then_inc(s("pool_stored"), 16)
            pool.wait_ge(s("hl_copied"), 2)
            pool.dma_start(pool_p[0, 0], hlast[1:16, :]).then_inc(s("pool_stored"), 16)
            for q in range(NB):
                pool.dma_start(pool_s[0, q, PBUF - NT:PBUF, :], hlast[16 + NT * q:16 + NT * (q + 1), :]).then_inc(s("pool_stored"), 16)
            pool.wait_ge(s("pool_stored"), 16 * (2 + NB))

        @block.sync
        def _(sp):
            sp.dma_start(const[:, :], a["constants"]).then_inc(s("const_loaded"), 16)
            sp.dma_start(crow[0:1, :], a["c_prompt"]).then_inc(s("c_loaded"), 16)
            sp.dma_start(crow[1:9, :], a["c_sample"]).then_inc(s("c_loaded"), 16)
            for blk in range(2):
                sp.dma_start(xrow[:, blk, :], a["x_prompt"][0, P * blk:P * (blk + 1), :]).then_inc(s("x_loaded"), 16)
            sp.dma_start(xrow[0:NS, 2, :], a["x_sample"].rearrange("b t d -> (b t) d")).then_inc(s("x_loaded"), 16)

            def load(g):
                if g >= SLOTS:
                    sp.wait_ge(*used(g - SLOTS))
                dst, src = tile_source(g)
                sp.dma_start(dst, src).then_inc(s(f"slot{g % SLOTS}"), 16)

            for g in range(4):
                load(g)
            small_loads = [(w2[:, :], a["rwkv_w2"][0]), (a2[:, :], a["rwkv_a2"][0]), (g2[:, :], a["rwkv_g2"][0]),
                           (fbias[:, :], a["fox_f_bias"].rearrange("o h -> h o")),
                           (routerw[:, :, :], a["moe_router_w"][0].rearrange("(c p) e -> p c e", p=P)),
                           (routerb[:, :], a["moe_router_b"].to_broadcast([P, NE])),
                           (pages[:, :], a["page_table"].rearrange("b j -> (b j)").unsqueeze(0))]
            for dst, src in small_loads:
                sp.dma_start(dst, src).then_inc(s("small_loaded"), 16)
            for g in range(4, MIX_TILE):
                load(g)
            sp.wait_ge(s("ada_mm"), 12)
            sp.dma_start(sst.rearrange("p v k -> p (v k)"),
                         a["state_rwkv"][0].rearrange("b h (f v) k -> (b h f) (v k)", f=2)).then_inc(s("sst_loaded"), 16)
            sp.wait_ge(s("small_loaded"), 16 * len(small_loads))
            for q in range(NB):
                if q >= 2:
                    sp.wait_ge(s("kt_mm"), 2 * (q - 1))
                for j in range(NPG):
                    page = sp.value_load(pages[0:1, NPG * q + j:NPG * q + j + 1], min_val=0,
                                         max_val=a["cache_fox_k"].shape[1] - 1)
                    for dst, name, sem in ((ksamp[:, q % 2, j, :], "cache_fox_k", f"k_page{q % 2}"),
                                           (vsamp[:, q, j, :], "cache_fox_v", "v_pages")):
                        sp.dma_start(dst, a[name][0, bass.ds(page, 1)].rearrange("o p h d -> (o p) (h d)")).then_inc(s(sem), 16)
                    sp.dma_start(pastlf[:, q, j, :], a["cache_fox_logf"][0, bass.ds(page, 1)].rearrange("o p h -> (o p) h"))\
                        .then_inc(s(f"k_page{q % 2}"), 16)
            sp.wait_ge(s("srow_copied"), 6)
            sp.dma_start(scratch.rearrange("b t q h k -> (b t) (q h k)"), srow.rearrange("p q k -> p (q k)")).then_inc(s("srow_stored"), 16)
            sp.wait_ge(s("srow_stored"), 16)
            for q in range(NB):
                for f in range(2):
                    sp.dma_start(svec[2 * H * q + f:2 * H * (q + 1):2].rearrange("p t i k -> p (t i) k"),
                                 scratch[q].rearrange("t i h k -> h (t i) k")).then_inc(s("svec_loaded"), 16)
                sp.dma_start(sval[2 * H * q:2 * H * (q + 1)], scratch[q, :, 5].rearrange("t h (f k) -> (h f) t k", f=2))\
                    .then_inc(s("svec_loaded"), 16)
            sp.wait_ge(*once("packed"))
            sp.wait_ge(*once("zv_ready"))
            sp.dma_start(wo_first.rearrange("p (c f) -> p c f", c=DC),
                         a["w_out"][0].rearrange("(c p) f -> p c f", p=P)[:, :, 0:WOUT[0][1]]).then_inc(s("wo_first"), 16)
            sp.wait_ge(s("sy_ready"), NT)
            for q in range(NB):
                sp.dma_start(scratch_y[q].rearrange("t f k -> f t k"), sy[2 * H * q:2 * H * (q + 1)]).then_inc(s("sy_stored"), 16)
            sp.wait_ge(s("sy_stored"), 16 * NB)
            sp.dma_start(syrow, scratch_y.rearrange("b t f k -> (b t) (f k)")).then_inc(s("syrow_loaded"), 16)
            sp.wait_ge(*once("mix_ready"))
            sp.wait_ge(s("mix_stored"), 16 * mix_stores[0])
            for g in range(MIX_TILE, MIX_TILE + 5):
                load(g)
            sp.wait_ge(s("wo_mm"), WOUT[0][1] // P)
            sp.dma_start(prow[0:NB * PBUF, :], a["state_pool"][0].rearrange("b r d -> (b r) d")).then_inc(s("pool_rows"), 16)
            sp.dma_start(poolw, a["pool_w"][0].rearrange("g (c p) f -> p g c f", p=P)).then_inc(s("poolw_loaded"), 16)
            for g in range(MIX_TILE + 5, len(TILES)):
                load(g)
            moe_sync(sp)
            sp.wait_ge(s("out_copied"), 6)
            sp.dma_start(y_p[0].rearrange("(b p) d -> p b d", p=P), outrow[:, 0:2, :]).then_inc(s("y_stored"), 16)
            sp.dma_start(y_s.rearrange("b t d -> (b t) d"), outrow[0:NS, 2, :]).then_inc(s("y_stored"), 16)
            sp.wait_ge(s("y_stored"), 32)


INPUTS = ["x_prompt", "x_sample", "c_prompt", "c_sample", "cache_fox_k", "cache_fox_v", "cache_fox_logf", "page_table",
          "state_rwkv", "state_rwkv_shift", "state_pool", "norm1_g", "norm2_g", "ada_w", "ada_b", "w_in", "w_out",
          "fox_q_gain", "fox_k_gain", "fox_f_bias", "rwkv_mu", "rwkv_w0", "rwkv_w2", "rwkv_a0", "rwkv_a2", "rwkv_g2",
          "rwkv_k_k", "rwkv_k_a", "rwkv_r_k", "rwkv_ln_w", "rwkv_ln_b", "ffn_w_gate", "ffn_w_up", "ffn_w_down",
          "pool_w", "pool_scale", "moe_router_w", "moe_router_b", "moe_w_gate", "moe_w_up", "moe_w_down"]
OUTPUTS = [(1, NP, D), (NB, NT, D), (1, 1, NP, H, DH), (1, NB, NT, H, DH), (1, 1, NP, H, DH), (1, NB, NT, H, DH),
           (1, 1, NP, H), (1, NB, NT, H), (1, 1, H, DH, DH), (1, NB, H, DH, DH), (1, 1, RW_IN), (1, NB, RW_IN),
           (1, 1, PBUF, D), (1, NB, PBUF, D)]


def kernel(**inputs):
    import concourse.bacc as bacc
    from concourse.bass_utils import run_bass_kernel_spmd

    nc = bacc.Bacc("TRN2", target_bir_lowering=False, num_devices=1)
    arrays, args = {}, {}
    for name in INPUTS + ["constants"]:
        x = constants() if name == "constants" else np.ascontiguousarray(inputs[name])
        arrays[f"in_{name}"] = x
        args[name] = nc.dram_tensor(f"in_{name}", x.shape, mybir.dt.from_np(x.dtype), kind="ExternalInput").ap()
    outs = [nc.dram_tensor(f"out_{i}", shape, F32, kind="ExternalOutput").ap() for i, shape in enumerate(OUTPUTS)]
    build_program(nc, args, *outs)
    r = run_bass_kernel_spmd(nc, [arrays], core_ids=[0])
    return tuple(r.results[0][f"out_{i}"] for i in range(len(OUTPUTS)))
```
